# Optimizing a Trainium2 kernel written in Bass

```python
import jax
import jax.numpy as jnp
from jax import lax
import numpy as np

D_MODEL = 2048
BATCH = 1
SEQ = 256
DEPTH = 1

HEAD_DIM = 128
MIX_WIDTH = D_MODEL
ATTN_WIDTH = MIX_WIDTH // 2
GMLP_WIDTH = MIX_WIDTH - ATTN_WIDTH
ATTN_HEADS = ATTN_WIDTH // HEAD_DIM
KV_HEADS = max(1, ATTN_HEADS // 4)
Q_PER_KV = ATTN_HEADS // KV_HEADS
KV_WIDTH = KV_HEADS * HEAD_DIM
GMLP_HEAD_DIM = 128
GMLP_HEADS = GMLP_WIDTH // GMLP_HEAD_DIM
IN_WIDTH = ATTN_WIDTH + 2 * KV_WIDTH + 2 * GMLP_WIDTH
WINDOW = 128
BLOCK = 128
CHUNK = 128
ROPE_THETA = 500000.0
ROPE_DIM = HEAD_DIM // 4
N_GROUPS = 4
EXPERTS_PER_GROUP = 4
TOP_K = 2
D_EXPERT = D_MODEL // 2
N_MOD = 6
EPS = 1e-6
NEG_INF = -1e30

kernel_name = 'hybrid_swa_gmlp_hmoe_block'

def rms_norm(x, g):
    xf = x.astype(jnp.float32)
    y = xf * lax.rsqrt(jnp.mean(xf * xf, axis=-1, keepdims=True) + EPS)
    return (y * g.astype(jnp.float32)).astype(x.dtype)

def partial_rope(x, positions):
    half = ROPE_DIM // 2
    inv_freq = ROPE_THETA ** (-jnp.arange(half, dtype=jnp.float32) * 2.0 / ROPE_DIM)
    ang = positions.astype(jnp.float32)[..., None] * inv_freq
    cos = jnp.cos(ang)[:, :, None, :]
    sin = jnp.sin(ang)[:, :, None, :]
    xf = x.astype(jnp.float32)
    x1 = xf[..., :half]
    x2 = xf[..., half:ROPE_DIM]
    out = jnp.concatenate([x1 * cos - x2 * sin, x2 * cos + x1 * sin, xf[..., ROPE_DIM:]], axis=-1)
    return out.astype(x.dtype)

def window_attention(q, k, v, sink):
    B, S = q.shape[0], q.shape[1]
    nb = S // BLOCK
    qb = q.reshape(B, nb, BLOCK, KV_HEADS, Q_PER_KV, HEAD_DIM)

    def band(t):
        tp = jnp.pad(t, ((0, 0), (BLOCK, BLOCK), (0, 0), (0, 0)))
        tb = tp.reshape(B, nb + 2, BLOCK, KV_HEADS, HEAD_DIM)
        return jnp.concatenate([tb[:, :-2], tb[:, 1:-1], tb[:, 2:]], axis=2)

    kb = band(k)
    vb = band(v)
    s = jnp.einsum('bnqhgd,bnkhd->bnhgqk', qb, kb).astype(jnp.float32) * (HEAD_DIM ** -0.5)
    q_off = jnp.arange(BLOCK)[:, None]
    k_off = jnp.arange(3 * BLOCK)[None, :] - BLOCK
    k_glob = jnp.arange(nb)[:, None, None] * BLOCK + k_off[None]
    valid = (jnp.abs(k_off - q_off) <= WINDOW)[None] & (k_glob >= 0) & (k_glob < S)
    s = jnp.where(valid[None, :, None, None], s, NEG_INF)
    sink_col = jnp.broadcast_to(sink.astype(jnp.float32).reshape(1, 1, KV_HEADS, Q_PER_KV, 1, 1),
                                s.shape[:-1] + (1,))
    p = jax.nn.softmax(jnp.concatenate([s, sink_col], axis=-1), axis=-1)[..., :-1]
    o = jnp.einsum('bnhgqk,bnkhd->bnqhgd', p.astype(v.dtype), vb)
    return o.reshape(B, S, ATTN_WIDTH)

def spatial_gating(u, v, g_norm, w_s, b_s):
    B, S = u.shape[0], u.shape[1]
    nc = S // CHUNK
    u = jax.nn.gelu(u, approximate=False).reshape(B, S, GMLP_HEADS, GMLP_HEAD_DIM)
    vf = jax.nn.gelu(v.astype(jnp.float32), approximate=False).reshape(B, S, GMLP_HEADS, GMLP_HEAD_DIM)
    mu = jnp.mean(vf, axis=-1, keepdims=True)
    var = jnp.mean(jnp.square(vf - mu), axis=-1, keepdims=True)
    vf = (vf - mu) * lax.rsqrt(var + EPS) * g_norm.astype(jnp.float32)
    vc = vf.astype(u.dtype).reshape(B, nc, CHUNK, GMLP_HEADS, GMLP_HEAD_DIM)
    mixed = jnp.einsum('hpq,bcqhd->bcphd', w_s, vc) + b_s.T[None, None, :, :, None]
    return (u * mixed.reshape(B, S, GMLP_HEADS, GMLP_HEAD_DIM)).reshape(B, S, GMLP_WIDTH)

def token_mixer(a, positions, w_in, sink, g_norm, w_s, b_s, g_group, w_out):
    B, S = a.shape[0], a.shape[1]
    z = a @ w_in
    o0 = ATTN_WIDTH
    o1 = o0 + KV_WIDTH
    o2 = o1 + KV_WIDTH
    o3 = o2 + GMLP_WIDTH
    q = partial_rope(z[..., :o0].reshape(B, S, ATTN_HEADS, HEAD_DIM), positions)
    k = partial_rope(z[..., o0:o1].reshape(B, S, KV_HEADS, HEAD_DIM), positions)
    v = z[..., o1:o2].reshape(B, S, KV_HEADS, HEAD_DIM)
    y_attn = window_attention(q, k, v, sink)
    y_gmlp = spatial_gating(z[..., o2:o3], z[..., o3:], g_norm, w_s, b_s)
    y = jnp.concatenate([rms_norm(y_attn, g_group[:ATTN_WIDTH]),
                         rms_norm(y_gmlp, g_group[ATTN_WIDTH:])], axis=-1)
    return y @ w_out

def hier_moe(f, w_rg, b_rg, w_re, b_re, w_gate, w_up, w_down):
    B, S, D = f.shape
    t = f.reshape(B * S, D)
    g_logits = (t @ w_rg).astype(jnp.float32) + b_rg.astype(jnp.float32)
    g_val, g_idx = lax.top_k(jax.nn.softmax(g_logits, axis=-1), 1)
    e_logits = jnp.einsum('td,dge->tge', t, w_re).astype(jnp.float32) + b_re.astype(jnp.float32)
    e_sel = jnp.take_along_axis(e_logits, g_idx[:, :, None], axis=1)[:, 0]
    e_val, e_idx = lax.top_k(jax.nn.softmax(e_sel, axis=-1), TOP_K)
    e_w = e_val / jnp.sum(e_val, axis=-1, keepdims=True) * g_val
    comb = jnp.sum(jax.nn.one_hot(e_idx, EXPERTS_PER_GROUP, dtype=jnp.float32) * e_w[..., None], axis=1)
    comb = jax.nn.one_hot(g_idx[:, 0], N_GROUPS, dtype=jnp.float32)[:, :, None] * comb[:, None, :]
    comb = comb.astype(t.dtype)
    y = jnp.zeros_like(t)
    for g in range(N_GROUPS):
        h_gate = jnp.einsum('td,edf->etf', t, w_gate[g])
        h_up = jnp.einsum('td,edf->etf', t, w_up[g])
        hid = jax.nn.silu(h_gate) * h_up * comb[:, g].T[:, :, None]
        y = y + jnp.einsum('etf,efd->td', hid, w_down[g])
    return y.reshape(B, S, D)

def setup_inputs(seed: int = 0) -> dict:
    key = jax.random.key(seed)
    ks = jax.random.split(key, 24)
    f32 = jnp.float32

    def nrm(k, shape, scale):
        return jax.random.normal(k, shape, f32) * scale

    def gain(k, shape):
        return 1.0 + 0.02 * jax.random.normal(k, shape, f32)

    G, E, D, F = N_GROUPS, EXPERTS_PER_GROUP, D_MODEL, D_EXPERT
    x = nrm(ks[0], (BATCH, SEQ, D), 1.0)
    c = nrm(ks[1], (BATCH, D), 1.0)
    offset = jax.random.randint(ks[2], (BATCH, 1), 0, 4096, dtype=jnp.int32)
    positions = offset + jnp.arange(SEQ, dtype=jnp.int32)[None, :]
    return {
        'x': x,
        'c': c,
        'positions': positions,
        'w_ada': nrm(ks[3], (DEPTH, D, N_MOD * D), 0.5 * D ** -0.5),
        'b_ada': nrm(ks[4], (DEPTH, N_MOD * D), 0.02),
        'g_mix_pre': gain(ks[5], (DEPTH, D)),
        'g_mix_post': gain(ks[6], (DEPTH, D)),
        'w_in': nrm(ks[7], (DEPTH, D, IN_WIDTH), D ** -0.5),
        'sink_logits': nrm(ks[8], (DEPTH, ATTN_HEADS), 1.0),
        'gmlp_norm_g': gain(ks[9], (DEPTH, GMLP_HEADS, GMLP_HEAD_DIM)),
        'w_spatial': nrm(ks[10], (DEPTH, GMLP_HEADS, CHUNK, CHUNK), CHUNK ** -0.5),
        'b_spatial': gain(ks[11], (DEPTH, GMLP_HEADS, CHUNK)),
        'g_group_out': gain(ks[12], (DEPTH, MIX_WIDTH)),
        'w_out': nrm(ks[13], (DEPTH, MIX_WIDTH, D), MIX_WIDTH ** -0.5),
        'g_ffn_pre': gain(ks[14], (DEPTH, D)),
        'g_ffn_post': gain(ks[15], (DEPTH, D)),
        'w_router_group': nrm(ks[16], (DEPTH, D, G), D ** -0.5),
        'b_router_group': nrm(ks[17], (DEPTH, G), 0.01),
        'w_router_expert': nrm(ks[18], (DEPTH, D, G, E), D ** -0.5),
        'b_router_expert': nrm(ks[19], (DEPTH, G, E), 0.01),
        'w_gate': nrm(ks[20], (DEPTH, G, E, D, F), D ** -0.5),
        'w_up': nrm(ks[21], (DEPTH, G, E, D, F), D ** -0.5),
        'w_down': nrm(ks[22], (DEPTH, G, E, F, D), F ** -0.5),
    }

def reference(x, c, positions, w_ada, b_ada, g_mix_pre, g_mix_post, w_in, sink_logits,
              gmlp_norm_g, w_spatial, b_spatial, g_group_out, w_out, g_ffn_pre, g_ffn_post,
              w_router_group, b_router_group, w_router_expert, b_router_expert,
              w_gate, w_up, w_down):
    h = x
    c_act = jax.nn.silu(c)
    for l in range(DEPTH):
        mod = c_act @ w_ada[l] + b_ada[l]
        sh1, sc1, gt1, sh2, sc2, gt2 = jnp.split(mod[:, None, :], N_MOD, axis=-1)
        a = rms_norm(h, g_mix_pre[l]) * (1 + sc1) + sh1
        mix = token_mixer(a, positions, w_in[l], sink_logits[l], gmlp_norm_g[l],
                          w_spatial[l], b_spatial[l], g_group_out[l], w_out[l])
        h = h + gt1 * rms_norm(mix, g_mix_post[l])
        f = rms_norm(h, g_ffn_pre[l]) * (1 + sc2) + sh2
        y = hier_moe(f, w_router_group[l], b_router_group[l], w_router_expert[l],
                     b_router_expert[l], w_gate[l], w_up[l], w_down[l])
        h = h + gt2 * rms_norm(y, g_ffn_post[l])
    return h


_drawn_inputs = setup_inputs


def setup_inputs(seed=0):
    import zlib

    import numpy as np

    out = dict(_drawn_inputs(seed))
    spreads = {}
    factors = {'g_mix_pre': 2.998,
     'g_mix_post': 3.081,
     'sink_logits': 64.0,
     'gmlp_norm_g': 8.0,
     'g_ffn_post': 25.512,
     'b_router_expert': 4.852,
     'b_spatial': 8.0,
     'b_router_group': 8.0}
    for name, (base, spread) in spreads.items():
        noise = np.random.default_rng([zlib.crc32(name.encode()), seed]).standard_normal(out[name].shape)
        drawn = base * np.exp(spread * noise) if base else spread * noise
        out[name] = jnp.asarray(drawn.astype(out[name].dtype))
    for name, factor in factors.items():
        out[name] = (out[name] * factor).astype(out[name].dtype)
    return out
```

```python
from contextlib import ExitStack

import numpy as np

import concourse.bass as bass
from concourse import mybir

F32 = mybir.dt.float32
I32 = mybir.dt.int32
ALU = mybir.AluOpType
ACT = mybir.ActivationFunctionType
AX = mybir.AxisListType

P = 128
SEQ, D = 256, 2048
TT = SEQ // P
KC = D // P
HEADS, KV, HD = 8, 2, 128
N_IN = 3584
O_K, O_V, O_U, O_G = 1024, 1280, 1536, 2560
GROUPS, EPG = 4, 4
E = GROUPS * EPG
FF = 1024
HALF = 1024
CH = 512
WIN = N_IN // CH
WOUT = D // CH
BLK = 64
BLOCKS = SEQ // BLK
CAP = BLK
MAX_EXTRA = (2 * SEQ - 1) // (CAP + 1)
SLOTS = 6
ROPE = HD // 4
HR = ROPE // 2
THETA = 500000.0
EPS = 1e-6
SCALE = HD ** -0.5
NEG = -1e30
FAR = 4096.0
MAGIC = 12582912.0
TWO_PI = (6.28125, 1.9340515136718750e-3, 1.2556659146735911e-6)
PI_SAFE = 3.1415925

SC1, SH1, GT1, GT2, SH2, SC2 = range(6)
MOD_COLUMN = {SH1: 0, SC1: 1, GT1: 2, SH2: 3, SC2: 4, GT2: 5}
HALVES = 12

T_GROUPS = ([("aT", n) for n in range(8)] + [("wsT", n) for n in range(2)]
            + [("q0", n) for n in range(2)] + [("k", 0)] + [("s0", n) for n in range(4)]
            + [("p0", n) for n in range(4)] + [("q1", n) for n in range(2)]
            + [("s1", n) for n in range(4)] + [("p1", n) for n in range(4)]
            + [("yT", n) for n in range(8)] + [("fT", n) for n in range(8)])
T_AT = {g: i for i, g in enumerate(T_GROUPS)}



class Steps:

    def __init__(self, engine, sem):
        self.engine, self.sem, self.n = engine, sem, 0

    def add(self, ins):
        ins.then_inc(self.sem, 1)
        self.n += 1
        return self.n

    def link(self, ins):
        self.engine.wait_ge(self.sem, self.add(ins))


def hybrid_block(nc, x, c, positions, w_ada, b_ada, g_mix_pre, g_mix_post, w_in, sink,
                 gmlp_g, w_spatial, b_spatial, g_group, w_out, g_ffn_pre, g_ffn_post,
                 w_rg, b_rg, w_re, b_re, w_gate, w_up, w_down, out):
    with ExitStack() as ctx:
        def sb(name, shape, dt=F32):
            return ctx.enter_context(nc.sbuf_tensor(name, shape, dt))

        def sem(name):
            return ctx.enter_context(nc.semaphore(name))

        ring = sb("ring", [P, SLOTS, 4096])
        X = sb("X", [P, 4096])
        Gt = sb("Gt", [P, 2, D])
        A = sb("A", [P, 4096])
        T = sb("T", [P, KC, SEQ])
        Z = sb("Z", [P, TT * N_IN])
        mod_rows = sb("mod_rows", [P, HALF])
        bias_rows = sb("bias_rows", [P, HALF])
        gain_rows = sb("gain_rows", [P, HALF])
        c_wide = sb("c_wide", [P, KC, 32])
        w_router = sb("w_router", [P, KC, GROUPS + E])
        ident = sb("ident", [P, P])
        rows4 = sb("rows4", [P, P])
        before = sb("before", [P, P])
        mask = sb("mask", [P, TT, P])
        vec_rows = c_wide[:].rearrange("p k n -> p (k n)")[0:40, 0:P]
        vec_cols = sb("vec_cols", [P, 40])

        xv = X[:].rearrange("p (t d) -> p t d", t=TT)
        av = A[:].rearrange("p (t d) -> p t d", t=TT)
        zv = Z[:].rearrange("p (t n) -> p t n", t=TT)
        hv = Z[:, 0:TT * D].rearrange("p (t d) -> p t d", t=TT)
        G1, sh1 = Z[:, 0:D], Z[:, D:2 * D]
        w_sp = Z[:, 4096:5120].rearrange("p (h q) -> p h q", h=HEADS)
        wsT = X[:, 0:1024].rearrange("p (h q) -> p h q", h=HEADS)
        gain_v = X[:, 1024:2048]
        G2, sh2 = X[:, 0:D], X[:, D:2 * D]
        kT = A[:, 0:512].rearrange("p (k s) -> p k s", k=KV)
        qT = A[:, 512:1536].rearrange("p (h s) -> p h s", h=HEADS)
        S = A[:, 1536:3584].rearrange("p (h s) -> p h s", h=HEADS)
        pT = [A[:, 3584:4096], A[:, 512:1024]]
        pT = [b.rearrange("p (h c s) -> p h c s", h=2, c=2) for b in pT]
        xT = X[:].rearrange("p (c s) -> p c s", c=KC)
        silu_s, hid = mod_rows[:, 0:CH], mod_rows[:, CH:2 * CH]
        hidT = bias_rows[:, 0:CH].rearrange("p (t s) -> p t s", t=4)
        down_s = gain_rows
        pick = Gt[:, 0, 0:TT * EPG * BLK].rearrange("p (t s) -> p t s", t=TT)
        wpick = Gt[:, 0, 1024:1024 + TT * P].rearrange("p (t s) -> p t s", t=TT)
        Y = T[:].rearrange("p c s -> p (c s)").rearrange("p (t d) -> p t d", t=TT)
        ZM = Z[:, 4096:7168]
        wpickT = ZM[:, 0:256]
        slot_id = ZM[:, 256:256 + BLOCKS * P].rearrange("p (b s) -> p b s", b=BLOCKS)
        route = ZM[:, 768:1536]
        items_f = ZM[0:1, 1536:1536 + 1024]
        ones = sb("ones", [P, P])
        inv_freq = sb("inv_freq", [P, HR])
        pos_i = sb("pos_i", [P, TT], I32)
        angle = sb("angle", [P, 2, TT, HR])
        turns = mod_rows[:, 0:2 * TT * HR].rearrange("p (a t n) -> p a t n", a=2, t=TT)
        sink_b = sb("sink_b", [P, HEADS])
        router_b = sb("router_b", [P, GROUPS + E])
        stats = sb("stats", [P, 96])
        newton = sb("newton", [P, 12])
        row0 = sb("row0", [P, 1])
        items = sb("items", [1, 32], I32)

        ps = ctx.enter_context(nc.psum_tensor("ps", [P, 8, CH], F32))
        flat = ps[:].rearrange("p b n -> p (b n)")
        ada_acc, ada_wide = flat[:, 0:1024], flat[:, 1024:2048]
        W0B, T0B = 4, 6

        x_in, small_in, vec_in, c_in, gain_in, x2_in = (sem(n) for n in (
            "x_in", "small_in", "vec_in", "c_in", "gain_in", "x2_in"))
        landed = [sem(f"landed{s}") for s in range(SLOTS)]
        slot_free = [sem(f"slot_free{s}") for s in range(SLOTS)]
        chunk_in = [sem(f"chunk_in{s}") for s in range(2)]
        bias_in, gainrow_in = sem("bias_in"), sem("gainrow_in")
        constants = sem("constants")
        vec_chain, act_chain, pool_chain = sem("vec_chain"), sem("act_chain"), sem("pool_chain")
        c_silu, vec_ps, c_ready = sem("c_silu"), sem("vec_ps"), sem("c_ready")
        x_square = sem("x_square")
        rows_ready, wide_done, wide_out = sem("rows_ready"), sem("wide_done"), sem("wide_out")
        scaled, a_ready = sem("scaled"), sem("a_ready")
        t_done = sem("t_done")
        t_out = [sem("t_out_vector"), sem("t_out_scalar")]
        w_done, z_out = sem("w_done"), sem("z_out")
        trig_in, trig = sem("trig_in"), sem("trig")
        roped = sem("roped")
        bias_max, probs, pv_done, o_out = sem("bias_max"), sem("probs"), sem("pv_done"), sem("o_out")
        vn_ready, mixed_done, gated = sem("vn_ready"), sem("mixed_done"), sem("gated")
        y_square, y_ready = sem("y_square"), sem("y_ready")
        mix_square, h_ready, h_square, f_ready = (sem(n) for n in (
            "mix_square", "h_ready", "h_square", "f_ready"))
        logits_done, gap_ready, gap_exp = sem("logits_done"), sem("gap_ready"), sem("gap_exp")
        chosen, ranks_done, list_ready = sem("chosen"), sem("ranks_done"), sem("list_ready")
        pick_ready, gathered, xT_ready = sem("pick_ready"), sem("gathered"), sem("xT_ready")
        wpick_ready, wpickT_done, wpickT_ready = (sem(n) for n in (
            "wpick_ready", "wpickT_done", "wpickT_ready"))
        silu_ready, hid_ready = sem("silu_ready"), sem("hid_ready")
        hidT_done, hidT_ready = sem("hidT_done"), sem("hidT_ready")
        down_ready = sem("down_ready")
        spread, summed = sem("spread"), sem("summed")
        out_square, out_ready, stored = (sem(n) for n in ("out_square", "out_ready", "stored"))

        x_d = x.rearrange("a (t p) d -> p (a t) d", p=P)
        out_d = out.rearrange("a (t p) d -> p (a t) d", p=P)
        ada_d = w_ada[0].rearrange("(k p) n -> p k n", p=P)
        win_d = w_in[0].rearrange("(k p) n -> p k n", p=P)
        wout_d = w_out[0].rearrange("(k p) n -> p k n", p=P)
        gate_d = w_gate.rearrange("a g e (k p) f -> p (a g e) k f", p=P)
        up_d = w_up.rearrange("a g e (k p) f -> p (a g e) k f", p=P)
        down_d = w_down.rearrange("a g e (k p) d -> p (a g e) k d", p=P)
        gain_of = {SC1: g_mix_pre, GT1: g_mix_post, SC2: g_ffn_pre, GT2: g_ffn_post}
        mod_to = {SC1: G1, SH1: sh1, GT1: Gt[:, 0, :], GT2: Gt[:, 1, :], SH2: sh2, SC2: G2}
        n_gained = [sum(1 for m in range(n + 1) if m // 2 in gain_of) for n in range(HALVES)]

        def ada_slot(s):
            return ring[:, s, :].rearrange("p (k n) -> p k n", k=4)

        def chunk_slot(s):
            return ring[:, s, :].rearrange("p (k n) -> p k n", k=8)

        def down_slot(s):
            return ring[:, s, :].rearrange("p (k n) -> p k n", k=2)

        USED = [HALVES] * 4 + [0, 0]
        FREED = [HALVES] * 4 + [WIN + WOUT, 1]

        def wait_products(eng, last, i):
            eng.wait_ge(slot_free[last % SLOTS], i * 2 + (FREED[last % SLOTS] + last // SLOTS + 1))

        GATHER_BANK = [0, 1, 2, 3, 4, 2, 3, 4]
        GATE_UP, DOWN = 7, 11

        block = ctx.enter_context(nc.Block())

        @block.sync
        def _(sp):
            for n in range(HALVES):
                col = D * MOD_COLUMN[n // 2] + HALF * (n % 2)
                for s in range(4):
                    if n:
                        sp.wait_ge(slot_free[s], n)
                    sp.dma_start(ada_slot(s), ada_d[:, 4 * s:4 * s + 4, col:col + HALF]).then_inc(landed[s], 16)
                if n == 0:
                    sp.wait_ge(constants, 1)
                else:
                    sp.wait_ge(rows_ready, n)
                sp.dma_start(bias_rows[0:1, :], b_ada[0:1, col:col + HALF]).then_inc(bias_in, 16)
                if n // 2 in gain_of:
                    g = gain_of[n // 2][0:1, HALF * (n % 2):HALF * (n % 2 + 1)]
                    sp.dma_start(gain_rows[0:97:32, :], g.broadcast_to([4, HALF])).then_inc(gainrow_in, 16)

            def load_expert(i, e):
                for q in range(12):
                    s = q % SLOTS
                    sp.wait_ge(slot_free[s], i * 2 + (FREED[s] + q // SLOTS))
                    if q == 5:
                        sp.wait_ge(w_done, TT * (WIN + WOUT))
                    if q < 8:
                        w = gate_d if q % 2 == 0 else up_d
                        src, dst = w[:, bass.ds(e, 1), 4 * (q // 2):4 * (q // 2) + 4, :], ada_slot(s)
                    else:
                        src, dst = down_d[:, bass.ds(e, 1), 2 * (q - 8):2 * (q - 8) + 2, :], down_slot(s)
                    sp.dma_start(dst.unsqueeze(1), src).then_inc(landed[s], 16)

            with sp.Fori(0, E) as i:
                load_expert(i, i)
            sp.wait_ge(list_ready, 1)
            n_extra = sp.value_load(items[0:1, 0:1], min_val=0, max_val=MAX_EXTRA)
            with sp.If(n_extra > 0):
                with sp.Fori(0, n_extra) as j:
                    e = sp.value_load(items[0:1, bass.ds(j + 1, 1)], min_val=0, max_val=E - 1)
                    load_expert(j + E, e)
            for t in range(TT):
                sp.wait_ge(out_ready, t + 1)
                sp.dma_start(out_d[:, t, :], Y[:, t, :]).then_inc(stored, 16)
            sp.wait_ge(stored, 16 * TT)

        @block.gpsimd
        def _(pool):
            ch = Steps(pool, pool_chain)
            nc.gpsimd.memset(bias_rows[:], 0.0)
            nc.gpsimd.memset(gain_rows[:], 1.0).then_inc(constants, 1)
            nc.gpsimd.memset(ones[:], 1.0)
            nc.gpsimd.memset(before[:], 1.0)
            nc.gpsimd.memset(mask[:], 0.0)
            nc.gpsimd.memset(rows4[:], 0.0)
            nc.gpsimd.memset(row0[:], 0.0)
            for n in range(HR):
                nc.gpsimd.memset(inv_freq[:, n:n + 1], float(np.float32(THETA) ** np.float32(-2.0 * n / ROPE)))
            ch.link(nc.gpsimd.memset(ident[:], 0.0))
            for r in range(4):
                ch.link(nc.gpsimd.memset(rows4[32 * r:32 * r + 1, :], 1.0))
            ch.link(nc.gpsimd.memset(row0[0:1, :], 1.0))
            nc.gpsimd.affine_select(out=ident[:], in_=ident[:], compare_op=ALU.not_equal, fill=1.0,
                                    base=0, pattern=[[-1, P]], channel_multiplier=1)
            nc.gpsimd.affine_select(out=before[:], in_=before[:], compare_op=ALU.is_ge, fill=0.0,
                                    base=-1, pattern=[[1, P]], channel_multiplier=-1)
            nc.gpsimd.affine_select(out=mask[:, 0, :], in_=mask[:, 0, :], compare_op=ALU.is_ge, fill=NEG,
                                    base=0, pattern=[[-1, P]], channel_multiplier=1)
            nc.gpsimd.affine_select(out=mask[:, 1, :], in_=mask[:, 1, :], compare_op=ALU.is_ge, fill=NEG,
                                    base=0, pattern=[[1, P]], channel_multiplier=-1).then_inc(constants, 1)

            def load_chunk(m, w_d, col):
                for half in range(2):
                    s = 4 + half
                    if m and half == 0:
                        pool.wait_ge(slot_free[4], m)
                    elif m:
                        pool.wait_ge(w_done, TT * m)
                    pool.dma_start(chunk_slot(s), w_d[:, 8 * half:8 * half + 8, col:col + CH]).then_inc(chunk_in[half], 16)

            pool.wait_ge(slot_free[3], 2)
            for m in range(WIN):
                load_chunk(m, win_d, CH * m)
            for m in range(WOUT):
                load_chunk(WIN + m, wout_d, CH * m)
                if m == 0:
                    pool.wait_ge(t_done, T_AT["yT", 7] + 1)
                    pool.dma_start(hv, x_d).then_inc(x2_in, 16)
            for b in range(BLOCKS):
                v = slot_id[:, b, :].rearrange("p (r s) -> p r s", r=2)
                ch.link(nc.gpsimd.iota(v, pattern=[[0, 2], [1, BLK]], base=CAP * b, channel_multiplier=0,
                                       allow_small_or_imprecise_dtypes=True))
                if CAP < BLK:
                    ch.link(nc.gpsimd.memset(v[:, :, CAP:BLK], -1.0))
            ch.link(nc.gpsimd.iota(route[:, 0:4], pattern=[[1, 4]], base=0, channel_multiplier=0,
                                   allow_small_or_imprecise_dtypes=True))
            nc.gpsimd.iota(items_f[0:1, 0:48], pattern=[[0, 3], [1, 16]], base=0, channel_multiplier=0,
                           allow_small_or_imprecise_dtypes=True)
            nc.gpsimd.iota(items_f[0:1, 48:96], pattern=[[1, 3], [0, 16]], base=1, channel_multiplier=0,
                           allow_small_or_imprecise_dtypes=True)
            nc.gpsimd.iota(items_f[0:1, 96:103], pattern=[[1, 7]], base=1, channel_multiplier=0,
                           allow_small_or_imprecise_dtypes=True).then_inc(constants, 1)

        @block.scalar
        def _(act):
            ch = Steps(act, act_chain)
            act.dma_start(vec_rows[0:16, :], c.rearrange("a (k p) -> (a k) p", p=P)).then_inc(c_in, 16)
            act.dma_start(vec_rows[16:32, :], g_group.rearrange("a (k p) -> (a k) p", p=P)).then_inc(vec_in, 16)
            act.dma_start(vec_rows[32:40, :], b_spatial[0]).then_inc(vec_in, 16)
            act.dma_start(xv, x_d).then_inc(x_in, 16)
            act.dma_start(pos_i[:], positions.rearrange("a (t p) -> p (a t)", p=P), allow_slow_non_contiguous=True).then_inc(small_in, 16)
            act.dma_start(sink_b[:], sink[0:1, :].broadcast_to([P, HEADS])).then_inc(small_in, 16)
            act.dma_start(router_b[:, 0:GROUPS], b_rg[0:1, :].broadcast_to([P, GROUPS])).then_inc(small_in, 16)
            act.dma_start(router_b[:, GROUPS:], b_re.rearrange("a g e -> a (g e)").broadcast_to([P, E])).then_inc(small_in, 16)
            act.dma_start(w_sp, w_spatial[0].rearrange("h p q -> p h q")).then_inc(small_in, 16)
            act.dma_start(w_router[:, :, 0:GROUPS], w_rg[0].rearrange("(p k) g -> p k g", k=KC)).then_inc(small_in, 16)
            act.dma_start(w_router[:, :, GROUPS:], w_re[0].rearrange("(p k) g e -> p k (g e)", k=KC)).then_inc(small_in, 16)
            act.wait_ge(c_in, 16)
            nc.scalar.activation(vec_rows[0:16, :], vec_rows[0:16, :], ACT.Silu).then_inc(c_silu, 1)
            act.wait_ge(x_in, 16)
            for t in range(TT):
                nc.scalar.activation(av[:, t, :], xv[:, t, :], ACT.Square, accum_out=stats[:, t:t + 1]).then_inc(x_square, 1)

            def wide(n):
                act.wait_ge(wide_done, n + 1)
                to = mod_to[n // 2][:, HALF * (n % 2):HALF * (n % 2 + 1)]
                nc.scalar.copy(to, ada_wide).then_inc(wide_out, 1)

            def t_group(name, n):
                g = T_AT[name, n]
                return g % 2 == 1, g

            def t_copy(name, n, to):
                odd, g = t_group(name, n)
                if odd:
                    act.wait_ge(t_done, g + 1)
                    src = ps[:, T0B + 1, :]
                    if name == "fT":
                        src = src.rearrange("p (k s) -> p k s", k=4)
                    nc.scalar.copy(to, src).then_inc(t_out[1], 1)

            def z_chunk(m):
                for t in range(TT):
                    act.wait_ge(w_done, 2 * m + t + 1)
                    nc.scalar.activation(zv[:, t, CH * m:CH * m + CH], ps[:, W0B + t, :],
                                         ACT.Copy if m < 3 else ACT.Gelu).then_inc(z_out, 1)

            wide(0)
            wide(1)
            wide(2)
            for n in range(4):
                t_copy("aT", n, T[:, 2 * n:2 * n + 2, :])
            wide(3)
            act.wait_ge(trig_in, 1)
            nc.scalar.activation(angle[:], angle[:], ACT.Sin).then_inc(trig, 1)
            for n in range(4, 8):
                t_copy("aT", n, T[:, 2 * n:2 * n + 2, :])
            act.wait_ge(scaled, 2)
            act.dma_start(gain_v, gmlp_g.rearrange("a h d -> a (h d)").broadcast_to([P, HEADS * HD])).then_inc(gain_in, 16)
            for n in range(2):
                t_copy("wsT", n, wsT[:, 4 * n:4 * n + 4, :])
            for m in range(3):
                z_chunk(m)
                wide(4 + m)
            for n in range(2):
                t_copy("q0", n, qT[:, 4 * n:4 * n + 4, :])
            t_copy("k", 0, kT)
            z_chunk(3)
            wide(7)

            def scores(t):
                for n in range(4):
                    t_copy(f"s{t}", n, S[:, 2 * n:2 * n + 2, :])

            def softmax(t):
                act.wait_ge(bias_max, t + 1)
                for h in range(HEADS):
                    ins = nc.scalar.activation(S[:, h, :], S[:, h, :], ACT.Exp, bias=stats[:, 16 + h:17 + h],
                                               scale=SCALE, accum_out=stats[:, 24 + h:25 + h])
                nc.scalar.activation(stats[:, 32:40], stats[:, 40:48], ACT.Exp).then_inc(probs, 1)

            def probs_out(t):
                for n in range(4):
                    odd, g = t_group(f"p{t}", n)
                    if odd and (n >= 2 or t):
                        act.wait_ge(pv_done, 4 * t + n - 1)
                    t_copy(f"p{t}", n, pT[n % 2])

            scores(0)
            softmax(0)
            z_chunk(4)
            wide(8)
            probs_out(0)
            for n in range(2):
                t_copy("q1", n, qT[:, 4 * n:4 * n + 4, :])
            scores(1)
            softmax(1)
            z_chunk(5)
            wide(9)
            probs_out(1)
            act.wait_ge(o_out, 2)
            for t in range(TT):
                nc.scalar.activation(A[:, 1536 + 1024 * t:2560 + 1024 * t], zv[:, t, 0:1024], ACT.Square,
                                     accum_out=stats[:, 48 + t:49 + t]).then_inc(y_square, 1)
            z_chunk(6)
            for t in range(TT):
                act.wait_ge(gated, 4)
                act.wait_ge(y_square, t + 1)
                nc.scalar.activation(A[:, 1536 + 1024 * t:2560 + 1024 * t], zv[:, t, O_U:O_U + 1024], ACT.Square,
                                     accum_out=stats[:, 50 + t:51 + t]).then_inc(y_square, 1)
            wide(10)
            for n in range(8):
                odd, g = t_group("yT", n)
                if odd:
                    act.wait_ge(t_done, g + 1)
                    for k in range(2):
                        ins = nc.scalar.activation(T[:, 2 * n + k, :], ps[:, T0B + 1, SEQ * k:SEQ * k + SEQ], ACT.Copy,
                                                   scale=vec_cols[:, 16 + 2 * n + k:17 + 2 * n + k])
                    ins.then_inc(t_out[1], 1)
            wide(11)
            act.wait_ge(rows_ready, HALVES)
            for m in range(WOUT):
                for t in range(TT):
                    act.wait_ge(w_done, 2 * (WIN + m) + t + 1)
                    if 2 * m + t >= 2:
                        act.wait_ge(mix_square, 2 * m + t - 1)
                    nc.scalar.activation(gain_rows[:, CH * t:CH * t + CH], ps[:, W0B + t, :], ACT.Square,
                                         accum_out=stats[:, 56 + 4 * t + m:57 + 4 * t + m]).then_inc(mix_square, 1)
                    nc.scalar.copy(av[:, t, CH * m:CH * m + CH], ps[:, W0B + t, :]).then_inc(z_out, 1)
            for t in range(TT):
                act.wait_ge(h_ready, t + 1)
                nc.scalar.activation(Y[:, t, :], hv[:, t, :], ACT.Square,
                                     accum_out=stats[:, 64 + t:65 + t]).then_inc(h_square, 1)
            for n in range(8):
                t_copy("fT", n, T[:, 4 * (n % 4):4 * (n % 4) + 4, P * (n // 4):P * (n // 4) + P])
            act.wait_ge(gap_ready, 1)
            nc.scalar.activation(route[:, 200:210], route[:, 180:190], ACT.Exp).then_inc(gap_exp, 1)

            def gather_out(g, width):
                for u in range(8):
                    act.wait_ge(gathered, g * 8 + (u + 2))
                    nc.scalar.copy(xT[:, 2 * u:2 * u + 2, 0:width],
                                   ps[:, GATHER_BANK[u], 0:2 * width].rearrange("p (c s) -> p c s", c=2)).then_inc(xT_ready, 1)

            def expert(i):
                wait_products(act, GATE_UP, i)
                act.wait_ge(hid_ready, i + 1)
                nc.scalar.activation(silu_s, ps[:, 0, :], ACT.Silu).then_inc(silu_ready, 1)
                act.wait_ge(wpickT_done, i + 2)
                nc.scalar.copy(wpickT, ps[:, 7, 0:256]).then_inc(wpickT_ready, 1)
                wait_products(act, DOWN, i)
                nc.scalar.copy(down_s[:], flat[:, 2560:3584]).then_inc(down_ready, 1)

            for s in (wpickT_ready, down_ready):
                act.sem_inc(s, 1)
            with act.Fori(0, GROUPS) as g:
                gather_out(g, EPG * BLK)
                for m in range(EPG):
                    expert(g * EPG + m)
            act.wait_ge(list_ready, 1)
            n_extra = act.value_load(items[0:1, 0:1], min_val=0, max_val=MAX_EXTRA)
            with act.If(n_extra > 0):
                with act.Fori(0, n_extra) as j:
                    gather_out(j + GROUPS, BLK)
                    expert(j + E)
            for t in range(TT):
                act.wait_ge(summed, n_extra * 8 + (8 * E + 4 * t + 5))
                nc.scalar.activation(av[:, t, :], Y[:, t, :], ACT.Square,
                                     accum_out=stats[:, 68 + t:69 + t]).then_inc(out_square, 1)

        @block.vector
        def _(dve):
            ch = Steps(dve, vec_chain)
            V = nc.vector

            def rsqrt_mean(to, square_sum, n):
                w = to.shape[-1]
                v, y, t = (newton[:, 4 * k:4 * k + w] for k in range(3))
                ch.link(V.tensor_scalar(v, square_sum, 1.0 / n, EPS, ALU.mult, ALU.add))
                ch.link(V.tensor_scalar(y.bitcast(I32), v.bitcast(I32), 1, None, ALU.logical_shift_right))
                ch.link(V.tensor_scalar(y.bitcast(I32), y.bitcast(I32), -1.0, float(0x5f3759df), ALU.mult, ALU.add))
                for step in range(3):
                    ch.link(V.tensor_tensor(t, y, y, ALU.mult))
                    ch.link(V.scalar_tensor_tensor(t, t, -0.5, v, ALU.mult, ALU.mult))
                    last = V.scalar_tensor_tensor(y if step < 2 else to, t, 1.5, y, ALU.add, ALU.mult)
                    if step < 2:
                        ch.link(last)
                return last

            dve.wait_ge(vec_ps, 1)
            ch.link(V.tensor_copy(vec_cols[:], ps[:, 7, 0:40]))
            V.tensor_copy(c_wide[:], vec_cols[:, 0:16].unsqueeze(2).broadcast_to([P, KC, 32])).then_inc(c_ready, 1)

            dve.wait_ge(small_in, 7 * 16)
            dve.wait_ge(constants, 2)
            ch.link(V.tensor_copy(stats[:, 4:6], pos_i[:]))
            for t in range(TT):
                ins = V.tensor_scalar(angle[:, 0, t, :], inv_freq[:], stats[:, 4 + t:5 + t], None, ALU.mult)
            ch.link(ins)
            ch.link(V.tensor_copy(angle[:, 1], angle[:, 0]))
            ch.link(V.tensor_scalar(turns[:, 0], angle[:, 0], float(0.5 / np.pi), None, ALU.mult))
            ch.link(V.tensor_scalar(turns[:, 1], angle[:, 1], float(0.5 / np.pi), 0.25, ALU.mult, ALU.add))
            ch.link(V.tensor_scalar(turns, turns, MAGIC, None, ALU.add))
            ch.link(V.tensor_scalar(turns, turns, -MAGIC, None, ALU.add))
            af, tf = (b.rearrange("p a t n -> p (a t n)") for b in (angle[:], turns))
            for part in TWO_PI:
                ch.link(V.scalar_tensor_tensor(af, tf, -part, af, ALU.mult, ALU.add))
            ch.link(V.tensor_scalar(angle[:, 1], angle[:, 1], float(np.pi / 2), None, ALU.add))
            V.tensor_scalar(af, af, PI_SAFE, -PI_SAFE, ALU.min, ALU.max).then_inc(trig_in, 1)

            dve.wait_ge(x_square, TT)
            ch.link(rsqrt_mean(stats[:, 2:4], stats[:, 0:2], D))

            def rows(n):
                kind = n // 2
                dve.wait_ge(slot_free[3], n + 1)
                dve.wait_ge(bias_in, 16 * (n + 1))
                if n:
                    dve.wait_ge(wide_done, n)
                gained = kind in gain_of
                if kind in (SC1, SC2):
                    ins = V.scalar_tensor_tensor(mod_rows[:], ada_acc, row0[:, 0:1], bias_rows[:], ALU.add, ALU.add)
                else:
                    ins = V.tensor_tensor(mod_rows[:], ada_acc, bias_rows[:], ALU.add)
                if gained:
                    ch.link(ins)
                    dve.wait_ge(gainrow_in, 16 * n_gained[n])
                    ins = V.tensor_tensor(mod_rows[:], mod_rows[:], gain_rows[:], ALU.mult)
                ins.then_inc(rows_ready, 1)

            def t_copy(name, n, to):
                g = T_AT[name, n]
                if g % 2 == 0:
                    dve.wait_ge(t_done, g + 1)
                    src = ps[:, T0B, :]
                    if name == "fT":
                        src = src.rearrange("p (k s) -> p k s", k=4)
                    V.tensor_copy(to, src).then_inc(t_out[0], 1)

            def scale_half(h):
                dve.wait_ge(wide_out, h + 1)
                cols = slice(HALF * h, HALF * h + HALF)
                for t in range(TT):
                    ins = V.scalar_tensor_tensor(av[:, t, cols], xv[:, t, cols], stats[:, 2 + t:3 + t], G1[:, cols], ALU.mult, ALU.mult)
                ins.then_inc(scaled, 1)

            def shift_half(h):
                dve.wait_ge(wide_out, 3 + h)
                dve.wait_ge(scaled, h + 1)
                cols = slice(HALF * h, HALF * h + HALF)
                for t in range(TT):
                    ins = V.tensor_tensor(av[:, t, cols], av[:, t, cols], sh1[:, cols], ALU.add)
                ins.then_inc(a_ready, 1)

            rows(0)
            rows(1)
            scale_half(0)
            rows(2)
            scale_half(1)
            rows(3)
            shift_half(0)
            for n in range(4):
                t_copy("aT", n, T[:, 2 * n:2 * n + 2, :])
            shift_half(1)
            for n in range(4, 8):
                t_copy("aT", n, T[:, 2 * n:2 * n + 2, :])
            for n in range(2):
                t_copy("wsT", n, wsT[:, 4 * n:4 * n + 4, :])
            for n in (4, 5, 6):
                rows(n)

            dve.wait_ge(z_out, 6)
            dve.wait_ge(trig, 1)
            NQ = HEADS + KV
            rope_tmp = A[:, 0:4 * NQ * HR].rearrange("p (n h r) -> p n h r", n=4, r=HR)
            for t in range(TT):
                qk = zv[:, t, 0:NQ * HD].rearrange("p (h d) -> p h d", d=HD)
                x1, x2 = qk[:, :, 0:HR], qk[:, :, HR:ROPE]
                sin, cos = (angle[:, k, t, :].unsqueeze(1).broadcast_to([P, NQ, HR]) for k in range(2))
                V.tensor_tensor(rope_tmp[:, 0], x1, cos, ALU.mult)
                V.tensor_tensor(rope_tmp[:, 1], x2, sin, ALU.mult)
                V.tensor_tensor(rope_tmp[:, 2], x2, cos, ALU.mult)
                ch.link(V.tensor_tensor(rope_tmp[:, 3], x1, sin, ALU.mult))
                V.tensor_tensor(x1, rope_tmp[:, 0], rope_tmp[:, 1], ALU.subtract)
                V.tensor_tensor(x2, rope_tmp[:, 2], rope_tmp[:, 3], ALU.add).then_inc(roped, 1)
                dve.wait_ge(roped, t + 1)
            rows(7)
            for n in range(2):
                t_copy("q0", n, qT[:, 4 * n:4 * n + 4, :])
            t_copy("k", 0, kT)

            def scores(t):
                for n in range(4):
                    t_copy(f"s{t}", n, S[:, 2 * n:2 * n + 2, :])
                dve.wait_ge(t_out[0], (T_AT[f"s{t}", 3] + 2) // 2)
                dve.wait_ge(t_out[1], (T_AT[f"s{t}", 3] + 1) // 2)
                if t:
                    dve.wait_ge(probs, t)
                ch.link(V.tensor_reduce(stats[:, 8:16], S, AX.X, ALU.max))
                ch.link(V.scalar_tensor_tensor(stats[:, 8:16], stats[:, 8:16], SCALE, sink_b[:], ALU.mult, ALU.max))
                V.tensor_tensor(stats[:, 40:48], sink_b[:], stats[:, 8:16], ALU.subtract)
                V.tensor_scalar(stats[:, 16:24], stats[:, 8:16], -1.0, None, ALU.mult).then_inc(bias_max, 1)

            def probs_out(t):
                dve.wait_ge(probs, t + 1)
                ch.link(V.tensor_tensor(stats[:, 72:80], stats[:, 24:32], stats[:, 32:40], ALU.add))
                ch.link(V.reciprocal(stats[:, 80:88], stats[:, 72:80]))
                for n in range(4):
                    if T_AT[f"p{t}", n] % 2 == 0 and (n >= 2 or t):
                        dve.wait_ge(pv_done, 4 * t + n - 1)
                    t_copy(f"p{t}", n, pT[n % 2])
                dve.wait_ge(pv_done, 4 * t + 4)
                o = zv[:, t, 0:1024].rearrange("p (h d) -> p h d", d=HD)
                V.tensor_tensor(o, flat[:, CH * W0B:CH * W0B + 1024].rearrange("p (h d) -> p h d", d=HD),
                                stats[:, 80:88].unsqueeze(2).broadcast_to([P, HEADS, HD]), ALU.mult).then_inc(o_out, 1)

            scores(0)
            rows(8)
            probs_out(0)
            for n in range(2):
                t_copy("q1", n, qT[:, 4 * n:4 * n + 4, :])
            scores(1)
            rows(9)
            probs_out(1)

            dve.wait_ge(y_square, 2)
            ch.link(rsqrt_mean(stats[:, 52:54], stats[:, 48:50], 1024))
            for t in range(TT):
                V.tensor_scalar(zv[:, t, 0:1024], zv[:, t, 0:1024], stats[:, 52 + t:53 + t], None, ALU.mult)

            dve.wait_ge(gain_in, 16)
            for m in (5, 6):
                for t in range(TT):
                    dve.wait_ge(z_out, 2 * m + t + 1)
                    v = zv[:, t, CH * m:CH * m + CH].rearrange("p (h d) -> p h d", d=HD)
                    sq = A[:, 0:CH].rearrange("p (h d) -> p h d", d=HD)
                    mu, var = stats[:, 88:92], stats[:, 92:96]

                    def wide_of(s):
                        return s.unsqueeze(2).broadcast_to([P, 4, HD])

                    ch.link(V.tensor_reduce(mu, v, AX.X, ALU.add))
                    ch.link(V.tensor_scalar(mu, mu, -1.0 / HD, None, ALU.mult))
                    ch.link(V.tensor_tensor(v, v, wide_of(mu), ALU.add))
                    ch.link(V.tensor_tensor(sq, v, v, ALU.mult))
                    ch.link(V.tensor_reduce(var, sq, AX.X, ALU.add))
                    ch.link(rsqrt_mean(var, var, HD))
                    ch.link(V.tensor_tensor(v, v, wide_of(var), ALU.mult))
                    g = gain_v[:, CH * (m - 5):CH * (m - 5) + CH].rearrange("p (h d) -> p h d", d=HD)
                    V.tensor_tensor(v, v, g, ALU.mult).then_inc(vn_ready, 1)
            for n in range(4):
                hh, t = n // 2, n % 2
                dve.wait_ge(mixed_done, n + 1)
                for k in range(4):
                    h = 4 * hh + k
                    u = zv[:, t, O_U + HD * h:O_U + HD * h + HD]
                    ins = V.scalar_tensor_tensor(u, ps[:, W0B + n % 2, HD * k:HD * k + HD],
                                                 vec_cols[:, 32 + h:33 + h], u, ALU.add, ALU.mult)
                ins.then_inc(gated, 1)
            rows(10)
            dve.wait_ge(y_square, 4)
            ch.link(rsqrt_mean(stats[:, 54:56], stats[:, 50:52], 1024))
            for t in range(TT):
                u = zv[:, t, O_U:O_U + 1024]
                ins = V.tensor_scalar(u, u, stats[:, 54 + t:55 + t], None, ALU.mult)
            ins.then_inc(y_ready, 1)
            for n in range(8):
                if T_AT["yT", n] % 2 == 0:
                    dve.wait_ge(t_done, T_AT["yT", n] + 1)
                    for k in range(2):
                        ins = V.tensor_scalar(T[:, 2 * n + k, :], ps[:, T0B, SEQ * k:SEQ * k + SEQ],
                                              vec_cols[:, 16 + 2 * n + k:17 + 2 * n + k], None, ALU.mult)
                    ins.then_inc(t_out[0], 1)
                if n == 3:
                    rows(11)

            dve.wait_ge(mix_square, 2 * WOUT)
            ch.link(V.tensor_reduce(stats[:, 4:6], stats[:, 56:64].rearrange("p (t m) -> p t m", t=TT), AX.X, ALU.add))
            ch.link(rsqrt_mean(stats[:, 6:8], stats[:, 4:6], D))
            dve.wait_ge(z_out, 2 * (WIN + WOUT))
            dve.wait_ge(x2_in, 16)
            dve.wait_ge(wide_out, HALVES)
            for t in range(TT):
                ch.link(V.scalar_tensor_tensor(av[:, t, :], av[:, t, :], stats[:, 6 + t:7 + t], Gt[:, 0, :], ALU.mult, ALU.mult))
                V.tensor_tensor(hv[:, t, :], hv[:, t, :], av[:, t, :], ALU.add).then_inc(h_ready, 1)
            for t in range(TT):
                dve.wait_ge(h_square, t + 1)
                ch.link(rsqrt_mean(stats[:, 66 + t:67 + t], stats[:, 64 + t:65 + t], D))
                ch.link(V.scalar_tensor_tensor(av[:, t, :], hv[:, t, :], stats[:, 66 + t:67 + t], G2, ALU.mult, ALU.mult))
                V.tensor_tensor(av[:, t, :], av[:, t, :], sh2, ALU.add).then_inc(f_ready, 1)
            for n in range(8):
                t_copy("fT", n, T[:, 4 * (n % 4):4 * (n % 4) + 4, P * (n // 4):P * (n // 4) + P])

            def r3(at, n):
                return route[:, at:at + TT * n].rearrange("p (t n) -> p t n", t=TT)

            def r1(at):
                return route[:, at:at + TT]

            iota4 = route[:, 0:4].unsqueeze(1).broadcast_to([P, TT, 4])

            def over4(s):
                return s.unsqueeze(2).broadcast_to([P, TT, 4])

            def first_of(to, logits, top, work, at):
                ch.link(V.tensor_tensor(work, logits, over4(top), ALU.is_lt))
                ch.link(V.scalar_tensor_tensor(work, work, 100.0, iota4, ALU.mult, ALU.add))
                ch.link(V.tensor_reduce(at, work, AX.X, ALU.min))
                return V.tensor_tensor(to, iota4, over4(at), ALU.is_equal)

            L = r3(8, 20)
            work, at = r3(48, 4), r1(56)
            gmax, pick_g = r1(58), r3(60, 4)
            esel, m1, oh1, m2, oh2 = r3(68, 4), r1(76), r3(78, 4), r1(86), r3(88, 4)
            weighted = route[:, 96:128].rearrange("p (t g e) -> p t g e", t=TT, g=GROUPS)
            esel2 = r3(130, 4)
            gaps = r3(180, 5)
            gexp = r3(200, 5)
            dve.wait_ge(logits_done, 1)
            dve.wait_ge(constants, 3)
            bias = router_b[:].unsqueeze(1).broadcast_to([P, TT, 20])
            ch.link(V.tensor_tensor(L, ps[:, W0B, 0:40].rearrange("p (t n) -> p t n", t=TT), bias, ALU.add))
            ch.link(V.tensor_reduce(gmax, L[:, :, 0:4], AX.X, ALU.max))
            V.tensor_tensor(gaps[:, :, 0:4], L[:, :, 0:4], over4(gmax), ALU.subtract)
            ch.link(first_of(pick_g, L[:, :, 0:4], gmax, work, at))
            for t in range(TT):
                ins = V.tensor_tensor(weighted[:, t], L[:, t, 4:20].rearrange("p (g e) -> p g e", g=GROUPS),
                                      pick_g[:, t].unsqueeze(2).broadcast_to([P, GROUPS, EPG]), ALU.mult)
            ch.link(ins)
            ch.link(V.tensor_reduce(esel, weighted.rearrange("p t g e -> p t e g"), AX.X, ALU.add))
            ch.link(V.tensor_reduce(m1, esel, AX.X, ALU.max))
            ch.link(first_of(oh1, esel, m1, work, at))
            ch.link(V.scalar_tensor_tensor(esel2, oh1, -1e38, esel, ALU.mult, ALU.add))
            ch.link(V.tensor_reduce(m2, esel2, AX.X, ALU.max))
            V.tensor_tensor(gaps[:, :, 4], m2, m1, ALU.subtract).then_inc(gap_ready, 1)
            ch.link(first_of(oh2, esel2, m2, work, at))
            both = r3(140, 4)
            ch.link(V.tensor_tensor(both, oh1, oh2, ALU.add))
            member = route[:, 220:252].rearrange("p (t g e) -> p t g e", t=TT, g=GROUPS)
            comb = route[:, 252:284].rearrange("p (t g e) -> p t g e", t=TT, g=GROUPS)
            for t in range(TT):
                ins = V.tensor_tensor(member[:, t], pick_g[:, t].unsqueeze(2).broadcast_to([P, GROUPS, EPG]),
                                      both[:, t].unsqueeze(1).broadcast_to([P, GROUPS, EPG]), ALU.mult)
            ins.then_inc(chosen, 1)
            dve.wait_ge(gap_exp, 1)
            den, w1, w2, wsum = r1(150), r1(152), r1(154), r1(156)
            ch.link(V.tensor_reduce(wsum, gexp[:, :, 0:4], AX.X, ALU.add))
            ch.link(V.tensor_scalar(den, gexp[:, :, 4], 1.0, None, ALU.add))
            ch.link(V.tensor_tensor(den, den, wsum, ALU.mult))
            ch.link(V.reciprocal(w1, den))
            ch.link(V.tensor_tensor(w2, w1, gexp[:, :, 4], ALU.mult))
            V.tensor_tensor(oh1, oh1, over4(w1), ALU.mult)
            ch.link(V.tensor_tensor(oh2, oh2, over4(w2), ALU.mult))
            ch.link(V.tensor_tensor(both, oh1, oh2, ALU.add))
            for t in range(TT):
                ins = V.tensor_tensor(comb[:, t], pick_g[:, t].unsqueeze(2).broadcast_to([P, GROUPS, EPG]),
                                      both[:, t].unsqueeze(1).broadcast_to([P, GROUPS, EPG]), ALU.mult)
            ch.link(ins)
            rank = route[:, 284:316]
            dve.wait_ge(ranks_done, 1)
            memf = route[:, 220:252]
            ch.link(V.scalar_tensor_tensor(rank, memf, -FAR, ps[:, W0B + 1, 0:32], ALU.mult, ALU.add))
            ch.link(V.tensor_scalar(rank, rank, FAR, None, ALU.add))
            ch.link(V.memset(T[:], 0.0))

            combf = route[:, 252:284]

            def list_blocks():
                f = items_f[0:1, :]
                e_id, b_id, j_id = f[:, 0:48], f[:, 48:96], f[:, 96:103]
                flag, run = f[:, 103:151], f[:, 151:199]
                for b in range(1, BLOCKS):
                    ins = V.tensor_scalar(flag[:, 16 * (b - 1):16 * b], ps[0:1, W0B + 1, 32:48], float(CAP * b), None, ALU.is_gt)
                ch.link(ins)
                ch.link(V.tensor_copy(run, flag))
                step = 1
                tmp48 = f[:, 200:248]
                while step < 48:
                    ch.link(V.tensor_copy(tmp48, run))
                    ch.link(V.tensor_tensor(run[:, step:48], tmp48[:, step:48], tmp48[:, 0:48 - step], ALU.add))
                    step *= 2
                sel = f[:, 248:248 + 7 * 48].rearrange("p (j n) -> p j n", j=7)

                def over_j(s):
                    return s.unsqueeze(1).broadcast_to([1, 7, 48])

                prod = f[:, 600:600 + 7 * 48].rearrange("p (j n) -> p j n", j=7)
                got = f[:, 940:957]
                ch.link(V.tensor_tensor(sel, over_j(run), j_id.unsqueeze(2).broadcast_to([1, 7, 48]), ALU.is_equal))
                ch.link(V.tensor_tensor(sel, sel, over_j(flag), ALU.mult))
                ch.link(V.tensor_tensor(prod, sel, over_j(e_id), ALU.mult))
                ch.link(V.tensor_reduce(got[:, 1:8], prod, AX.X, ALU.add))
                ch.link(V.tensor_tensor(prod, sel, over_j(b_id), ALU.mult))
                ch.link(V.tensor_reduce(got[:, 8:15], prod, AX.X, ALU.add))
                ch.link(V.tensor_copy(got[:, 0:1], run[:, 47:48]))
                V.tensor_copy(items[:, 0:15], got[:, 0:15]).then_inc(list_ready, 1)


            def picks(g, experts, ids):
                dve.wait_ge(gathered, g * 8 + 1)
                for m, e in enumerate(experts):
                    for t in range(TT):
                        ins = V.tensor_scalar(pick[:, t, BLK * m:BLK * m + BLK], ids[:, 0:BLK],
                                              rank[:, bass.ds(e + 16 * t, 1)], None, ALU.is_equal)
                ins.then_inc(pick_ready, 1)

            def add(i, n):
                t, col = n // 4, CH * (n % 4)
                dve.wait_ge(spread, i * 8 + (n + 1))
                V.tensor_tensor(Y[:, t, col:col + CH], Y[:, t, col:col + CH], ps[:, 2 + n % 2, :], ALU.add).then_inc(summed, 1)

            def expert(i, e, ids, then=None):
                dve.wait_ge(wpickT_done, i + 1)
                for t in range(TT):
                    ins = V.tensor_scalar(wpick[:, t, :], ids, rank[:, bass.ds(e + 16 * t, 1)],
                                          combf[:, bass.ds(e + 16 * t, 1)], ALU.is_equal, ALU.mult)
                ins.then_inc(wpick_ready, 1)
                if then:
                    then()
                dve.wait_ge(silu_ready, i + 1)
                dve.wait_ge(hidT_done, i + 1)
                V.tensor_tensor(hid, silu_s, ps[:, 1, :], ALU.mult).then_inc(hid_ready, 1)
                for n in range(4):
                    add(i, n)
                dve.wait_ge(hidT_done, i + 2)
                dve.wait_ge(slot_free[5], i * 2 + 1)
                V.tensor_copy(bias_rows[:, 0:CH], ps[:, 4, :]).then_inc(hidT_ready, 1)
                for n in range(4, 8):
                    add(i, n)
                dve.wait_ge(summed, i * 8 + 9)

            def group(g, then=None):
                picks(g, [g * EPG + m for m in range(EPG)], slot_id[:, 0, :])
                for m in range(EPG):
                    expert(g * EPG + m, g * EPG + m, slot_id[:, 0, :], then if m == 0 else None)

            V.memset(down_s[:], 0.0)
            ch.link(V.memset(wpickT, 0.0))
            for s in (hid_ready, summed):
                dve.sem_inc(s, 1)
            group(0, list_blocks)
            with dve.Fori(1, GROUPS) as g:
                group(g)
            n_extra = dve.value_load(items[0:1, 0:1], min_val=0, max_val=MAX_EXTRA)
            with dve.If(n_extra > 0):
                with dve.Fori(0, n_extra) as j:
                    e = dve.value_load(items[0:1, bass.ds(j + 1, 1)], min_val=0, max_val=E - 1)
                    b = dve.value_load(items[0:1, bass.ds(j + 8, 1)], min_val=1, max_val=BLOCKS - 1)
                    ids = slot_id[:, bass.ds(b, 1), :].rearrange("p b s -> p (b s)")
                    picks(j + GROUPS, [e], ids)
                    expert(j + E, e, ids)
            for n in range(8):
                add(n_extra + E, n)

            for t in range(TT):
                dve.wait_ge(out_square, t + 1)
                ch.link(rsqrt_mean(stats[:, 4 + t:5 + t], stats[:, 68 + t:69 + t], D))
                ch.link(V.scalar_tensor_tensor(Y[:, t, :], Y[:, t, :], stats[:, 4 + t:5 + t], Gt[:, 1, :], ALU.mult, ALU.mult))
                V.tensor_tensor(Y[:, t, :], Y[:, t, :], hv[:, t, :], ALU.add).then_inc(out_ready, 1)

        @block.tensor
        def _(pe):
            M = nc.tensor

            def t_bank(name, n):
                g = T_AT[name, n]
                if g >= 2:
                    pe.wait_ge(t_out[g % 2], g // 2)
                return ps[:, T0B + g % 2, :]

            pe.wait_ge(constants, 2)
            pe.wait_ge(c_silu, 1)
            pe.wait_ge(vec_in, 2 * 16)
            M.transpose(ps[:, 7, 0:40], vec_rows, ident[0:40, 0:40]).then_inc(vec_ps, 1)

            def ada(n):
                for s in range(4):
                    pe.wait_ge(landed[s], 16 * (n + 1))
                    if s == 0:
                        if n:
                            pe.wait_ge(rows_ready, n)
                        else:
                            pe.wait_ge(c_ready, 1)
                    for cc in range(2):
                        for j in range(4):
                            ins = M.matmul(ada_acc[32 * j:32 * j + 32, CH * cc:CH * cc + CH], c_wide[:, 4 * s + j, :],
                                           ada_slot(s)[:, j, CH * cc:CH * cc + CH], start=(s == 0), stop=(s == 3))
                    ins.then_inc(slot_free[s], 1)

            def widen(n):
                pe.wait_ge(rows_ready, n + 1)
                if n:
                    pe.wait_ge(wide_out, n)
                for cc in range(2):
                    ins = M.matmul(ada_wide[:, CH * cc:CH * cc + CH], rows4[:], mod_rows[:, CH * cc:CH * cc + CH], start=True, stop=True)
                ins.then_inc(wide_done, 1)

            def transposes(name, n, blocks):
                bank = t_bank(name, n)
                for k, src in enumerate(blocks):
                    ins = M.transpose(bank[:, P * k:P * k + P], src, ident[:])
                ins.then_inc(t_done, 1)

            def project(m):
                for half in range(2):
                    pe.wait_ge(chunk_in[half], 16 * (m + 1))
                    for t in range(TT):
                        if half == 0 and m:
                            pe.wait_ge(z_out, 2 * m - 1 + t)
                        for k in range(8):
                            kk = 8 * half + k
                            ins = M.matmul(ps[:, W0B + t, :], T[:, kk, P * t:P * t + P], chunk_slot(4 + half)[:, k, :],
                                           start=(kk == 0), stop=(kk == KC - 1))
                        if half == 0 and t == TT - 1:
                            ins.then_inc(slot_free[4], 1)
                        elif half == 1:
                            ins.then_inc(w_done, 1)

            ada(0)
            ada(1)
            widen(0)
            ada(2)
            widen(1)
            ada(3)
            widen(2)
            for half in range(2):
                if half:
                    widen(3)
                pe.wait_ge(a_ready, half + 1)
                for n in range(4 * half, 4 * half + 4):
                    transposes("aT", n, [av[:, t, P * k:P * k + P] for k in (2 * n, 2 * n + 1) for t in range(TT)])
            pe.wait_ge(small_in, 7 * 16)
            for n in range(2):
                transposes("wsT", n, [w_sp[:, h, :] for h in range(4 * n, 4 * n + 4)])
            pe.wait_ge(t_out[0], (T_AT["aT", 7] + 2) // 2)
            pe.wait_ge(t_out[1], (T_AT["aT", 7] + 1) // 2)
            for m in range(3):
                ada(4 + m)
                project(m)
                widen(4 + m)
            ada(7)

            def q_tile(t):
                pe.wait_ge(roped, TT)
                for n in range(2):
                    transposes(f"q{t}", n, [zv[:, t, HD * h:HD * h + HD] for h in range(4 * n, 4 * n + 4)])

            def scores(t):
                last = T_AT["k", 0] if t == 0 else T_AT["q1", 1]
                pe.wait_ge(t_out[0], (last + 2) // 2)
                pe.wait_ge(t_out[1], (last + 1) // 2)
                for n in range(4):
                    bank = t_bank(f"s{t}", n)
                    for k in range(2):
                        h = 2 * n + k
                        own = slice(SEQ * k, SEQ * k + SEQ)
                        edge = slice(SEQ * k + P * (1 - t), SEQ * k + P * (1 - t) + P)
                        M.matmul(bank[:, own], qT[:, h, :], kT[:, h // (HEADS // KV), :], start=True, stop=True)
                        ins = M.matmul(bank[:, edge], ident[:], mask[:, t, :], start=False, stop=True, skip_group_check=True)
                    ins.then_inc(t_done, 1)

            def attend(t):
                pe.wait_ge(probs, t + 1)

                def pv(n):
                    g = T_AT[f"p{t}", n]
                    pe.wait_ge(t_out[g % 2], g // 2 + 1)
                    if n == 0:
                        pe.wait_ge(z_out, 2 * (5 + t))
                    for k in range(2):
                        h = 2 * n + k
                        v0 = O_V + HD * (h // (HEADS // KV))
                        for kc in range(2):
                            ins = M.matmul(ps[:, W0B + h // 4, HD * (h % 4):HD * (h % 4) + HD], pT[n % 2][:, k, kc, :],
                                           zv[:, kc, v0:v0 + HD], start=(kc == 0), stop=(kc == 1))
                    ins.then_inc(pv_done, 1)

                for n in range(4):
                    transposes(f"p{t}", n, [S[:, h, P * kc:P * kc + P] for h in (2 * n, 2 * n + 1) for kc in range(2)])
                    if n:
                        pv(n - 1)
                pv(3)

            pe.wait_ge(roped, TT)
            q_tile(0)
            transposes("k", 0, [zv[:, t, O_K + HD * k:O_K + HD * k + HD] for k in range(KV) for t in range(TT)])
            project(3)
            widen(7)
            scores(0)
            ada(8)
            project(4)
            widen(8)
            attend(0)
            q_tile(1)
            scores(1)
            ada(9)
            pe.wait_ge(o_out, 1)
            project(5)
            widen(9)
            attend(1)
            pe.wait_ge(o_out, 2)
            project(6)
            ada(10)
            pe.wait_ge(z_out, 2 * WIN)
            for n in range(4):
                hh, t = n // 2, n % 2
                pe.wait_ge(vn_ready, n + 1)
                if n >= 2:
                    pe.wait_ge(gated, n - 1)
                for k in range(4):
                    h = 4 * hh + k
                    ins = M.matmul(ps[:, W0B + n % 2, HD * k:HD * k + HD], wsT[:, h, :],
                                   zv[:, t, O_G + HD * h:O_G + HD * h + HD], start=True, stop=True)
                ins.then_inc(mixed_done, 1)
            pe.wait_ge(gated, 4)
            widen(10)
            pe.wait_ge(y_ready, 1)
            for n in range(8):
                base = 0 if n < 4 else O_U - 1024
                transposes("yT", n, [zv[:, t, base + P * k:base + P * k + P] for k in (2 * n, 2 * n + 1) for t in range(TT)])
                if n == 3:
                    ada(11)
            pe.wait_ge(t_out[0], (T_AT["yT", 7] + 2) // 2)
            pe.wait_ge(t_out[1], (T_AT["yT", 7] + 1) // 2)
            for m in range(WOUT):
                project(WIN + m)
                if m == 0:
                    widen(11)

            for n in range(8):
                t = n // 4
                if n % 4 == 0:
                    pe.wait_ge(f_ready, t + 1)
                transposes("fT", n, [av[:, t, k:D:KC] for k in range(4 * (n % 4), 4 * (n % 4) + 4)])
            pe.wait_ge(t_out[0], (T_AT["fT", 7] + 2) // 2)
            pe.wait_ge(t_out[1], (T_AT["fT", 7] + 1) // 2)
            pe.wait_ge(z_out, 2 * (WIN + WOUT))
            for t in range(TT):
                for k in range(KC):
                    ins = M.matmul(ps[:, W0B, 20 * t:20 * t + 20], T[:, k, P * t:P * t + P], w_router[:, k, :],
                                   start=(k == 0), stop=(k == KC - 1))
            ins.then_inc(logits_done, 1)
            mem = [route[:, 220 + 16 * t:236 + 16 * t] for t in range(TT)]
            pe.wait_ge(chosen, 1)
            rb = ps[:, W0B + 1, :]
            M.matmul(rb[:, 0:16], before[:], mem[0], start=True, stop=True)
            M.matmul(rb[:, 16:32], ones[:], mem[0], start=True, stop=False)
            M.matmul(rb[:, 16:32], before[:], mem[1], start=False, stop=True)
            M.matmul(rb[:, 32:48], ones[:], mem[0], start=True, stop=False)
            M.matmul(rb[:, 32:48], ones[:], mem[1], start=False, stop=True).then_inc(ranks_done, 1)

            def gather(g, i, width):
                pe.wait_ge(pick_ready, g + 1)
                pe.wait_ge(summed, i * 8 + 1)
                for u in range(8):
                    if u >= 5:
                        pe.wait_ge(xT_ready, g * 8 + (u - 2))
                    for c in range(2):
                        k = 2 * u + c
                        for t in range(TT):
                            ins = M.matmul(ps[:, GATHER_BANK[u], width * c:width * c + width], av[:, t, P * k:P * k + P],
                                           pick[:, t, 0:width], start=(t == 0), stop=(t == TT - 1))
                    ins.then_inc(gathered, 1)

            def spread_part(i, n):
                t, col = n // 4, CH * (n % 4)
                h, cc = col // 1024, col % 1024
                if n >= 1:
                    pe.wait_ge(summed, i * 8 + n)
                else:
                    pe.wait_ge(wpickT_ready, i + 1)
                    pe.wait_ge(down_ready, i + 1)
                    pe.wait_ge(summed, i * 8 + 1)
                M.matmul(ps[:, 2 + n % 2, :], wpickT[64 * h:64 * h + 64, P * t:P * t + P],
                         down_s[64 * h:64 * h + 64, cc:cc + CH], start=True, stop=True).then_inc(spread, 1)

            def expert(i, g, m):
                for q in range(8):
                    s, n = q % SLOTS, q // 2
                    if m == 0 and q % 2 == 0:
                        pe.wait_ge(xT_ready, g * 8 + (2 * n + 2))
                    pe.wait_ge(landed[s], i * 32 + 16 * (USED[s] + q // SLOTS + 1))
                    for j in range(4):
                        k = 4 * n + j
                        for h in range(2):
                            ins = M.matmul(ps[64 * h:64 * h + 64, q % 2, :], xT[:, k, BLK * m:BLK * m + BLK],
                                           ada_slot(s)[:, j, CH * h:CH * h + CH], start=(k == 0), stop=(k == KC - 1))
                    ins.then_inc(slot_free[s], 1)
                for n in range(4):
                    spread_part(i, n)
                pe.wait_ge(hid_ready, i + 2)
                for t in range(4):
                    ins = M.transpose(ps[:, 4, P * t:P * t + P], hid[:, P * t:P * t + P], ident[:])
                ins.then_inc(hidT_done, 1)
                for n in range(4, 8):
                    spread_part(i, n)
                pe.wait_ge(wpick_ready, i + 1)
                for t in range(TT):
                    ins = M.transpose(ps[:, 7, P * t:P * t + P], wpick[:, t, :], ident[:])
                ins.then_inc(wpickT_done, 1)
                pe.wait_ge(hidT_ready, i + 1)
                for q in range(8, 12):
                    s = q % SLOTS
                    pe.wait_ge(landed[s], i * 32 + 16 * (USED[s] + q // SLOTS + 1))
                    for j in range(2):
                        k = 2 * (q - 8) + j
                        w = hidT[:, k % 4, 64 * (k // 4):64 * (k // 4) + 64]
                        for cc in range(2):
                            for h in range(2):
                                ins = M.matmul(ps[64 * h:64 * h + 64, 5 + cc, :], w,
                                               down_slot(s)[:, j, 1024 * h + CH * cc:1024 * h + CH * cc + CH],
                                               start=(k == 0), stop=(k == 7))
                    ins.then_inc(slot_free[s], 1)

            for s in (gathered, wpickT_done, hidT_done, slot_free[5]):
                pe.sem_inc(s, 1)
            with pe.Fori(0, GROUPS) as g:
                gather(g, g * EPG, EPG * BLK)
                for m in range(EPG):
                    expert(g * EPG + m, g, m)
            pe.wait_ge(list_ready, 1)
            n_extra = pe.value_load(items[0:1, 0:1], min_val=0, max_val=MAX_EXTRA)
            with pe.If(n_extra > 0):
                with pe.Fori(0, n_extra) as j:
                    gather(j + GROUPS, j + E, BLK)
                    expert(j + E, j + GROUPS, 0)
            for n in range(8):
                spread_part(n_extra + E, n)


_INS = ['x', 'c', 'positions', 'w_ada', 'b_ada', 'g_mix_pre', 'g_mix_post', 'w_in', 'sink_logits',
        'gmlp_norm_g', 'w_spatial', 'b_spatial', 'g_group_out', 'w_out', 'g_ffn_pre', 'g_ffn_post',
        'w_router_group', 'b_router_group', 'w_router_expert', 'b_router_expert', 'w_gate', 'w_up', 'w_down']


def kernel(**inputs):
    import numpy as _np
    import concourse.bacc as _bacc
    from concourse import mybir as _mybir
    from concourse.bass_utils import run_bass_kernel_spmd as _run

    nc = _bacc.Bacc("TRN2", target_bir_lowering=False, num_devices=1)
    arrays, args = {}, []
    for name in _INS:
        a = _np.ascontiguousarray(inputs[name])
        arrays[f"in_{name}"] = a
        args.append(nc.dram_tensor(f"in_{name}", a.shape, _mybir.dt.from_np(a.dtype), kind="ExternalInput").ap())
    args.append(nc.dram_tensor("out_0", (1, 256, 2048), _mybir.dt.float32, kind="ExternalOutput").ap())
    hybrid_block(nc, *args)
    r = _run(nc, [arrays], core_ids=[0])
    return r.results[0]["out_0"]
```

```python
from contextlib import ExitStack

import numpy as np

import concourse.bass as bass
from concourse import mybir

F32 = mybir.dt.float32
I32 = mybir.dt.int32
ALU = mybir.AluOpType
ACT = mybir.ActivationFunctionType
AX = mybir.AxisListType

P = 128
SEQ, D = 256, 2048
TT = SEQ // P
KC = D // P
HEADS, KV, HD = 8, 2, 128
N_IN = 3584
O_K, O_V, O_U, O_G = 1024, 1280, 1536, 2560
GROUPS, EPG = 4, 4
E = GROUPS * EPG
FF = 1024
HALF = 1024
CH = 512
WIN = N_IN // CH
WOUT = D // CH
BLK = 64
BLOCKS = SEQ // BLK
CAP = BLK
MAX_EXTRA = (2 * SEQ - 1) // (CAP + 1)
SLOTS = 6
ROPE = HD // 4
HR = ROPE // 2
THETA = 500000.0
EPS = 1e-6
SCALE = HD ** -0.5
NEG = -1e30
FAR = 4096.0
MAGIC = 12582912.0
TWO_PI = (6.28125, 1.9340515136718750e-3, 1.2556659146735911e-6)
PI_SAFE = 3.1415925

SC1, SH1, GT1, GT2, SH2, SC2 = range(6)
MOD_COLUMN = {SH1: 0, SC1: 1, GT1: 2, SH2: 3, SC2: 4, GT2: 5}
HALVES = 12
PE_HALVES = (0, 1, 2, 3, 9)

T_GROUPS = ([("aT", n) for n in range(8)] + [("wsT", n) for n in range(2)]
            + [("q0", n) for n in range(2)] + [("k", 0)] + [("s0", n) for n in range(4)]
            + [("p0", n) for n in range(4)] + [("q1", n) for n in range(2)]
            + [("s1", n) for n in range(4)] + [("p1", n) for n in range(4)]
            + [("yT", n) for n in range(8)])
T_AT = {g: i for i, g in enumerate(T_GROUPS)}



class Steps:

    def __init__(self, engine, sem):
        self.engine, self.sem, self.n = engine, sem, 0

    def add(self, ins):
        ins.then_inc(self.sem, 1)
        self.n += 1
        return self.n

    def link(self, ins):
        self.engine.wait_ge(self.sem, self.add(ins))


def hybrid_block(nc, x, c, positions, w_ada, b_ada, g_mix_pre, g_mix_post, w_in, sink,
                 gmlp_g, w_spatial, b_spatial, g_group, w_out, g_ffn_pre, g_ffn_post,
                 w_rg, b_rg, w_re, b_re, w_gate, w_up, w_down, out):
    with ExitStack() as ctx:
        def sb(name, shape, dt=F32):
            return ctx.enter_context(nc.sbuf_tensor(name, shape, dt))

        def sem(name):
            return ctx.enter_context(nc.semaphore(name))

        ring = sb("ring", [P, SLOTS, 4096])
        X = sb("X", [P, 4096])
        Gt = sb("Gt", [P, 2, D])
        A = sb("A", [P, 4096])
        T = sb("T", [P, KC, SEQ])
        Z = sb("Z", [P, TT * N_IN])
        mod_rows = sb("mod_rows", [P, HALF])
        bias_rows = sb("bias_rows", [P, HALF])
        gain_rows = sb("gain_rows", [P, HALF])
        c_wide = sb("c_wide", [P, KC, 32])
        w_router = sb("w_router", [P, KC, GROUPS + E])
        ident = sb("ident", [P, P])
        rows4 = sb("rows4", [P, P])
        before = sb("before", [P, P])
        mask = sb("mask", [P, TT, P])
        vec_rows = c_wide[:].rearrange("p k n -> p (k n)")[0:40, 0:P]
        vec_cols = sb("vec_cols", [P, 40])

        xv = X[:].rearrange("p (t d) -> p t d", t=TT)
        av = A[:].rearrange("p (t d) -> p t d", t=TT)
        zv = Z[:].rearrange("p (t n) -> p t n", t=TT)
        hv = Z[:, 0:TT * D].rearrange("p (t d) -> p t d", t=TT)
        G1, sh1 = Z[:, 0:D], Z[:, D:2 * D]
        w_sp = Z[:, 4096:5120].rearrange("p (h q) -> p h q", h=HEADS)
        wsT = X[:, 0:1024].rearrange("p (h q) -> p h q", h=HEADS)
        gain_v = X[:, 1024:2048]
        G2, sh2 = X[:, 0:D], X[:, D:2 * D]
        kT = A[:, 0:512].rearrange("p (k s) -> p k s", k=KV)
        qT = A[:, 512:1536].rearrange("p (h s) -> p h s", h=HEADS)
        S = A[:, 1536:3584].rearrange("p (h s) -> p h s", h=HEADS)
        pT = [A[:, 3584:4096], A[:, 512:1024]]
        pT = [b.rearrange("p (h c s) -> p h c s", h=2, c=2) for b in pT]
        xT = X[:].rearrange("p (c s) -> p c s", c=KC)
        silu_s, hid = mod_rows[:, 0:CH], mod_rows[:, CH:2 * CH]
        hidT = bias_rows[:, 0:CH].rearrange("p (t s) -> p t s", t=4)
        down_s = gain_rows
        pick = Gt[:, 0, 0:TT * EPG * BLK].rearrange("p (t s) -> p t s", t=TT)
        wpick = Gt[:, 0, 1024:1024 + TT * P].rearrange("p (t s) -> p t s", t=TT)
        Y = T[:].rearrange("p c s -> p (c s)").rearrange("p (t d) -> p t d", t=TT)
        ZM = Z[:, 4096:7168]
        wpickT = ZM[:, 0:256]
        slot_id = ZM[:, 256:256 + BLOCKS * P].rearrange("p (b s) -> p b s", b=BLOCKS)
        route = ZM[:, 768:1536]
        items_f = ZM[0:1, 1536:1536 + 1024]
        mix_scratch = ZM[:, 2560:2560 + CH]
        ones = sb("ones", [P, P])
        inv_freq = sb("inv_freq", [P, HR])
        pos_i = sb("pos_i", [P, TT], I32)
        angle = sb("angle", [P, 2, TT, HR])
        turns = mod_rows[:, 0:2 * TT * HR].rearrange("p (a t n) -> p a t n", a=2, t=TT)
        sink_b = sb("sink_b", [P, HEADS])
        router_b = sb("router_b", [P, GROUPS + E])
        stats = sb("stats", [P, 96])
        newton = sb("newton", [P, 12])
        row0 = sb("row0", [P, 1])
        bn = sb("bn", [P, 6 * 4 + 2 * 4])
        items = sb("items", [1, 32], I32)

        ps = ctx.enter_context(nc.psum_tensor("ps", [P, 8, CH], F32))
        flat = ps[:].rearrange("p b n -> p (b n)")
        ada_acc, ada_wide = flat[:, 0:1024], flat[:, 1024:2048]
        W0B, T0B = 4, 6

        x_in, small_in, vec_in, c_in, gain_in, x2_in = (sem(n) for n in (
            "x_in", "small_in", "vec_in", "c_in", "gain_in", "x2_in"))
        landed = [sem(f"landed{s}") for s in range(SLOTS)]
        slot_free = [sem(f"slot_free{s}") for s in range(SLOTS)]
        chunk_in = [sem(f"chunk_in{s}") for s in range(2)]
        bias_in, gainrow_in = sem("bias_in"), sem("gainrow_in")
        constants = sem("constants")
        vec_chain, act_chain, pool_chain = sem("vec_chain"), sem("act_chain"), sem("pool_chain")
        c_silu, vec_ps, c_ready = sem("c_silu"), sem("vec_ps"), sem("c_ready")
        x_square = sem("x_square")
        rows_ready, wide_done, wide_out = sem("rows_ready"), sem("wide_done"), sem("wide_out")
        scaled, a_ready = sem("scaled"), sem("a_ready")
        fT_done, fT_out = sem("fT_done"), [sem("fT_out_vector"), sem("fT_out_scalar")]
        y_clear = sem("y_clear")
        t_done = sem("t_done")
        t_out = [sem("t_out_vector"), sem("t_out_scalar")]
        w_done, z_out = sem("w_done"), sem("z_out")
        trig_in, trig = sem("trig_in"), sem("trig")
        roped = sem("roped")
        bias_max, probs, pv_done, o_out = sem("bias_max"), sem("probs"), sem("pv_done"), sem("o_out")
        vn_ready, mixed_done, gated = sem("vn_ready"), sem("mixed_done"), sem("gated")
        y_square, y_ready = sem("y_square"), sem("y_ready")
        mix_square, h_ready, h_square, f_ready = (sem(n) for n in (
            "mix_square", "h_ready", "h_square", "f_ready"))
        logits_done, gap_ready, gap_exp = sem("logits_done"), sem("gap_ready"), sem("gap_exp")
        chosen, ranks_done, list_ready = sem("chosen"), sem("ranks_done"), sem("list_ready")
        pick_ready, gathered, xT_ready = sem("pick_ready"), sem("gathered"), sem("xT_ready")
        wpick_ready, wpickT_done, wpickT_ready = (sem(n) for n in (
            "wpick_ready", "wpickT_done", "wpickT_ready"))
        silu_ready, hid_ready = sem("silu_ready"), sem("hid_ready")
        hidT_done, hidT_ready = sem("hidT_done"), sem("hidT_ready")
        down_ready = sem("down_ready")
        spread, summed = sem("spread"), sem("summed")
        out_square, out_ready, stored = (sem(n) for n in ("out_square", "out_ready", "stored"))

        x_d = x.rearrange("a (t p) d -> p (a t) d", p=P)
        out_d = out.rearrange("a (t p) d -> p (a t) d", p=P)
        ada_d = w_ada[0].rearrange("(k p) n -> p k n", p=P)
        win_d = w_in[0].rearrange("(k p) n -> p k n", p=P)
        wout_d = w_out[0].rearrange("(k p) n -> p k n", p=P)
        gate_d = w_gate.rearrange("a g e (k p) f -> p (a g e) k f", p=P)
        up_d = w_up.rearrange("a g e (k p) f -> p (a g e) k f", p=P)
        down_d = w_down.rearrange("a g e (k p) d -> p (a g e) k d", p=P)
        gain_of = {SC1: g_mix_pre, GT1: g_mix_post, SC2: g_ffn_pre, GT2: g_ffn_post}
        mod_to = {SC1: G1, SH1: sh1, GT1: Gt[:, 0, :], GT2: Gt[:, 1, :], SH2: sh2, SC2: G2}
        n_gained = [sum(1 for m in range(n + 1) if m // 2 in gain_of) for n in range(HALVES)]

        def pe_halves(n):
            return sum(1 for m in range(n) if m in PE_HALVES)

        def ada_slot(s):
            return ring[:, s, :].rearrange("p (k n) -> p k n", k=4)

        def chunk_slot(s):
            return ring[:, s, :].rearrange("p (k n) -> p k n", k=8)

        def down_slot(s):
            return ring[:, s, :].rearrange("p (k n) -> p k n", k=2)

        USED = [HALVES] * 4 + [0, 0]
        FREED = [HALVES] * 4 + [WIN + WOUT, 1]

        def wait_products(eng, last, i):
            eng.wait_ge(slot_free[last % SLOTS], i * 2 + (FREED[last % SLOTS] + last // SLOTS + 1))

        GATHER_BANK = [0, 1, 2, 3, 4, 2, 3, 4]
        GATE_UP, DOWN = 7, 11

        block = ctx.enter_context(nc.Block())

        @block.sync
        def _(sp):
            for n in range(HALVES):
                col = D * MOD_COLUMN[n // 2] + HALF * (n % 2)
                for s in range(4):
                    if n:
                        sp.wait_ge(slot_free[s], n)
                    sp.dma_start(ada_slot(s), ada_d[:, 4 * s:4 * s + 4, col:col + HALF]).then_inc(landed[s], 16)
                if n == 0:
                    sp.wait_ge(constants, 1)
                else:
                    sp.wait_ge(rows_ready, n)
                sp.dma_start(bias_rows[0:1, :], b_ada[0:1, col:col + HALF]).then_inc(bias_in, 16)
                if n // 2 in gain_of:
                    g = gain_of[n // 2][0:1, HALF * (n % 2):HALF * (n % 2 + 1)]
                    to = gain_rows[0:97:32, :] if n in PE_HALVES else gain_rows[:]
                    sp.dma_start(to, g.broadcast_to([to.shape[0], HALF])).then_inc(gainrow_in, 16)

            def load_expert(i, e):
                for q in range(12):
                    s = q % SLOTS
                    sp.wait_ge(slot_free[s], i * 2 + (FREED[s] + q // SLOTS))
                    if q == 5:
                        sp.wait_ge(w_done, TT * (WIN + WOUT))
                    if q < 8:
                        w = gate_d if q % 2 == 0 else up_d
                        src, dst = w[:, bass.ds(e, 1), 4 * (q // 2):4 * (q // 2) + 4, :], ada_slot(s)
                    else:
                        src, dst = down_d[:, bass.ds(e, 1), 2 * (q - 8):2 * (q - 8) + 2, :], down_slot(s)
                    sp.dma_start(dst.unsqueeze(1), src).then_inc(landed[s], 16)

            with sp.Fori(0, E) as i:
                load_expert(i, i)
            sp.wait_ge(list_ready, 1)
            n_extra = sp.value_load(items[0:1, 0:1], min_val=0, max_val=MAX_EXTRA)
            with sp.If(n_extra > 0):
                with sp.Fori(0, n_extra) as j:
                    e = sp.value_load(items[0:1, bass.ds(j + 1, 1)], min_val=0, max_val=E - 1)
                    load_expert(j + E, e)
            for t in range(TT):
                sp.wait_ge(out_ready, t + 1)
                sp.dma_start(out_d[:, t, :], Y[:, t, :]).then_inc(stored, 16)
            sp.wait_ge(stored, 16 * TT)

        @block.gpsimd
        def _(pool):
            ch = Steps(pool, pool_chain)
            nc.gpsimd.memset(bias_rows[:], 0.0)
            nc.gpsimd.memset(gain_rows[:], 1.0).then_inc(constants, 1)
            nc.gpsimd.memset(ones[:], 1.0)
            nc.gpsimd.memset(before[:], 1.0)
            nc.gpsimd.memset(mask[:], 0.0)
            nc.gpsimd.memset(rows4[:], 0.0)
            nc.gpsimd.memset(row0[:], 0.0)
            for n in range(HR):
                nc.gpsimd.memset(inv_freq[:, n:n + 1], float(np.float32(THETA) ** np.float32(-2.0 * n / ROPE)))
            ch.link(nc.gpsimd.memset(ident[:], 0.0))
            for r in range(4):
                ch.link(nc.gpsimd.memset(rows4[32 * r:32 * r + 1, :], 1.0))
            ch.link(nc.gpsimd.memset(row0[0:1, :], 1.0))
            nc.gpsimd.affine_select(out=ident[:], in_=ident[:], compare_op=ALU.not_equal, fill=1.0,
                                    base=0, pattern=[[-1, P]], channel_multiplier=1)
            nc.gpsimd.affine_select(out=before[:], in_=before[:], compare_op=ALU.is_ge, fill=0.0,
                                    base=-1, pattern=[[1, P]], channel_multiplier=-1)
            nc.gpsimd.affine_select(out=mask[:, 0, :], in_=mask[:, 0, :], compare_op=ALU.is_ge, fill=NEG,
                                    base=0, pattern=[[-1, P]], channel_multiplier=1)
            nc.gpsimd.affine_select(out=mask[:, 1, :], in_=mask[:, 1, :], compare_op=ALU.is_ge, fill=NEG,
                                    base=0, pattern=[[1, P]], channel_multiplier=-1).then_inc(constants, 1)

            def load_chunk(m, w_d, col):
                for half in range(2):
                    s = 4 + half
                    if m and half == 0:
                        pool.wait_ge(slot_free[4], m)
                    elif m:
                        pool.wait_ge(w_done, TT * m)
                    pool.dma_start(chunk_slot(s), w_d[:, 8 * half:8 * half + 8, col:col + CH]).then_inc(chunk_in[half], 16)

            pool.wait_ge(slot_free[3], 3)
            for m in range(WIN):
                load_chunk(m, win_d, CH * m)
            for m in range(WOUT):
                load_chunk(WIN + m, wout_d, CH * m)
                if m == 0:
                    pool.wait_ge(t_done, T_AT["yT", 7] + 1)
                    pool.dma_start(hv, x_d).then_inc(x2_in, 16)
            for b in range(BLOCKS):
                v = slot_id[:, b, :].rearrange("p (r s) -> p r s", r=2)
                ch.link(nc.gpsimd.iota(v, pattern=[[0, 2], [1, BLK]], base=CAP * b, channel_multiplier=0,
                                       allow_small_or_imprecise_dtypes=True))
                if CAP < BLK:
                    ch.link(nc.gpsimd.memset(v[:, :, CAP:BLK], -1.0))
            ch.link(nc.gpsimd.iota(route[:, 0:4], pattern=[[1, 4]], base=0, channel_multiplier=0,
                                   allow_small_or_imprecise_dtypes=True))
            nc.gpsimd.iota(items_f[0:1, 0:48], pattern=[[0, 3], [1, 16]], base=0, channel_multiplier=0,
                           allow_small_or_imprecise_dtypes=True)
            nc.gpsimd.iota(items_f[0:1, 48:96], pattern=[[1, 3], [0, 16]], base=1, channel_multiplier=0,
                           allow_small_or_imprecise_dtypes=True)
            nc.gpsimd.iota(items_f[0:1, 96:103], pattern=[[1, 7]], base=1, channel_multiplier=0,
                           allow_small_or_imprecise_dtypes=True).then_inc(constants, 1)
            pool.wait_ge(logits_done, 1)
            nc.gpsimd.memset(T[:], 0.0).then_inc(y_clear, 1)

        @block.scalar
        def _(act):
            ch = Steps(act, act_chain)
            act.dma_start(vec_rows[0:16, :], c.rearrange("a (k p) -> (a k) p", p=P)).then_inc(c_in, 16)
            act.dma_start(vec_rows[16:32, :], g_group.rearrange("a (k p) -> (a k) p", p=P)).then_inc(vec_in, 16)
            act.dma_start(vec_rows[32:40, :], b_spatial[0]).then_inc(vec_in, 16)
            act.dma_start(xv, x_d).then_inc(x_in, 16)
            act.dma_start(pos_i[:], positions.rearrange("a (t p) -> p (a t)", p=P), allow_slow_non_contiguous=True).then_inc(small_in, 16)
            act.dma_start(sink_b[:], sink[0:1, :].broadcast_to([P, HEADS])).then_inc(small_in, 16)
            act.dma_start(router_b[:, 0:GROUPS], b_rg[0:1, :].broadcast_to([P, GROUPS])).then_inc(small_in, 16)
            act.dma_start(router_b[:, GROUPS:], b_re.rearrange("a g e -> a (g e)").broadcast_to([P, E])).then_inc(small_in, 16)
            act.dma_start(w_sp, w_spatial[0].rearrange("h p q -> p h q")).then_inc(small_in, 16)
            act.dma_start(w_router[:, :, 0:GROUPS], w_rg[0].rearrange("(p k) g -> p k g", k=KC)).then_inc(small_in, 16)
            act.dma_start(w_router[:, :, GROUPS:], w_re[0].rearrange("(p k) g e -> p k (g e)", k=KC)).then_inc(small_in, 16)
            act.wait_ge(c_in, 16)
            nc.scalar.activation(vec_rows[0:16, :], vec_rows[0:16, :], ACT.Silu).then_inc(c_silu, 1)
            act.wait_ge(x_in, 16)
            for t in range(TT):
                nc.scalar.activation(av[:, t, :], xv[:, t, :], ACT.Square, accum_out=stats[:, t:t + 1]).then_inc(x_square, 1)

            def wide(n):
                if n in PE_HALVES:
                    act.wait_ge(wide_done, pe_halves(n) + 1)
                else:
                    act.wait_ge(slot_free[3], n + 1)
                to = mod_to[n // 2][:, HALF * (n % 2):HALF * (n % 2 + 1)]
                nc.scalar.copy(to, ada_wide).then_inc(wide_out, 1)

            def t_group(name, n):
                g = T_AT[name, n]
                return g % 2 == 1, g

            def t_copy(name, n, to):
                odd, g = t_group(name, n)
                if odd:
                    act.wait_ge(t_done, g + 1)
                    src = ps[:, T0B + 1, :]
                    nc.scalar.copy(to, src).then_inc(t_out[1], 1)

            def z_chunk(m):
                for t in range(TT):
                    act.wait_ge(w_done, 2 * m + t + 1)
                    nc.scalar.activation(zv[:, t, CH * m:CH * m + CH], ps[:, W0B + t, :],
                                         ACT.Copy if m < 3 else ACT.Gelu).then_inc(z_out, 1)

            wide(0)
            wide(1)
            wide(2)
            for n in range(4):
                t_copy("aT", n, T[:, 2 * n:2 * n + 2, :])
            wide(3)
            act.wait_ge(trig_in, 1)
            nc.scalar.activation(angle[:], angle[:], ACT.Sin).then_inc(trig, 1)
            for n in range(4, 8):
                t_copy("aT", n, T[:, 2 * n:2 * n + 2, :])
            act.wait_ge(scaled, 2)
            act.dma_start(gain_v, gmlp_g.rearrange("a h d -> a (h d)").broadcast_to([P, HEADS * HD])).then_inc(gain_in, 16)
            for n in range(2):
                t_copy("wsT", n, wsT[:, 4 * n:4 * n + 4, :])
            z_chunk(0)
            z_chunk(1)
            wide(4)
            z_chunk(2)
            wide(5)
            z_chunk(3)
            wide(6)
            for n in range(2):
                t_copy("q0", n, qT[:, 4 * n:4 * n + 4, :])
            t_copy("k", 0, kT)

            def scores(t):
                for n in range(4):
                    t_copy(f"s{t}", n, S[:, 2 * n:2 * n + 2, :])

            def softmax(t):
                act.wait_ge(bias_max, t + 1)
                for h in range(HEADS):
                    ins = nc.scalar.activation(S[:, h, :], S[:, h, :], ACT.Exp, bias=stats[:, 16 + h:17 + h],
                                               scale=SCALE, accum_out=stats[:, 24 + h:25 + h])
                nc.scalar.activation(stats[:, 32:40], stats[:, 40:48], ACT.Exp).then_inc(probs, 1)

            def probs_out(t):
                for n in range(4):
                    odd, g = t_group(f"p{t}", n)
                    if odd and (n >= 2 or t):
                        act.wait_ge(pv_done, 4 * t + n - 1)
                    t_copy(f"p{t}", n, pT[n % 2])

            scores(0)
            softmax(0)
            z_chunk(4)
            wide(7)
            probs_out(0)
            for n in range(2):
                t_copy("q1", n, qT[:, 4 * n:4 * n + 4, :])
            scores(1)
            softmax(1)
            z_chunk(5)
            wide(8)
            probs_out(1)
            act.wait_ge(o_out, 2)
            for t in range(TT):
                nc.scalar.activation(A[:, 1536 + 1024 * t:2560 + 1024 * t], zv[:, t, 0:1024], ACT.Square,
                                     accum_out=stats[:, 48 + t:49 + t]).then_inc(y_square, 1)
            z_chunk(6)
            for t in range(TT):
                act.wait_ge(gated, 3 + t)
                act.wait_ge(y_square, t + 1)
                nc.scalar.activation(A[:, 1536 + 1024 * t:2560 + 1024 * t], zv[:, t, O_U:O_U + 1024], ACT.Square,
                                     accum_out=stats[:, 50 + t:51 + t]).then_inc(y_square, 1)
            for n in range(8):
                odd, g = t_group("yT", n)
                if odd:
                    act.wait_ge(t_done, g + 1)
                    for k in range(2):
                        ins = nc.scalar.activation(T[:, 2 * n + k, :], ps[:, T0B + 1, SEQ * k:SEQ * k + SEQ], ACT.Copy,
                                                   scale=vec_cols[:, 16 + 2 * n + k:17 + 2 * n + k])
                    ins.then_inc(t_out[1], 1)
            for m in range(WOUT):
                if m < 3:
                    wide(9 + m)
                for t in range(TT):
                    act.wait_ge(w_done, 2 * (WIN + m) + t + 1)
                    if m or t:
                        act.wait_ge(mix_square, 2 * m + t)
                    nc.scalar.activation(mix_scratch, ps[:, W0B + t, :], ACT.Square,
                                         accum_out=stats[:, 56 + 4 * t + m:57 + 4 * t + m]).then_inc(mix_square, 1)
                    nc.scalar.copy(av[:, t, CH * m:CH * m + CH], ps[:, W0B + t, :]).then_inc(z_out, 1)

            def square_h(t):
                act.wait_ge(h_ready, t + 1)
                nc.scalar.activation(T[:, :, P * t:P * t + P], hv[:, t, :].rearrange("p (k s) -> p k s", k=KC), ACT.Square,
                                     accum_out=stats[:, 64 + t:65 + t]).then_inc(h_square, 1)

            def fT_copy(n):
                t = n // 4
                act.wait_ge(fT_done, n + 1)
                act.wait_ge(h_square, t + 1)
                nc.scalar.copy(T[:, 4 * (n % 4):4 * (n % 4) + 4, P * t:P * t + P],
                               ps[:, n % 4, :].rearrange("p (k s) -> p k s", k=4)).then_inc(fT_out[1], 1)

            square_h(0)
            fT_copy(0)
            fT_copy(1)
            square_h(1)
            fT_copy(2)
            fT_copy(3)
            fT_copy(5)
            fT_copy(7)
            act.wait_ge(gap_ready, 1)
            nc.scalar.activation(route[:, 200:210], route[:, 180:190], ACT.Exp).then_inc(gap_exp, 1)

            def gather_out(g, width):
                for u in range(8):
                    act.wait_ge(gathered, g * 8 + (u + 2))
                    nc.scalar.copy(xT[:, 2 * u:2 * u + 2, 0:width],
                                   ps[:, GATHER_BANK[u], 0:2 * width].rearrange("p (c s) -> p c s", c=2)).then_inc(xT_ready, 1)

            def expert(i):
                wait_products(act, GATE_UP, i)
                act.wait_ge(hid_ready, i + 1)
                nc.scalar.activation(silu_s, ps[:, 0, :], ACT.Silu).then_inc(silu_ready, 1)
                act.wait_ge(wpickT_done, i + 2)
                nc.scalar.copy(wpickT, ps[:, 7, 0:256]).then_inc(wpickT_ready, 1)
                wait_products(act, DOWN, i)
                nc.scalar.copy(down_s[:], flat[:, 2560:3584]).then_inc(down_ready, 1)

            for s in (wpickT_ready, down_ready):
                act.sem_inc(s, 1)
            with act.Fori(0, GROUPS) as g:
                gather_out(g, EPG * BLK)
                for m in range(EPG):
                    expert(g * EPG + m)
            act.wait_ge(list_ready, 1)
            n_extra = act.value_load(items[0:1, 0:1], min_val=0, max_val=MAX_EXTRA)
            with act.If(n_extra > 0):
                with act.Fori(0, n_extra) as j:
                    gather_out(j + GROUPS, BLK)
                    expert(j + E)
            for t in range(TT):
                act.wait_ge(summed, n_extra * 8 + (8 * E + 4 * t + 5))
                nc.scalar.activation(av[:, t, :], Y[:, t, :], ACT.Square,
                                     accum_out=stats[:, 68 + t:69 + t]).then_inc(out_square, 1)

        @block.vector
        def _(dve):
            ch = Steps(dve, vec_chain)
            V = nc.vector

            def rsqrt_mean(to, square_sum, n):
                w = to.shape[-1]
                v, y, t = (newton[:, 4 * k:4 * k + w] for k in range(3))
                ch.link(V.tensor_scalar(v, square_sum, 1.0 / n, EPS, ALU.mult, ALU.add))
                ch.link(V.tensor_scalar(y.bitcast(I32), v.bitcast(I32), 1, None, ALU.logical_shift_right))
                ch.link(V.tensor_scalar(y.bitcast(I32), y.bitcast(I32), -1.0, float(0x5f3759df), ALU.mult, ALU.add))
                for step in range(3):
                    ch.link(V.tensor_tensor(t, y, y, ALU.mult))
                    ch.link(V.scalar_tensor_tensor(t, t, -0.5, v, ALU.mult, ALU.mult))
                    last = V.scalar_tensor_tensor(y if step < 2 else to, t, 1.5, y, ALU.add, ALU.mult)
                    if step < 2:
                        ch.link(last)
                return last

            dve.wait_ge(vec_ps, 1)
            ch.link(V.tensor_copy(vec_cols[:], ps[:, 7, 0:40]))
            V.tensor_copy(c_wide[:], vec_cols[:, 0:16].unsqueeze(2).broadcast_to([P, KC, 32])).then_inc(c_ready, 1)

            dve.wait_ge(small_in, 7 * 16)
            dve.wait_ge(constants, 2)
            ch.link(V.tensor_copy(stats[:, 4:6], pos_i[:]))
            for t in range(TT):
                ins = V.tensor_scalar(angle[:, 0, t, :], inv_freq[:], stats[:, 4 + t:5 + t], None, ALU.mult)
            ch.link(ins)
            ch.link(V.tensor_copy(angle[:, 1], angle[:, 0]))
            ch.link(V.tensor_scalar(turns[:, 0], angle[:, 0], float(0.5 / np.pi), None, ALU.mult))
            ch.link(V.tensor_scalar(turns[:, 1], angle[:, 1], float(0.5 / np.pi), 0.25, ALU.mult, ALU.add))
            ch.link(V.tensor_scalar(turns, turns, MAGIC, None, ALU.add))
            ch.link(V.tensor_scalar(turns, turns, -MAGIC, None, ALU.add))
            af, tf = (b.rearrange("p a t n -> p (a t n)") for b in (angle[:], turns))
            for part in TWO_PI:
                ch.link(V.scalar_tensor_tensor(af, tf, -part, af, ALU.mult, ALU.add))
            ch.link(V.tensor_scalar(angle[:, 1], angle[:, 1], float(np.pi / 2), None, ALU.add))
            V.tensor_scalar(af, af, PI_SAFE, -PI_SAFE, ALU.min, ALU.max).then_inc(trig_in, 1)

            dve.wait_ge(x_square, TT)
            ch.link(rsqrt_mean(stats[:, 2:4], stats[:, 0:2], D))

            def rows(n):
                kind = n // 2
                dve.wait_ge(slot_free[3], n + 1)
                dve.wait_ge(bias_in, 16 * (n + 1))
                if n:
                    dve.wait_ge(wide_done, pe_halves(n))
                gained = kind in gain_of
                if kind in (SC1, SC2):
                    ins = V.scalar_tensor_tensor(mod_rows[:], ada_acc, row0[:, 0:1], bias_rows[:], ALU.add, ALU.add)
                else:
                    ins = V.tensor_tensor(mod_rows[:], ada_acc, bias_rows[:], ALU.add)
                if gained:
                    ch.link(ins)
                    dve.wait_ge(gainrow_in, 16 * n_gained[n])
                    ins = V.tensor_tensor(mod_rows[:], mod_rows[:], gain_rows[:], ALU.mult)
                ins.then_inc(rows_ready, 1)

            def t_copy(name, n, to):
                g = T_AT[name, n]
                if g % 2 == 0:
                    dve.wait_ge(t_done, g + 1)
                    src = ps[:, T0B, :]
                    V.tensor_copy(to, src).then_inc(t_out[0], 1)

            def scale_half(h):
                dve.wait_ge(wide_out, h + 1)
                cols = slice(HALF * h, HALF * h + HALF)
                for t in range(TT):
                    ins = V.scalar_tensor_tensor(av[:, t, cols], xv[:, t, cols], stats[:, 2 + t:3 + t], G1[:, cols], ALU.mult, ALU.mult)
                ins.then_inc(scaled, 1)

            def shift_half(h):
                dve.wait_ge(wide_out, 3 + h)
                dve.wait_ge(scaled, h + 1)
                cols = slice(HALF * h, HALF * h + HALF)
                for t in range(TT):
                    ins = V.tensor_tensor(av[:, t, cols], av[:, t, cols], sh1[:, cols], ALU.add)
                ins.then_inc(a_ready, 1)

            rows(0)
            rows(1)
            scale_half(0)
            rows(2)
            scale_half(1)
            rows(3)
            shift_half(0)
            for n in range(4):
                t_copy("aT", n, T[:, 2 * n:2 * n + 2, :])
            shift_half(1)
            for n in range(4, 8):
                t_copy("aT", n, T[:, 2 * n:2 * n + 2, :])
            for n in range(2):
                t_copy("wsT", n, wsT[:, 4 * n:4 * n + 4, :])

            def products(n, slots):
                for s in slots:
                    dve.wait_ge(landed[s], 16 * (n + 1))
                    for j in range(4):
                        k = 4 * s + j
                        own, w = ada_slot(s)[:, 0, :], ada_slot(s)[:, j, :]
                        if k == 0:
                            ch.link(V.tensor_scalar(own, w, vec_cols[:, 0:1], None, ALU.mult))
                        elif j == 0:
                            ins = V.scalar_tensor_tensor(own, w, vec_cols[:, k:k + 1], ada_slot(s - 1)[:, 0, :], ALU.mult, ALU.add)
                            ins.then_inc(slot_free[s - 1], 1)
                            dve.wait_ge(slot_free[s - 1], n + 1)
                        else:
                            ins = V.scalar_tensor_tensor(own, w, vec_cols[:, k:k + 1], own, ALU.mult, ALU.add)
                            ch.link(ins)
                if k == KC - 1:
                    dve.wait_ge(bias_in, 16 * (n + 1))
                    if n // 2 == SC2:
                        ins = V.scalar_tensor_tensor(own, own, row0[:, 0:1], bias_rows[:], ALU.add, ALU.add)
                    else:
                        ins = V.tensor_tensor(own, own, bias_rows[:], ALU.add)
                    if n // 2 in gain_of:
                        ch.link(ins)
                        dve.wait_ge(gainrow_in, 16 * n_gained[n])
                        ins = V.tensor_tensor(own, own, gain_rows[:], ALU.mult)
                    ins.then_inc(rows_ready, 1)

            products(4, range(4))
            products(5, range(4))
            products(6, range(2))

            dve.wait_ge(z_out, 6)
            dve.wait_ge(trig, 1)
            NQ = HEADS + KV
            rope_tmp = A[:, 0:4 * NQ * HR].rearrange("p (n h r) -> p n h r", n=4, r=HR)
            for t in range(TT):
                qk = zv[:, t, 0:NQ * HD].rearrange("p (h d) -> p h d", d=HD)
                x1, x2 = qk[:, :, 0:HR], qk[:, :, HR:ROPE]
                sin, cos = (angle[:, k, t, :].unsqueeze(1).broadcast_to([P, NQ, HR]) for k in range(2))
                V.tensor_tensor(rope_tmp[:, 0], x1, cos, ALU.mult)
                V.tensor_tensor(rope_tmp[:, 1], x2, sin, ALU.mult)
                V.tensor_tensor(rope_tmp[:, 2], x2, cos, ALU.mult)
                ch.link(V.tensor_tensor(rope_tmp[:, 3], x1, sin, ALU.mult))
                V.tensor_tensor(x1, rope_tmp[:, 0], rope_tmp[:, 1], ALU.subtract)
                V.tensor_tensor(x2, rope_tmp[:, 2], rope_tmp[:, 3], ALU.add).then_inc(roped, 1)
                dve.wait_ge(roped, t + 1)
            products(6, range(2, 4))
            for n in range(2):
                t_copy("q0", n, qT[:, 4 * n:4 * n + 4, :])
            t_copy("k", 0, kT)

            def scores(t):
                for n in range(4):
                    t_copy(f"s{t}", n, S[:, 2 * n:2 * n + 2, :])
                dve.wait_ge(t_out[0], (T_AT[f"s{t}", 3] + 2) // 2)
                dve.wait_ge(t_out[1], (T_AT[f"s{t}", 3] + 1) // 2)
                if t:
                    dve.wait_ge(probs, t)
                ch.link(V.tensor_reduce(stats[:, 8:16], S, AX.X, ALU.max))
                ch.link(V.scalar_tensor_tensor(stats[:, 8:16], stats[:, 8:16], SCALE, sink_b[:], ALU.mult, ALU.max))
                V.tensor_tensor(stats[:, 40:48], sink_b[:], stats[:, 8:16], ALU.subtract)
                V.tensor_scalar(stats[:, 16:24], stats[:, 8:16], -1.0, None, ALU.mult).then_inc(bias_max, 1)

            def probs_out(t):
                dve.wait_ge(probs, t + 1)
                ch.link(V.tensor_tensor(stats[:, 72:80], stats[:, 24:32], stats[:, 32:40], ALU.add))
                ch.link(V.reciprocal(stats[:, 80:88], stats[:, 72:80]))
                for n in range(4):
                    if T_AT[f"p{t}", n] % 2 == 0 and (n >= 2 or t):
                        dve.wait_ge(pv_done, 4 * t + n - 1)
                    t_copy(f"p{t}", n, pT[n % 2])
                dve.wait_ge(pv_done, 4 * t + 4)
                o = zv[:, t, 0:1024].rearrange("p (h d) -> p h d", d=HD)
                V.tensor_tensor(o, flat[:, CH * W0B:CH * W0B + 1024].rearrange("p (h d) -> p h d", d=HD),
                                stats[:, 80:88].unsqueeze(2).broadcast_to([P, HEADS, HD]), ALU.mult).then_inc(o_out, 1)

            scores(0)
            products(7, range(4))
            probs_out(0)
            for n in range(2):
                t_copy("q1", n, qT[:, 4 * n:4 * n + 4, :])
            scores(1)
            products(8, range(4))
            probs_out(1)

            dve.wait_ge(y_square, 2)
            ch.link(rsqrt_mean(stats[:, 52:54], stats[:, 48:50], 1024))
            for t in range(TT):
                V.tensor_scalar(zv[:, t, 0:1024], zv[:, t, 0:1024], stats[:, 52 + t:53 + t], None, ALU.mult)

            dve.wait_ge(gain_in, 16)
            for m in (5, 6):
                for t in range(TT):
                    dve.wait_ge(z_out, 2 * m + t + 1)
                    v = zv[:, t, CH * m:CH * m + CH]
                    for h in range(4):
                        ins = V.bn_stats(bn[:, 6 * h:6 * h + 6], v[:, HD * h:HD * h + HD])
                    ch.link(ins)
                    for h in range(4):
                        ins = V.bn_aggr(bn[:, 24 + 2 * h:26 + 2 * h], bn[:, 6 * h:6 * h + 6])
                    ch.link(ins)
                    moments = bn[:, 24:32].rearrange("p (h two) -> p h two", two=2)
                    ch.link(V.tensor_copy(stats[:, 88:92], moments[:, :, 1]))
                    ch.link(rsqrt_mean(stats[:, 92:96], stats[:, 88:92], 1))
                    for h in range(4):
                        ins = V.tensor_scalar(v[:, HD * h:HD * h + HD], v[:, HD * h:HD * h + HD], moments[:, h, 0:1],
                                              stats[:, 92 + h:93 + h], ALU.subtract, ALU.mult)
                    ch.link(ins)
                    V.tensor_tensor(v, v, gain_v[:, CH * (m - 5):CH * (m - 5) + CH], ALU.mult).then_inc(vn_ready, 1)
            for n in range(4):
                hh, t = n // 2, n % 2
                dve.wait_ge(mixed_done, n + 1)
                for k in range(4):
                    h = 4 * hh + k
                    u = zv[:, t, O_U + HD * h:O_U + HD * h + HD]
                    ins = V.scalar_tensor_tensor(u, ps[:, W0B + n % 2, HD * k:HD * k + HD],
                                                 vec_cols[:, 32 + h:33 + h], u, ALU.add, ALU.mult)
                ins.then_inc(gated, 1)
            dve.wait_ge(y_square, 4)
            ch.link(rsqrt_mean(stats[:, 54:56], stats[:, 50:52], 1024))
            for t in range(TT):
                u = zv[:, t, O_U:O_U + 1024]
                ins = V.tensor_scalar(u, u, stats[:, 54 + t:55 + t], None, ALU.mult)
            ins.then_inc(y_ready, 1)
            for n in range(8):
                if T_AT["yT", n] % 2 == 0:
                    dve.wait_ge(t_done, T_AT["yT", n] + 1)
                    for k in range(2):
                        ins = V.tensor_scalar(T[:, 2 * n + k, :], ps[:, T0B, SEQ * k:SEQ * k + SEQ],
                                              vec_cols[:, 16 + 2 * n + k:17 + 2 * n + k], None, ALU.mult)
                    ins.then_inc(t_out[0], 1)
            rows(9)
            products(10, range(4))

            def mix_gain(m, t):
                dve.wait_ge(wide_out, 6)
                dve.wait_ge(z_out, 2 * (WIN + m) + t + 1)
                part = av[:, t, CH * m:CH * m + CH]
                ch.link(V.tensor_tensor(part, part, Gt[:, 0, CH * m:CH * m + CH], ALU.mult))

            for t in range(TT):
                mix_gain(0, t)
            products(11, range(4))
            for t in range(TT):
                mix_gain(1, t)
            for t in range(TT):
                mix_gain(2, t)

            dve.wait_ge(x2_in, 16)
            dve.wait_ge(wide_out, HALVES)
            for t in range(TT):
                mix_gain(3, t)
                dve.wait_ge(mix_square, 2 * WOUT - 1 + t)
                ch.link(V.tensor_reduce(stats[:, 4 + t:5 + t], stats[:, 56 + 4 * t:60 + 4 * t], AX.X, ALU.add))
                ch.link(rsqrt_mean(stats[:, 6 + t:7 + t], stats[:, 4 + t:5 + t], D))
                V.scalar_tensor_tensor(hv[:, t, :], av[:, t, :], stats[:, 6 + t:7 + t], hv[:, t, :], ALU.mult, ALU.add).then_inc(h_ready, 1)
                dve.wait_ge(h_ready, t + 1)
                ch.link(V.tensor_tensor(av[:, t, :], hv[:, t, :], G2, ALU.mult))
                dve.wait_ge(h_square, t + 1)
                ch.link(rsqrt_mean(stats[:, 66 + t:67 + t], stats[:, 64 + t:65 + t], D))
                V.scalar_tensor_tensor(av[:, t, :], av[:, t, :], stats[:, 66 + t:67 + t], sh2, ALU.mult, ALU.add).then_inc(f_ready, 1)
            for n in (4, 6):
                dve.wait_ge(fT_done, n + 1)
                V.tensor_copy(T[:, 4 * (n % 4):4 * (n % 4) + 4, P:2 * P],
                              ps[:, n % 4, :].rearrange("p (k s) -> p k s", k=4)).then_inc(fT_out[0], 1)

            def r3(at, n):
                return route[:, at:at + TT * n].rearrange("p (t n) -> p t n", t=TT)

            def r1(at):
                return route[:, at:at + TT]

            iota4 = route[:, 0:4].unsqueeze(1).broadcast_to([P, TT, 4])

            def over4(s):
                return s.unsqueeze(2).broadcast_to([P, TT, 4])

            def first_of(to, logits, top, work, at):
                ch.link(V.tensor_tensor(work, logits, over4(top), ALU.is_lt))
                ch.link(V.scalar_tensor_tensor(work, work, 100.0, iota4, ALU.mult, ALU.add))
                ch.link(V.tensor_reduce(at, work, AX.X, ALU.min))
                return V.tensor_tensor(to, iota4, over4(at), ALU.is_equal)

            L = r3(8, 20)
            work, at = r3(48, 4), r1(56)
            gmax, pick_g = r1(58), r3(60, 4)
            esel, m1, oh1, m2, oh2 = r3(68, 4), r1(76), r3(78, 4), r1(86), r3(88, 4)
            weighted = route[:, 96:128].rearrange("p (t g e) -> p t g e", t=TT, g=GROUPS)
            esel2 = r3(130, 4)
            gaps = r3(180, 5)
            gexp = r3(200, 5)
            dve.wait_ge(logits_done, 1)
            dve.wait_ge(constants, 3)
            bias = router_b[:].unsqueeze(1).broadcast_to([P, TT, 20])
            ch.link(V.tensor_tensor(L, ps[:, W0B, 0:40].rearrange("p (t n) -> p t n", t=TT), bias, ALU.add))
            ch.link(V.tensor_reduce(gmax, L[:, :, 0:4], AX.X, ALU.max))
            V.tensor_tensor(gaps[:, :, 0:4], L[:, :, 0:4], over4(gmax), ALU.subtract)
            ch.link(first_of(pick_g, L[:, :, 0:4], gmax, work, at))
            for t in range(TT):
                ins = V.tensor_tensor(weighted[:, t], L[:, t, 4:20].rearrange("p (g e) -> p g e", g=GROUPS),
                                      pick_g[:, t].unsqueeze(2).broadcast_to([P, GROUPS, EPG]), ALU.mult)
            ch.link(ins)
            ch.link(V.tensor_reduce(esel, weighted.rearrange("p t g e -> p t e g"), AX.X, ALU.add))
            ch.link(V.tensor_reduce(m1, esel, AX.X, ALU.max))
            ch.link(first_of(oh1, esel, m1, work, at))
            ch.link(V.scalar_tensor_tensor(esel2, oh1, -1e38, esel, ALU.mult, ALU.add))
            ch.link(V.tensor_reduce(m2, esel2, AX.X, ALU.max))
            V.tensor_tensor(gaps[:, :, 4], m2, m1, ALU.subtract).then_inc(gap_ready, 1)
            ch.link(first_of(oh2, esel2, m2, work, at))
            both = r3(140, 4)
            ch.link(V.tensor_tensor(both, oh1, oh2, ALU.add))
            member = route[:, 220:252].rearrange("p (t g e) -> p t g e", t=TT, g=GROUPS)
            comb = route[:, 252:284].rearrange("p (t g e) -> p t g e", t=TT, g=GROUPS)
            for t in range(TT):
                ins = V.tensor_tensor(member[:, t], pick_g[:, t].unsqueeze(2).broadcast_to([P, GROUPS, EPG]),
                                      both[:, t].unsqueeze(1).broadcast_to([P, GROUPS, EPG]), ALU.mult)
            ins.then_inc(chosen, 1)
            rank = route[:, 284:316]
            dve.wait_ge(ranks_done, 1)
            memf = route[:, 220:252]
            ch.link(V.scalar_tensor_tensor(rank, memf, -FAR, ps[:, W0B + 1, 0:32], ALU.mult, ALU.add))
            ch.link(V.tensor_scalar(rank, rank, FAR, None, ALU.add))

            combf = route[:, 252:284]

            def list_blocks():
                dve.wait_ge(ranks_done, 2)
                f = items_f[0:1, :]
                e_id, b_id, j_id = f[:, 0:48], f[:, 48:96], f[:, 96:103]
                flag, run = f[:, 103:151], f[:, 151:199]
                for b in range(1, BLOCKS):
                    ins = V.tensor_scalar(flag[:, 16 * (b - 1):16 * b], ps[0:1, T0B, 0:16], float(CAP * b), None, ALU.is_gt)
                ch.link(ins)
                ch.link(V.tensor_copy(run, flag))
                step = 1
                tmp48 = f[:, 200:248]
                while step < 48:
                    ch.link(V.tensor_copy(tmp48, run))
                    ch.link(V.tensor_tensor(run[:, step:48], tmp48[:, step:48], tmp48[:, 0:48 - step], ALU.add))
                    step *= 2
                sel = f[:, 248:248 + 7 * 48].rearrange("p (j n) -> p j n", j=7)

                def over_j(s):
                    return s.unsqueeze(1).broadcast_to([1, 7, 48])

                prod = f[:, 600:600 + 7 * 48].rearrange("p (j n) -> p j n", j=7)
                got = f[:, 940:957]
                ch.link(V.tensor_tensor(sel, over_j(run), j_id.unsqueeze(2).broadcast_to([1, 7, 48]), ALU.is_equal))
                ch.link(V.tensor_tensor(sel, sel, over_j(flag), ALU.mult))
                ch.link(V.tensor_tensor(prod, sel, over_j(e_id), ALU.mult))
                ch.link(V.tensor_reduce(got[:, 1:8], prod, AX.X, ALU.add))
                ch.link(V.tensor_tensor(prod, sel, over_j(b_id), ALU.mult))
                ch.link(V.tensor_reduce(got[:, 8:15], prod, AX.X, ALU.add))
                ch.link(V.tensor_copy(got[:, 0:1], run[:, 47:48]))
                V.tensor_copy(items[:, 0:15], got[:, 0:15]).then_inc(list_ready, 1)


            def weigh():
                dve.wait_ge(gap_exp, 1)
                den, w1, w2, wsum = r1(150), r1(152), r1(154), r1(156)
                ch.link(V.tensor_reduce(wsum, gexp[:, :, 0:4], AX.X, ALU.add))
                ch.link(V.tensor_scalar(den, gexp[:, :, 4], 1.0, None, ALU.add))
                ch.link(V.tensor_tensor(den, den, wsum, ALU.mult))
                ch.link(V.reciprocal(w1, den))
                ch.link(V.tensor_tensor(w2, w1, gexp[:, :, 4], ALU.mult))
                V.tensor_tensor(oh1, oh1, over4(w1), ALU.mult)
                ch.link(V.tensor_tensor(oh2, oh2, over4(w2), ALU.mult))
                ch.link(V.tensor_tensor(both, oh1, oh2, ALU.add))
                for t in range(TT):
                    ins = V.tensor_tensor(comb[:, t], pick_g[:, t].unsqueeze(2).broadcast_to([P, GROUPS, EPG]),
                                          both[:, t].unsqueeze(1).broadcast_to([P, GROUPS, EPG]), ALU.mult)
                ch.link(ins)

            def picks(g, experts, ids):
                dve.wait_ge(gathered, g * 8 + 1)
                for m, e in enumerate(experts):
                    for t in range(TT):
                        ins = V.tensor_scalar(pick[:, t, BLK * m:BLK * m + BLK], ids[:, 0:BLK],
                                              rank[:, bass.ds(e + 16 * t, 1)], None, ALU.is_equal)
                ins.then_inc(pick_ready, 1)

            def add(i, n):
                t, col = n // 4, CH * (n % 4)
                dve.wait_ge(spread, i * 8 + (n + 1))
                V.tensor_tensor(Y[:, t, col:col + CH], Y[:, t, col:col + CH], ps[:, 2 + n % 2, :], ALU.add).then_inc(summed, 1)

            def expert(i, e, ids, then=None):
                dve.wait_ge(wpickT_done, i + 1)
                for t in range(TT):
                    ins = V.tensor_scalar(wpick[:, t, :], ids, rank[:, bass.ds(e + 16 * t, 1)],
                                          combf[:, bass.ds(e + 16 * t, 1)], ALU.is_equal, ALU.mult)
                ins.then_inc(wpick_ready, 1)
                if then:
                    then()
                dve.wait_ge(silu_ready, i + 1)
                dve.wait_ge(hidT_done, i + 1)
                V.tensor_tensor(hid, silu_s, ps[:, 1, :], ALU.mult).then_inc(hid_ready, 1)
                for n in range(0 if then else 4):
                    add(i, n)
                dve.wait_ge(hidT_done, i + 2)
                dve.wait_ge(slot_free[5], i * 2 + 1)
                V.tensor_copy(bias_rows[:, 0:CH], ps[:, 4, :]).then_inc(hidT_ready, 1)
                for n in range(4, 4 if then else 8):
                    add(i, n)
                if not then:
                    dve.wait_ge(summed, i * 8 + 9)

            def group(g, then=None):
                picks(g, [g * EPG + m for m in range(EPG)], slot_id[:, 0, :])
                if then:
                    weigh()
                for m in range(EPG):
                    expert(g * EPG + m, g * EPG + m, slot_id[:, 0, :], then if m == 0 else None)

            dve.sem_inc(hid_ready, 1)
            dve.sem_inc(summed, 9)
            dve.wait_ge(y_clear, 1)
            group(0, list_blocks)
            with dve.Fori(1, GROUPS) as g:
                group(g)
            n_extra = dve.value_load(items[0:1, 0:1], min_val=0, max_val=MAX_EXTRA)
            with dve.If(n_extra > 0):
                with dve.Fori(0, n_extra) as j:
                    e = dve.value_load(items[0:1, bass.ds(j + 1, 1)], min_val=0, max_val=E - 1)
                    b = dve.value_load(items[0:1, bass.ds(j + 8, 1)], min_val=1, max_val=BLOCKS - 1)
                    ids = slot_id[:, bass.ds(b, 1), :].rearrange("p b s -> p (b s)")
                    picks(j + GROUPS, [e], ids)
                    expert(j + E, e, ids)
            for n in range(8):
                add(n_extra + E, n)

            for t in range(TT):
                dve.wait_ge(out_square, t + 1)
                ch.link(rsqrt_mean(stats[:, 4 + t:5 + t], stats[:, 68 + t:69 + t], D))
                ch.link(V.scalar_tensor_tensor(Y[:, t, :], Y[:, t, :], stats[:, 4 + t:5 + t], Gt[:, 1, :], ALU.mult, ALU.mult))
                V.tensor_tensor(Y[:, t, :], Y[:, t, :], hv[:, t, :], ALU.add).then_inc(out_ready, 1)

        @block.tensor
        def _(pe):
            M = nc.tensor

            def t_bank(name, n):
                g = T_AT[name, n]
                if g >= 2:
                    pe.wait_ge(t_out[g % 2], g // 2)
                return ps[:, T0B + g % 2, :]

            pe.wait_ge(constants, 2)
            pe.wait_ge(c_silu, 1)
            pe.wait_ge(vec_in, 2 * 16)
            M.transpose(ps[:, 7, 0:40], vec_rows, ident[0:40, 0:40]).then_inc(vec_ps, 1)

            def ada(n):
                for s in range(4):
                    pe.wait_ge(landed[s], 16 * (n + 1))
                    if s == 0:
                        if n:
                            pe.wait_ge(rows_ready, 1 + max(m for m in PE_HALVES if m < n))
                        else:
                            pe.wait_ge(c_ready, 1)
                    for cc in range(2):
                        for j in range(4):
                            ins = M.matmul(ada_acc[32 * j:32 * j + 32, CH * cc:CH * cc + CH], c_wide[:, 4 * s + j, :],
                                           ada_slot(s)[:, j, CH * cc:CH * cc + CH], start=(s == 0), stop=(s == 3))
                    ins.then_inc(slot_free[s], 1)

            def widen(n, lhs=rows4, rows=mod_rows[:], signal=wide_done):
                pe.wait_ge(rows_ready, n + 1)
                if n:
                    pe.wait_ge(wide_out, n)
                for cc in range(2):
                    ins = M.matmul(ada_wide[:, CH * cc:CH * cc + CH], lhs[:], rows[:, CH * cc:CH * cc + CH], start=True, stop=True)
                ins.then_inc(signal, 1)

            def add_up(n):
                widen(n, ones, ada_slot(3)[:, 0, :], slot_free[3])

            def transposes(name, n, blocks):
                bank = t_bank(name, n)
                for k, src in enumerate(blocks):
                    ins = M.transpose(bank[:, P * k:P * k + P], src, ident[:])
                ins.then_inc(t_done, 1)

            def project(m):
                for half in range(2):
                    pe.wait_ge(chunk_in[half], 16 * (m + 1))
                    for t in range(TT):
                        if half == 0 and m:
                            pe.wait_ge(z_out, 2 * m - 1 + t)
                        for k in range(8):
                            kk = 8 * half + k
                            ins = M.matmul(ps[:, W0B + t, :], T[:, kk, P * t:P * t + P], chunk_slot(4 + half)[:, k, :],
                                           start=(kk == 0), stop=(kk == KC - 1))
                        if half == 0 and t == TT - 1:
                            ins.then_inc(slot_free[4], 1)
                        elif half == 1:
                            ins.then_inc(w_done, 1)

            ada(0)
            ada(1)
            widen(0)
            ada(2)
            widen(1)
            ada(3)
            widen(2)
            for half in range(2):
                if half:
                    widen(3)
                pe.wait_ge(a_ready, half + 1)
                for n in range(4 * half, 4 * half + 4):
                    transposes("aT", n, [av[:, t, P * k:P * k + P] for k in (2 * n, 2 * n + 1) for t in range(TT)])
            pe.wait_ge(small_in, 7 * 16)
            for n in range(2):
                transposes("wsT", n, [w_sp[:, h, :] for h in range(4 * n, 4 * n + 4)])
            pe.wait_ge(t_out[0], (T_AT["aT", 7] + 2) // 2)
            pe.wait_ge(t_out[1], (T_AT["aT", 7] + 1) // 2)
            project(0)
            project(1)
            add_up(4)
            project(2)
            add_up(5)
            project(3)
            add_up(6)

            def q_tile(t):
                pe.wait_ge(roped, TT)
                for n in range(2):
                    transposes(f"q{t}", n, [zv[:, t, HD * h:HD * h + HD] for h in range(4 * n, 4 * n + 4)])

            def scores(t):
                last = T_AT["k", 0] if t == 0 else T_AT["q1", 1]
                pe.wait_ge(t_out[0], (last + 2) // 2)
                pe.wait_ge(t_out[1], (last + 1) // 2)
                for n in range(4):
                    bank = t_bank(f"s{t}", n)
                    for k in range(2):
                        h = 2 * n + k
                        own = slice(SEQ * k, SEQ * k + SEQ)
                        edge = slice(SEQ * k + P * (1 - t), SEQ * k + P * (1 - t) + P)
                        M.matmul(bank[:, own], qT[:, h, :], kT[:, h // (HEADS // KV), :], start=True, stop=True)
                        ins = M.matmul(bank[:, edge], ident[:], mask[:, t, :], start=False, stop=True, skip_group_check=True)
                    ins.then_inc(t_done, 1)

            def attend(t):
                pe.wait_ge(probs, t + 1)

                def pv(n):
                    g = T_AT[f"p{t}", n]
                    pe.wait_ge(t_out[g % 2], g // 2 + 1)
                    if n == 0:
                        pe.wait_ge(z_out, 2 * (5 + t))
                    for k in range(2):
                        h = 2 * n + k
                        v0 = O_V + HD * (h // (HEADS // KV))
                        for kc in range(2):
                            ins = M.matmul(ps[:, W0B + h // 4, HD * (h % 4):HD * (h % 4) + HD], pT[n % 2][:, k, kc, :],
                                           zv[:, kc, v0:v0 + HD], start=(kc == 0), stop=(kc == 1))
                    ins.then_inc(pv_done, 1)

                for n in range(4):
                    transposes(f"p{t}", n, [S[:, h, P * kc:P * kc + P] for h in (2 * n, 2 * n + 1) for kc in range(2)])
                    if n:
                        pv(n - 1)
                pv(3)

            q_tile(0)
            transposes("k", 0, [zv[:, t, O_K + HD * k:O_K + HD * k + HD] for k in range(KV) for t in range(TT)])
            scores(0)
            project(4)
            add_up(7)
            attend(0)
            q_tile(1)
            scores(1)
            pe.wait_ge(o_out, 1)
            project(5)
            add_up(8)
            attend(1)
            pe.wait_ge(o_out, 2)
            project(6)
            ada(9)
            pe.wait_ge(z_out, 2 * WIN)
            for n in range(4):
                hh, t = n // 2, n % 2
                pe.wait_ge(vn_ready, n + 1)
                if n >= 2:
                    pe.wait_ge(gated, n - 1)
                for k in range(4):
                    h = 4 * hh + k
                    ins = M.matmul(ps[:, W0B + n % 2, HD * k:HD * k + HD], wsT[:, h, :],
                                   zv[:, t, O_G + HD * h:O_G + HD * h + HD], start=True, stop=True)
                ins.then_inc(mixed_done, 1)
            pe.wait_ge(gated, 4)
            pe.wait_ge(y_ready, 1)
            for n in range(8):
                base = 0 if n < 4 else O_U - 1024
                transposes("yT", n, [zv[:, t, base + P * k:base + P * k + P] for k in (2 * n, 2 * n + 1) for t in range(TT)])
            pe.wait_ge(t_out[0], (T_AT["yT", 7] + 2) // 2)
            pe.wait_ge(t_out[1], (T_AT["yT", 7] + 1) // 2)
            widen(9)
            project(WIN)
            add_up(10)
            project(WIN + 1)
            add_up(11)
            project(WIN + 2)
            project(WIN + 3)
            pe.sem_inc(slot_free[5], 1)

            for t in range(TT):
                pe.wait_ge(f_ready, t + 1)
                for n in range(4):
                    if t:
                        pe.wait_ge(fT_out[1], n + 1)
                    for j in range(4):
                        ins = M.transpose(ps[:, n, P * j:P * j + P], av[:, t, 4 * n + j:D:KC], ident[:])
                    ins.then_inc(fT_done, 1)
                if t == 0:
                    pe.wait_ge(fT_out[1], 4)
                    pe.wait_ge(z_out, 2 * (WIN + WOUT))
                else:
                    pe.wait_ge(fT_out[0], 2)
                    pe.wait_ge(fT_out[1], 6)
                for k in range(KC):
                    ins = M.matmul(ps[:, W0B, 20 * t:20 * t + 20], T[:, k, P * t:P * t + P], w_router[:, k, :],
                                   start=(k == 0), stop=(k == KC - 1))
            ins.then_inc(logits_done, 1)
            mem = [route[:, 220 + 16 * t:236 + 16 * t] for t in range(TT)]
            pe.wait_ge(chosen, 1)
            rb = ps[:, W0B + 1, :]
            M.matmul(rb[:, 0:16], before[:], mem[0], start=True, stop=True)
            M.matmul(rb[:, 16:32], ones[:], mem[0], start=True, stop=False)
            M.matmul(rb[:, 16:32], before[:], mem[1], start=False, stop=True).then_inc(ranks_done, 1)
            M.matmul(ps[:, T0B, 0:16], ones[:], mem[0], start=True, stop=False)
            M.matmul(ps[:, T0B, 0:16], ones[:], mem[1], start=False, stop=True).then_inc(ranks_done, 1)

            def gather(g, u, width):
                if u >= 5:
                    pe.wait_ge(xT_ready, g * 8 + (u - 2))
                for c in range(2):
                    k = 2 * u + c
                    for t in range(TT):
                        ins = M.matmul(ps[:, GATHER_BANK[u], width * c:width * c + width], av[:, t, P * k:P * k + P],
                                       pick[:, t, 0:width], start=(t == 0), stop=(t == TT - 1))
                ins.then_inc(gathered, 1)

            def spread_part(i, n):
                t, col = n // 4, CH * (n % 4)
                h, cc = col // 1024, col % 1024
                if n >= 1:
                    pe.wait_ge(summed, i * 8 + n)
                else:
                    pe.wait_ge(wpickT_ready, i + 1)
                    pe.wait_ge(down_ready, i + 1)
                    pe.wait_ge(summed, i * 8 + 1)
                M.matmul(ps[:, 2 + n % 2, :], wpickT[64 * h:64 * h + 64, P * t:P * t + P],
                         down_s[64 * h:64 * h + 64, cc:cc + CH], start=True, stop=True).then_inc(spread, 1)

            def expert(i, g, m, width, first=False):
                if m == 0:
                    pe.wait_ge(pick_ready, g + 1)
                    if not first:
                        pe.wait_ge(summed, i * 8 + 1)
                    for u in range(4):
                        gather(g, u, width)
                for q in range(8):
                    s, n = q % SLOTS, q // 2
                    if m == 0 and q in (2, 4):
                        for u in (q + 2, q + 3):
                            gather(g, u, width)
                    if m == 0 and q % 2 == 0:
                        pe.wait_ge(xT_ready, g * 8 + (2 * n + 2))
                    pe.wait_ge(landed[s], i * 32 + 16 * (USED[s] + q // SLOTS + 1))
                    for j in range(4):
                        k = 4 * n + j
                        for h in range(2):
                            ins = M.matmul(ps[64 * h:64 * h + 64, q % 2, :], xT[:, k, BLK * m:BLK * m + BLK],
                                           ada_slot(s)[:, j, CH * h:CH * h + CH], start=(k == 0), stop=(k == KC - 1))
                    ins.then_inc(slot_free[s], 1)
                for n in range(0 if first else 4):
                    spread_part(i, n)
                pe.wait_ge(hid_ready, i + 2)
                for t in range(4):
                    ins = M.transpose(ps[:, 4, P * t:P * t + P], hid[:, P * t:P * t + P], ident[:])
                ins.then_inc(hidT_done, 1)
                for n in range(4, 4 if first else 8):
                    spread_part(i, n)
                pe.wait_ge(wpick_ready, i + 1)
                for t in range(TT):
                    ins = M.transpose(ps[:, 7, P * t:P * t + P], wpick[:, t, :], ident[:])
                ins.then_inc(wpickT_done, 1)
                pe.wait_ge(hidT_ready, i + 1)
                for q in range(8, 12):
                    s = q % SLOTS
                    pe.wait_ge(landed[s], i * 32 + 16 * (USED[s] + q // SLOTS + 1))
                    for j in range(2):
                        k = 2 * (q - 8) + j
                        w = hidT[:, k % 4, 64 * (k // 4):64 * (k // 4) + 64]
                        for cc in range(2):
                            for h in range(2):
                                ins = M.matmul(ps[64 * h:64 * h + 64, 5 + cc, :], w,
                                               down_slot(s)[:, j, 1024 * h + CH * cc:1024 * h + CH * cc + CH],
                                               start=(k == 0), stop=(k == 7))
                    ins.then_inc(slot_free[s], 1)

            for s in (gathered, wpickT_done, hidT_done):
                pe.sem_inc(s, 1)
            pe.sem_inc(spread, 8)
            for m in range(EPG):
                expert(m, 0, m, EPG * BLK, m == 0)
            with pe.Fori(1, GROUPS) as g:
                for m in range(EPG):
                    expert(g * EPG + m, g, m, EPG * BLK)
            pe.wait_ge(list_ready, 1)
            n_extra = pe.value_load(items[0:1, 0:1], min_val=0, max_val=MAX_EXTRA)
            with pe.If(n_extra > 0):
                with pe.Fori(0, n_extra) as j:
                    expert(j + E, j + GROUPS, 0, BLK)
            for n in range(8):
                spread_part(n_extra + E, n)


_INS = ['x', 'c', 'positions', 'w_ada', 'b_ada', 'g_mix_pre', 'g_mix_post', 'w_in', 'sink_logits',
        'gmlp_norm_g', 'w_spatial', 'b_spatial', 'g_group_out', 'w_out', 'g_ffn_pre', 'g_ffn_post',
        'w_router_group', 'b_router_group', 'w_router_expert', 'b_router_expert', 'w_gate', 'w_up', 'w_down']


def kernel(**inputs):
    import numpy as _np
    import concourse.bacc as _bacc
    from concourse import mybir as _mybir
    from concourse.bass_utils import run_bass_kernel_spmd as _run

    nc = _bacc.Bacc("TRN2", target_bir_lowering=False, num_devices=1)
    arrays, args = {}, []
    for name in _INS:
        a = _np.ascontiguousarray(inputs[name])
        arrays[f"in_{name}"] = a
        args.append(nc.dram_tensor(f"in_{name}", a.shape, _mybir.dt.from_np(a.dtype), kind="ExternalInput").ap())
    args.append(nc.dram_tensor("out_0", (1, 256, 2048), _mybir.dt.float32, kind="ExternalOutput").ap())
    hybrid_block(nc, *args)
    r = _run(nc, [arrays], core_ids=[0])
    return r.results[0]["out_0"]
```

```python
from contextlib import ExitStack

import numpy as np

import concourse.bass as bass
from concourse import mybir

F32 = mybir.dt.float32
I32 = mybir.dt.int32
ALU = mybir.AluOpType
ACT = mybir.ActivationFunctionType
AX = mybir.AxisListType

P = 128
SEQ, D = 256, 2048
TT = SEQ // P
KC = D // P
HEADS, KV, HD = 8, 2, 128
N_IN = 3584
O_K, O_V, O_U, O_G = 1024, 1280, 1536, 2560
GROUPS, EPG = 4, 4
E = GROUPS * EPG
FF = 1024
HALF = 1024
CH = 512
WIN = N_IN // CH
WOUT = D // CH
BLK = 64
BLOCKS = SEQ // BLK
CAP = BLK
MAX_EXTRA = (2 * SEQ - 1) // (CAP + 1)
SLOTS = 6
ROPE = HD // 4
HR = ROPE // 2
THETA = 500000.0
EPS = 1e-6
SCALE = HD ** -0.5
NEG = -1e30
FAR = 4096.0
MAGIC = 12582912.0
TWO_PI = (6.28125, 1.9340515136718750e-3, 1.2556659146735911e-6)
PI_SAFE = 3.1415925

SC1, SH1, GT1, GT2, SH2, SC2 = range(6)
MOD_COLUMN = {SH1: 0, SC1: 1, GT1: 2, SH2: 3, SC2: 4, GT2: 5}
HALVES = 12
PE_HALVES = (0, 1, 2, 3, 9)

T_GROUPS = ([("aT", n) for n in range(8)] + [("wsT", n) for n in range(2)]
            + [("q0", n) for n in range(2)] + [("k", 0)] + [("s0", n) for n in range(4)]
            + [("p0", n) for n in range(4)] + [("q1", n) for n in range(2)]
            + [("s1", n) for n in range(4)] + [("p1", n) for n in range(4)]
            + [("yT", n) for n in range(8)])
T_AT = {g: i for i, g in enumerate(T_GROUPS)}


class Steps:

    def __init__(self, engine, sem):
        self.engine, self.sem, self.n = engine, sem, 0

    def add(self, ins):
        ins.then_inc(self.sem, 1)
        self.n += 1
        return self.n

    def link(self, ins):
        self.engine.wait_ge(self.sem, self.add(ins))


def hybrid_block(nc, x, c, positions, w_ada, b_ada, g_mix_pre, g_mix_post, w_in, sink,
                 gmlp_g, w_spatial, b_spatial, g_group, w_out, g_ffn_pre, g_ffn_post,
                 w_rg, b_rg, w_re, b_re, w_gate, w_up, w_down, out):
    with ExitStack() as ctx:
        def sb(name, shape, dt=F32):
            return ctx.enter_context(nc.sbuf_tensor(name, shape, dt))

        def sem(name):
            return ctx.enter_context(nc.semaphore(name))

        ring = sb("ring", [P, SLOTS, 4096])
        X = sb("X", [P, 4096])
        Gt = sb("Gt", [P, 2, D])
        A = sb("A", [P, 4096])
        T = sb("T", [P, KC, SEQ])
        Z = sb("Z", [P, TT * N_IN])
        mod_rows = sb("mod_rows", [P, HALF])
        bias_rows = sb("bias_rows", [P, HALF])
        gain_rows = sb("gain_rows", [P, HALF])
        c_wide = sb("c_wide", [P, KC, 32])
        w_router = sb("w_router", [P, KC, GROUPS + E])
        ident = sb("ident", [P, P])
        rows4 = sb("rows4", [P, P])
        before = sb("before", [P, P])
        mask = sb("mask", [P, TT, P])
        vec_rows = c_wide[:].rearrange("p k n -> p (k n)")[0:40, 0:P]
        vec_cols = sb("vec_cols", [P, 40])

        xv = X[:].rearrange("p (t d) -> p t d", t=TT)
        av = A[:].rearrange("p (t d) -> p t d", t=TT)
        zv = Z[:].rearrange("p (t n) -> p t n", t=TT)
        hv = Z[:, 0:TT * D].rearrange("p (t d) -> p t d", t=TT)
        G1, sh1 = Z[:, 0:D], Z[:, D:2 * D]
        w_sp = Z[:, 4096:5120].rearrange("p (h q) -> p h q", h=HEADS)
        wsT = X[:, 0:1024].rearrange("p (h q) -> p h q", h=HEADS)
        gain_v = X[:, 1024:2048]
        G2, sh2 = X[:, 0:D], X[:, D:2 * D]
        kT = A[:, 0:512].rearrange("p (k s) -> p k s", k=KV)
        qT = A[:, 512:1536].rearrange("p (h s) -> p h s", h=HEADS)
        S = A[:, 1536:3584].rearrange("p (h s) -> p h s", h=HEADS)
        pT = [A[:, 3584:4096], A[:, 512:1024]]
        pT = [b.rearrange("p (h c s) -> p h c s", h=2, c=2) for b in pT]
        xT = X[:].rearrange("p (c s) -> p c s", c=KC)
        silu_s, hid = mod_rows[:, 0:CH], mod_rows[:, CH:2 * CH]
        hidT = bias_rows[:, 0:CH].rearrange("p (t s) -> p t s", t=4)
        down_s = gain_rows
        pick = Gt[:, 0, 0:TT * EPG * BLK].rearrange("p (t s) -> p t s", t=TT)
        wpick = Gt[:, 0, 1024:1024 + TT * P].rearrange("p (t s) -> p t s", t=TT)
        y_gained = xv
        Y = T[:].rearrange("p c s -> p (c s)").rearrange("p (t d) -> p t d", t=TT)
        ZM = Z[:, 4096:7168]
        wpickT = ZM[:, 0:256]
        slot_id = ZM[:, 256:256 + BLOCKS * P].rearrange("p (b s) -> p b s", b=BLOCKS)
        route = ZM[:, 768:1536]
        scale_pk, shift_pk = route[:, 320:336], route[:, 336:352]
        mod_cols = route[:, 352:384]
        mod_blocks = route[0:32, 384:512]
        shift_part = route[:, 512:532]
        fold = route[:, 532:564]
        logit_bias = route[:, 564:584]
        router_wide = c_wide
        logit_parts = mod_rows[:, 0:TT * P].rearrange("p (t s) -> p t s", t=TT)
        items_f = ZM[0:1, 1536:1536 + 1024]
        mix_scratch = ZM[:, 2560:2560 + CH]
        ones = sb("ones", [P, P])
        inv_freq = sb("inv_freq", [P, HR])
        pos_i = sb("pos_i", [P, TT], I32)
        angle = sb("angle", [P, 2, TT, HR])
        turns = mod_rows[:, 0:2 * TT * HR].rearrange("p (a t n) -> p a t n", a=2, t=TT)
        sink_b = sb("sink_b", [P, HEADS])
        router_b = sb("router_b", [P, GROUPS + E])
        stats = sb("stats", [P, 96])
        newton = sb("newton", [P, 12])
        row0 = sb("row0", [P, 1])
        bn = sb("bn", [P, 6 * 4 + 2 * 4])
        items = sb("items", [1, 32], I32)

        ps = ctx.enter_context(nc.psum_tensor("ps", [P, 8, CH], F32))
        flat = ps[:].rearrange("p b n -> p (b n)")
        ada_acc, ada_wide = flat[:, 0:1024], flat[:, 1024:2048]
        W0B, T0B = 4, 6

        x_in, small_in, vec_in, c_in, gain_in, x2_in = (sem(n) for n in (
            "x_in", "small_in", "vec_in", "c_in", "gain_in", "x2_in"))
        landed = [sem(f"landed{s}") for s in range(SLOTS)]
        slot_free = [sem(f"slot_free{s}") for s in range(SLOTS)]
        chunk_in = [sem(f"chunk_in{s}") for s in range(2)]
        bias_in, gainrow_in = sem("bias_in"), sem("gainrow_in")
        constants = sem("constants")
        vec_chain, act_chain, pool_chain = sem("vec_chain"), sem("act_chain"), sem("pool_chain")
        c_silu, vec_ps, c_ready = sem("c_silu"), sem("vec_ps"), sem("c_ready")
        x_square = sem("x_square")
        rows_ready, wide_done, wide_out = sem("rows_ready"), sem("wide_done"), sem("wide_out")
        scaled, a_ready = sem("scaled"), sem("a_ready")
        hT_done, hT_out = sem("hT_done"), [sem("hT_out_vector"), sem("hT_out_scalar")]
        y_clear, gained = sem("y_clear"), sem("gained")
        t_done = sem("t_done")
        t_out = [sem("t_out_vector"), sem("t_out_scalar")]
        w_done, z_out = sem("w_done"), sem("z_out")
        trig_in, trig = sem("trig_in"), sem("trig")
        roped = sem("roped")
        bias_max, probs, pv_done, o_out = sem("bias_max"), sem("probs"), sem("pv_done"), sem("o_out")
        vn_ready, mixed_done, gated = sem("vn_ready"), sem("mixed_done"), sem("gated")
        y_square, y_ready = sem("y_square"), sem("y_ready")
        mix_square, h_ready, h_square = (sem(n) for n in ("mix_square", "h_ready", "h_square"))
        mod_in, router_ready, cols_done, cols_ready = (sem(n) for n in (
            "mod_in", "router_ready", "cols_done", "cols_ready"))
        parts_done, parts_ready = sem("parts_done"), sem("parts_ready")
        logits_done, gap_ready, gap_exp = sem("logits_done"), sem("gap_ready"), sem("gap_exp")
        chosen, ranks_done, list_ready = sem("chosen"), sem("ranks_done"), sem("list_ready")
        pick_ready, gathered, xT_ready = sem("pick_ready"), sem("gathered"), sem("xT_ready")
        wpick_ready, wpickT_done, wpickT_ready = (sem(n) for n in (
            "wpick_ready", "wpickT_done", "wpickT_ready"))
        silu_ready, hid_ready = sem("silu_ready"), sem("hid_ready")
        hidT_done, hidT_ready = sem("hidT_done"), sem("hidT_ready")
        down_ready = sem("down_ready")
        spread, summed = sem("spread"), sem("summed")
        out_square, out_ready, stored = (sem(n) for n in ("out_square", "out_ready", "stored"))

        x_d = x.rearrange("a (t p) d -> p (a t) d", p=P)
        out_d = out.rearrange("a (t p) d -> p (a t) d", p=P)
        ada_d = w_ada[0].rearrange("(k p) n -> p k n", p=P)
        win_d = w_in[0].rearrange("(k p) n -> p k n", p=P)
        wout_d = w_out[0].rearrange("(k p) n -> p k n", p=P)
        gate_d = w_gate.rearrange("a g e (k p) f -> p (a g e) k f", p=P)
        up_d = w_up.rearrange("a g e (k p) f -> p (a g e) k f", p=P)
        down_d = w_down.rearrange("a g e (k p) d -> p (a g e) k d", p=P)
        gain_of = {SC1: g_mix_pre, GT1: g_mix_post, SC2: g_ffn_pre, GT2: g_ffn_post}
        mod_to = {SC1: G1, SH1: sh1, GT1: Gt[:, 0, :], GT2: Gt[:, 1, :], SH2: sh2, SC2: G2}
        n_gained = [sum(1 for m in range(n + 1) if m // 2 in gain_of) for n in range(HALVES)]

        def ada_slot(s):
            return ring[:, s, :].rearrange("p (k n) -> p k n", k=4)

        def chunk_slot(s):
            return ring[:, s, :].rearrange("p (k n) -> p k n", k=8)

        def down_slot(s):
            return ring[:, s, :].rearrange("p (k n) -> p k n", k=2)

        USED = [HALVES] * 4 + [0, 0]
        FREED = [HALVES] * 4 + [WIN + WOUT, 1]

        def wait_products(eng, last, i):
            eng.wait_ge(slot_free[last % SLOTS], i * 2 + (FREED[last % SLOTS] + last // SLOTS + 1))

        GATHER_BANK = [0, 1, 2, 3, 4, 2, 3, 4]
        GATE_UP, DOWN = 7, 11

        block = ctx.enter_context(nc.Block())

        @block.sync
        def _(sp):
            for n in range(HALVES):
                col = D * MOD_COLUMN[n // 2] + HALF * (n % 2)
                for s in range(4):
                    if n:
                        sp.wait_ge(slot_free[s], n)
                    ahead = 4 * n + s - 4 * 5
                    if ahead >= 0:
                        piece = min(2 + ahead * 4 // 7, 18)
                        sp.wait_ge(chunk_in[piece % 2], 16 * (piece // 2 + 1))
                    sp.dma_start(ada_slot(s), ada_d[:, 4 * s:4 * s + 4, col:col + HALF]).then_inc(landed[s], 16)
                if n == 0:
                    sp.wait_ge(constants, 1)
                else:
                    sp.wait_ge(rows_ready, n)
                sp.dma_start(bias_rows[0:1, :], b_ada[0:1, col:col + HALF]).then_inc(bias_in, 16)
                if n // 2 in gain_of:
                    g = gain_of[n // 2][0:1, HALF * (n % 2):HALF * (n % 2 + 1)]
                    to = gain_rows[0:97:32, :] if n in PE_HALVES else gain_rows[:]
                    sp.dma_start(to, g.broadcast_to([to.shape[0], HALF])).then_inc(gainrow_in, 16)

            def load_expert(i, e):
                for q in range(12):
                    s = q % SLOTS
                    sp.wait_ge(slot_free[s], i * 2 + (FREED[s] + q // SLOTS))
                    if q == 5:
                        sp.wait_ge(w_done, TT * (WIN + WOUT))
                    if q < 8:
                        w = gate_d if q % 2 == 0 else up_d
                        src, dst = w[:, bass.ds(e, 1), 4 * (q // 2):4 * (q // 2) + 4, :], ada_slot(s)
                    else:
                        src, dst = down_d[:, bass.ds(e, 1), 2 * (q - 8):2 * (q - 8) + 2, :], down_slot(s)
                    sp.dma_start(dst.unsqueeze(1), src).then_inc(landed[s], 16)

            sp.wait_ge(chunk_in[1], 16 * (WIN + WOUT))
            with sp.Fori(0, E) as i:
                load_expert(i, i)
            sp.wait_ge(list_ready, 1)
            n_extra = sp.value_load(items[0:1, 0:1], min_val=0, max_val=MAX_EXTRA)
            with sp.If(n_extra > 0):
                with sp.Fori(0, n_extra) as j:
                    e = sp.value_load(items[0:1, bass.ds(j + 1, 1)], min_val=0, max_val=E - 1)
                    load_expert(j + E, e)
            for t in range(TT):
                for half in range(2):
                    cols = slice(HALF * half, HALF * half + HALF)
                    sp.wait_ge(out_ready, 2 * t + half + 1)
                    sp.dma_start(out_d[:, t, cols], Y[:, t, cols]).then_inc(stored, 16)
            sp.wait_ge(stored, 16 * 2 * TT)

        @block.gpsimd
        def _(pool):
            ch = Steps(pool, pool_chain)
            nc.gpsimd.memset(bias_rows[:], 0.0)
            nc.gpsimd.memset(gain_rows[:], 1.0).then_inc(constants, 1)
            nc.gpsimd.memset(ones[:], 1.0)
            nc.gpsimd.memset(before[:], 1.0)
            nc.gpsimd.memset(mask[:], 0.0)
            nc.gpsimd.memset(rows4[:], 0.0)
            nc.gpsimd.memset(row0[:], 0.0)
            for n in range(HR):
                nc.gpsimd.memset(inv_freq[:, n:n + 1], float(np.float32(THETA) ** np.float32(-2.0 * n / ROPE)))
            ch.link(nc.gpsimd.memset(ident[:], 0.0))
            for r in range(4):
                ch.link(nc.gpsimd.memset(rows4[32 * r:32 * r + 1, :], 1.0))
            ch.link(nc.gpsimd.memset(row0[0:1, :], 1.0))
            nc.gpsimd.affine_select(out=ident[:], in_=ident[:], compare_op=ALU.not_equal, fill=1.0,
                                    base=0, pattern=[[-1, P]], channel_multiplier=1)
            nc.gpsimd.affine_select(out=before[:], in_=before[:], compare_op=ALU.is_ge, fill=0.0,
                                    base=-1, pattern=[[1, P]], channel_multiplier=-1)
            nc.gpsimd.affine_select(out=mask[:, 0, :], in_=mask[:, 0, :], compare_op=ALU.is_ge, fill=NEG,
                                    base=0, pattern=[[-1, P]], channel_multiplier=1)
            nc.gpsimd.affine_select(out=mask[:, 1, :], in_=mask[:, 1, :], compare_op=ALU.is_ge, fill=NEG,
                                    base=0, pattern=[[1, P]], channel_multiplier=-1).then_inc(constants, 1)

            def load_chunk(m, w_d, col):
                for half in range(2):
                    s = 4 + half
                    if m and half == 0:
                        pool.wait_ge(slot_free[4], m)
                    elif m:
                        pool.wait_ge(w_done, TT * m)
                    pool.dma_start(chunk_slot(s), w_d[:, 8 * half:8 * half + 8, col:col + CH]).then_inc(chunk_in[half], 16)

            pool.wait_ge(slot_free[3], 3)
            for m in range(WIN):
                load_chunk(m, win_d, CH * m)
            for m in range(WOUT):
                load_chunk(WIN + m, wout_d, CH * m)
                if m == WOUT - 1:
                    pool.wait_ge(t_done, T_AT["yT", 7] + 1)
                    pool.dma_start(hv, x_d).then_inc(x2_in, 16)
            for b in range(BLOCKS):
                v = slot_id[:, b, :].rearrange("p (r s) -> p r s", r=2)
                ch.link(nc.gpsimd.iota(v, pattern=[[0, 2], [1, BLK]], base=CAP * b, channel_multiplier=0,
                                       allow_small_or_imprecise_dtypes=True))
                if CAP < BLK:
                    ch.link(nc.gpsimd.memset(v[:, :, CAP:BLK], -1.0))
            ch.link(nc.gpsimd.iota(route[:, 0:4], pattern=[[1, 4]], base=0, channel_multiplier=0,
                                   allow_small_or_imprecise_dtypes=True))
            nc.gpsimd.iota(items_f[0:1, 0:48], pattern=[[0, 3], [1, 16]], base=0, channel_multiplier=0,
                           allow_small_or_imprecise_dtypes=True)
            nc.gpsimd.iota(items_f[0:1, 48:96], pattern=[[1, 3], [0, 16]], base=1, channel_multiplier=0,
                           allow_small_or_imprecise_dtypes=True)
            nc.gpsimd.iota(items_f[0:1, 96:103], pattern=[[1, 7]], base=1, channel_multiplier=0,
                           allow_small_or_imprecise_dtypes=True).then_inc(constants, 1)
            pool.wait_ge(logits_done, 1)
            nc.gpsimd.memset(T[:], 0.0).then_inc(y_clear, 1)
            pool.wait_ge(list_ready, 1)
            n_extra = pool.value_load(items[0:1, 0:1], min_val=0, max_val=MAX_EXTRA)
            pool.wait_ge(summed, n_extra * 8 + (8 * E + 5))
            nc.gpsimd.tensor_tensor(y_gained[:, 0, :], Y[:, 0, :], Gt[:, 1, :], ALU.mult).then_inc(gained, 1)

        @block.scalar
        def _(act):
            ch = Steps(act, act_chain)
            act.dma_start(vec_rows[0:16, :], c.rearrange("a (k p) -> (a k) p", p=P)).then_inc(c_in, 16)
            act.dma_start(vec_rows[16:32, :], g_group.rearrange("a (k p) -> (a k) p", p=P)).then_inc(vec_in, 16)
            act.dma_start(vec_rows[32:40, :], b_spatial[0]).then_inc(vec_in, 16)
            act.dma_start(xv, x_d).then_inc(x_in, 16)
            act.dma_start(pos_i[:], positions.rearrange("a (t p) -> p (a t)", p=P), allow_slow_non_contiguous=True).then_inc(small_in, 16)
            act.dma_start(sink_b[:], sink[0:1, :].broadcast_to([P, HEADS])).then_inc(small_in, 16)
            act.dma_start(router_b[:, 0:GROUPS], b_rg[0:1, :].broadcast_to([P, GROUPS])).then_inc(small_in, 16)
            act.dma_start(router_b[:, GROUPS:], b_re.rearrange("a g e -> a (g e)").broadcast_to([P, E])).then_inc(small_in, 16)
            act.dma_start(w_sp, w_spatial[0].rearrange("h p q -> p h q")).then_inc(small_in, 16)
            act.dma_start(w_router[:, :, 0:GROUPS], w_rg[0].rearrange("(p k) g -> p k g", k=KC)).then_inc(small_in, 16)
            act.dma_start(w_router[:, :, GROUPS:], w_re[0].rearrange("(p k) g e -> p k (g e)", k=KC)).then_inc(small_in, 16)
            act.wait_ge(c_in, 16)
            nc.scalar.activation(vec_rows[0:16, :], vec_rows[0:16, :], ACT.Silu).then_inc(c_silu, 1)
            act.wait_ge(x_in, 16)
            for t in range(TT):
                nc.scalar.activation(av[:, t, :], xv[:, t, :], ACT.Square, accum_out=stats[:, t:t + 1]).then_inc(x_square, 1)

            def wide(n):
                act.wait_ge(wide_done, n + 1)
                to = mod_to[n // 2][:, HALF * (n % 2):HALF * (n % 2 + 1)]
                nc.scalar.copy(to, ada_wide).then_inc(wide_out, 1)

            def t_group(name, n):
                g = T_AT[name, n]
                return g % 2 == 1, g

            def t_copy(name, n, to):
                odd, g = t_group(name, n)
                if odd:
                    act.wait_ge(t_done, g + 1)
                    src = ps[:, T0B + 1, :]
                    nc.scalar.copy(to, src).then_inc(t_out[1], 1)

            def z_chunk(m):
                for t in range(TT):
                    act.wait_ge(w_done, 2 * m + t + 1)
                    nc.scalar.activation(zv[:, t, CH * m:CH * m + CH], ps[:, W0B + t, :],
                                         ACT.Copy if m < 3 else ACT.Gelu).then_inc(z_out, 1)

            wide(0)
            act.wait_ge(trig_in, 1)
            nc.scalar.activation(angle[:], angle[:], ACT.Sin).then_inc(trig, 1)
            wide(1)
            wide(2)
            for n in range(4):
                t_copy("aT", n, T[:, 2 * n:2 * n + 2, :])
            wide(3)
            for n in range(4, 8):
                t_copy("aT", n, T[:, 2 * n:2 * n + 2, :])
            act.wait_ge(scaled, 2)
            act.dma_start(gain_v, gmlp_g.rearrange("a h d -> a (h d)").broadcast_to([P, HEADS * HD])).then_inc(gain_in, 16)
            for n in range(2):
                t_copy("wsT", n, wsT[:, 4 * n:4 * n + 4, :])
            z_chunk(0)
            z_chunk(1)
            wide(4)
            z_chunk(2)
            wide(5)
            z_chunk(3)
            wide(6)
            for n in range(2):
                t_copy("q0", n, qT[:, 4 * n:4 * n + 4, :])
            t_copy("k", 0, kT)

            def scores(t):
                for n in range(4):
                    t_copy(f"s{t}", n, S[:, 2 * n:2 * n + 2, :])

            def softmax(t):
                act.wait_ge(bias_max, t + 1)
                for h in range(HEADS):
                    ins = nc.scalar.activation(S[:, h, :], S[:, h, :], ACT.Exp, bias=stats[:, 16 + h:17 + h],
                                               scale=SCALE, accum_out=stats[:, 24 + h:25 + h])
                nc.scalar.activation(stats[:, 32:40], stats[:, 40:48], ACT.Exp).then_inc(probs, 1)

            def probs_out(t):
                for n in range(4):
                    odd, g = t_group(f"p{t}", n)
                    if odd and (n >= 2 or t):
                        act.wait_ge(pv_done, 4 * t + n - 1)
                    t_copy(f"p{t}", n, pT[n % 2])

            scores(0)
            softmax(0)
            z_chunk(4)
            wide(7)
            probs_out(0)
            for n in range(2):
                t_copy("q1", n, qT[:, 4 * n:4 * n + 4, :])
            scores(1)
            softmax(1)
            z_chunk(5)
            wide(8)
            probs_out(1)
            act.wait_ge(o_out, 2)
            for t in range(TT):
                nc.scalar.activation(A[:, 1536 + 1024 * t:2560 + 1024 * t], zv[:, t, 0:1024], ACT.Square,
                                     accum_out=stats[:, 48 + t:49 + t]).then_inc(y_square, 1)
            z_chunk(6)

            def yT_copy(n):
                odd, g = t_group("yT", n)
                if odd:
                    act.wait_ge(t_done, g + 1)
                    for k in range(2):
                        ins = nc.scalar.activation(T[:, 2 * n + k, :], ps[:, T0B + 1, SEQ * k:SEQ * k + SEQ], ACT.Copy,
                                                   scale=vec_cols[:, 16 + 2 * n + k:17 + 2 * n + k])
                    ins.then_inc(t_out[1], 1)

            for t in range(TT):
                act.wait_ge(gated, 3 + t)
                act.wait_ge(y_square, t + 1)
                nc.scalar.activation(A[:, 1536 + 1024 * t:2560 + 1024 * t], zv[:, t, O_U:O_U + 1024], ACT.Square,
                                     accum_out=stats[:, 50 + t:51 + t]).then_inc(y_square, 1)
                for n in (2 * t, 2 * t + 1):
                    yT_copy(n)
            for n in range(4, 8):
                yT_copy(n)
            for m in range(WOUT):
                if m < 2:
                    wide(9 + m)
                for t in range(TT):
                    act.wait_ge(w_done, 2 * (WIN + m) + t + 1)
                    if m or t:
                        act.wait_ge(mix_square, 2 * m + t)
                    nc.scalar.activation(mix_scratch, ps[:, W0B + t, :], ACT.Square,
                                         accum_out=stats[:, 56 + 4 * t + m:57 + 4 * t + m]).then_inc(mix_square, 1)
                    nc.scalar.copy(av[:, t, CH * m:CH * m + CH], ps[:, W0B + t, :]).then_inc(z_out, 1)
                if m == 2:
                    wide(11)
                    act.wait_ge(wide_out, HALVES)
                    act.dma_start(scale_pk, G2[0:1, :].rearrange("o (p k) -> o p k", k=KC)).then_inc(mod_in, 16)
                    act.dma_start(shift_pk, sh2[0:1, :].rearrange("o (p k) -> o p k", k=KC)).then_inc(mod_in, 16)
                    act.dma_start(mod_blocks, X[0:1, :].rearrange("o (k p) -> o k p", p=P)).then_inc(mod_in, 16)

            def square_h(t):
                act.wait_ge(h_ready, t + 1)
                nc.scalar.activation(av[:, t, :], hv[:, t, :], ACT.Square, accum_out=stats[:, 64 + t:65 + t]).then_inc(h_square, 1)

            def hT_copy(n):
                act.wait_ge(hT_done, n + 1)
                nc.scalar.copy(T[:, 4 * (n % 4):4 * (n % 4) + 4, P * (n // 4):P * (n // 4) + P],
                               ps[:, n % 4, :].rearrange("p (k s) -> p k s", k=4)).then_inc(hT_out[1], 1)

            for n in range(4):
                hT_copy(n)
            square_h(0)
            square_h(1)
            hT_copy(5)
            hT_copy(7)
            act.wait_ge(gap_ready, 1)
            nc.scalar.activation(route[:, 200:210], route[:, 180:190], ACT.Exp).then_inc(gap_exp, 1)

            def gather_out(g, width):
                for u in range(8):
                    act.wait_ge(gathered, g * 8 + (u + 2))
                    for c in range(2):
                        k = 2 * u + c
                        ins = nc.scalar.activation(xT[:, k, 0:width], ps[:, GATHER_BANK[u], width * c:width * c + width],
                                                   ACT.Identity, bias=mod_cols[:, 16 + k:17 + k], scale=mod_cols[:, k:k + 1])
                    ins.then_inc(xT_ready, 1)

            def expert(i):
                wait_products(act, GATE_UP, i)
                act.wait_ge(hid_ready, i + 1)
                nc.scalar.activation(silu_s, ps[:, 0, :], ACT.Silu).then_inc(silu_ready, 1)
                act.wait_ge(wpickT_done, i + 2)
                nc.scalar.copy(wpickT, ps[:, 7, 0:256]).then_inc(wpickT_ready, 1)
                wait_products(act, DOWN, i)
                nc.scalar.copy(down_s[:], flat[:, 2560:3584]).then_inc(down_ready, 1)

            for s in (wpickT_ready, down_ready):
                act.sem_inc(s, 1)
            act.wait_ge(cols_ready, 1)
            with act.Fori(0, GROUPS) as g:
                gather_out(g, EPG * BLK)
                for m in range(EPG):
                    expert(g * EPG + m)
            act.wait_ge(list_ready, 1)
            n_extra = act.value_load(items[0:1, 0:1], min_val=0, max_val=MAX_EXTRA)
            with act.If(n_extra > 0):
                with act.Fori(0, n_extra) as j:
                    gather_out(j + GROUPS, BLK)
                    expert(j + E)
            for t in range(TT):
                act.wait_ge(summed, n_extra * 8 + (8 * E + 4 * t + 5))
                nc.scalar.activation(av[:, t, :], Y[:, t, :], ACT.Square,
                                     accum_out=stats[:, 68 + t:69 + t]).then_inc(out_square, 1)

        @block.vector
        def _(dve):
            ch = Steps(dve, vec_chain)
            V = nc.vector

            def rsqrt_mean(to, square_sum, n):
                w = to.shape[-1]
                v, y, t = (newton[:, 4 * k:4 * k + w] for k in range(3))
                ch.link(V.tensor_scalar(v, square_sum, 1.0 / n, EPS, ALU.mult, ALU.add))
                ch.link(V.tensor_scalar(y.bitcast(I32), v.bitcast(I32), 1, None, ALU.logical_shift_right))
                if w == 1:
                    V.tensor_scalar(v, v, -0.5, None, ALU.mult)
                ch.link(V.tensor_scalar(y.bitcast(I32), y.bitcast(I32), -1.0, float(0x5f3759df), ALU.mult, ALU.add))
                for step in range(3):
                    if w == 1:
                        ch.link(V.tensor_scalar(t, y, y, v, ALU.mult, ALU.mult))
                    else:
                        ch.link(V.tensor_tensor(t, y, y, ALU.mult))
                        ch.link(V.scalar_tensor_tensor(t, t, -0.5, v, ALU.mult, ALU.mult))
                    last = V.scalar_tensor_tensor(y if step < 2 else to, t, 1.5, y, ALU.add, ALU.mult)
                    if step < 2:
                        ch.link(last)
                return last

            dve.wait_ge(vec_ps, 1)
            ch.link(V.tensor_copy(vec_cols[:], ps[:, 7, 0:40]))
            V.tensor_copy(c_wide[:], vec_cols[:, 0:16].unsqueeze(2).broadcast_to([P, KC, 32])).then_inc(c_ready, 1)

            dve.wait_ge(small_in, 7 * 16)
            dve.wait_ge(constants, 2)
            ch.link(V.tensor_copy(stats[:, 4:6], pos_i[:]))
            for t in range(TT):
                ins = V.tensor_scalar(angle[:, 0, t, :], inv_freq[:], stats[:, 4 + t:5 + t], None, ALU.mult)
            ch.link(ins)
            ch.link(V.tensor_copy(angle[:, 1], angle[:, 0]))
            ch.link(V.tensor_scalar(turns[:, 0], angle[:, 0], float(0.5 / np.pi), None, ALU.mult))
            ch.link(V.tensor_scalar(turns[:, 1], angle[:, 1], float(0.5 / np.pi), 0.25, ALU.mult, ALU.add))
            ch.link(V.tensor_scalar(turns, turns, MAGIC, None, ALU.add))
            ch.link(V.tensor_scalar(turns, turns, -MAGIC, None, ALU.add))
            af, tf = (b.rearrange("p a t n -> p (a t n)") for b in (angle[:], turns))
            for part in TWO_PI:
                ch.link(V.scalar_tensor_tensor(af, tf, -part, af, ALU.mult, ALU.add))
            ch.link(V.tensor_scalar(angle[:, 1], angle[:, 1], float(np.pi / 2), None, ALU.add))
            V.tensor_scalar(af, af, PI_SAFE, -PI_SAFE, ALU.min, ALU.max).then_inc(trig_in, 1)

            dve.wait_ge(x_square, TT)
            ch.link(rsqrt_mean(stats[:, 2:4], stats[:, 0:2], D))

            def rows(n):
                kind = n // 2
                dve.wait_ge(slot_free[3], n + 1)
                dve.wait_ge(bias_in, 16 * (n + 1))
                if n:
                    dve.wait_ge(wide_done, n)
                gained = kind in gain_of
                if kind in (SC1, SC2):
                    ins = V.scalar_tensor_tensor(mod_rows[:], ada_acc, row0[:, 0:1], bias_rows[:], ALU.add, ALU.add)
                else:
                    ins = V.tensor_tensor(mod_rows[:], ada_acc, bias_rows[:], ALU.add)
                if gained:
                    ch.link(ins)
                    dve.wait_ge(gainrow_in, 16 * n_gained[n])
                    ins = V.tensor_tensor(mod_rows[:], mod_rows[:], gain_rows[:], ALU.mult)
                ins.then_inc(rows_ready, 1)

            def t_copy(name, n, to):
                g = T_AT[name, n]
                if g % 2 == 0:
                    dve.wait_ge(t_done, g + 1)
                    src = ps[:, T0B, :]
                    V.tensor_copy(to, src).then_inc(t_out[0], 1)

            def scale_half(h):
                dve.wait_ge(wide_out, h + 1)
                cols = slice(HALF * h, HALF * h + HALF)
                for t in range(TT):
                    ins = V.scalar_tensor_tensor(av[:, t, cols], xv[:, t, cols], stats[:, 2 + t:3 + t], G1[:, cols], ALU.mult, ALU.mult)
                ins.then_inc(scaled, 1)

            def shift_half(h):
                dve.wait_ge(wide_out, 3 + h)
                dve.wait_ge(scaled, h + 1)
                cols = slice(HALF * h, HALF * h + HALF)
                for t in range(TT):
                    ins = V.tensor_tensor(av[:, t, cols], av[:, t, cols], sh1[:, cols], ALU.add)
                ins.then_inc(a_ready, 1)

            rows(0)
            rows(1)
            scale_half(0)
            rows(2)
            scale_half(1)
            shift_half(0)
            rows(3)
            for n in range(4):
                t_copy("aT", n, T[:, 2 * n:2 * n + 2, :])
            shift_half(1)
            for n in range(4, 8):
                t_copy("aT", n, T[:, 2 * n:2 * n + 2, :])
            for n in range(2):
                t_copy("wsT", n, wsT[:, 4 * n:4 * n + 4, :])

            def products(n, slots):
                for s in slots:
                    dve.wait_ge(landed[s], 16 * (n + 1))
                    for j in range(4):
                        k = 4 * s + j
                        own, w = ada_slot(s)[:, 0, :], ada_slot(s)[:, j, :]
                        if k == 0:
                            ch.link(V.tensor_scalar(own, w, vec_cols[:, 0:1], None, ALU.mult))
                        elif j == 0:
                            ins = V.scalar_tensor_tensor(own, w, vec_cols[:, k:k + 1], ada_slot(s - 1)[:, 0, :], ALU.mult, ALU.add)
                            ins.then_inc(slot_free[s - 1], 1)
                            dve.wait_ge(slot_free[s - 1], n + 1)
                        elif k < KC - 1:
                            ch.link(V.scalar_tensor_tensor(own, w, vec_cols[:, k:k + 1], own, ALU.mult, ALU.add))
                if k == KC - 1:
                    dve.wait_ge(wide_done, n)
                    V.scalar_tensor_tensor(mod_rows[:], w, vec_cols[:, k:k + 1], own, ALU.mult, ALU.add).then_inc(slot_free[3], 1)
                    dve.wait_ge(slot_free[3], n + 1)
                    dve.wait_ge(bias_in, 16 * (n + 1))
                    if n // 2 == SC2:
                        ins = V.scalar_tensor_tensor(mod_rows[:], mod_rows[:], row0[:, 0:1], bias_rows[:], ALU.add, ALU.add)
                    else:
                        ins = V.tensor_tensor(mod_rows[:], mod_rows[:], bias_rows[:], ALU.add)
                    if n // 2 in gain_of:
                        ch.link(ins)
                        dve.wait_ge(gainrow_in, 16 * n_gained[n])
                        ins = V.tensor_tensor(mod_rows[:], mod_rows[:], gain_rows[:], ALU.mult)
                    ins.then_inc(rows_ready, 1)

            products(4, range(4))
            products(5, range(4))
            products(6, range(2))

            dve.wait_ge(z_out, 6)
            dve.wait_ge(trig, 1)
            NQ = HEADS + KV
            rope_tmp = A[:, 0:4 * NQ * HR].rearrange("p (n h r) -> p n h r", n=4, r=HR)
            for t in range(TT):
                qk = zv[:, t, 0:NQ * HD].rearrange("p (h d) -> p h d", d=HD)
                x1, x2 = qk[:, :, 0:HR], qk[:, :, HR:ROPE]
                sin, cos = (angle[:, k, t, :].unsqueeze(1).broadcast_to([P, NQ, HR]) for k in range(2))
                V.tensor_tensor(rope_tmp[:, 0], x1, cos, ALU.mult)
                V.tensor_tensor(rope_tmp[:, 1], x2, sin, ALU.mult)
                V.tensor_tensor(rope_tmp[:, 2], x2, cos, ALU.mult)
                ch.link(V.tensor_tensor(rope_tmp[:, 3], x1, sin, ALU.mult))
                V.tensor_tensor(x1, rope_tmp[:, 0], rope_tmp[:, 1], ALU.subtract)
                V.tensor_tensor(x2, rope_tmp[:, 2], rope_tmp[:, 3], ALU.add).then_inc(roped, 1)
                dve.wait_ge(roped, t + 1)
            products(6, range(2, 4))
            for n in range(2):
                t_copy("q0", n, qT[:, 4 * n:4 * n + 4, :])
            t_copy("k", 0, kT)

            def scores(t):
                for n in range(4):
                    t_copy(f"s{t}", n, S[:, 2 * n:2 * n + 2, :])
                dve.wait_ge(t_out[0], (T_AT[f"s{t}", 3] + 2) // 2)
                dve.wait_ge(t_out[1], (T_AT[f"s{t}", 3] + 1) // 2)
                if t:
                    dve.wait_ge(probs, t)
                ch.link(V.tensor_reduce(stats[:, 8:16], S, AX.X, ALU.max))
                ch.link(V.scalar_tensor_tensor(stats[:, 8:16], stats[:, 8:16], SCALE, sink_b[:], ALU.mult, ALU.max))
                V.tensor_tensor(stats[:, 40:48], sink_b[:], stats[:, 8:16], ALU.subtract)
                V.tensor_scalar(stats[:, 16:24], stats[:, 8:16], -1.0, None, ALU.mult).then_inc(bias_max, 1)

            def probs_out(t):
                dve.wait_ge(probs, t + 1)
                ch.link(V.tensor_tensor(stats[:, 72:80], stats[:, 24:32], stats[:, 32:40], ALU.add))
                ch.link(V.reciprocal(stats[:, 80:88], stats[:, 72:80]))
                for n in range(4):
                    if T_AT[f"p{t}", n] % 2 == 0 and (n >= 2 or t):
                        dve.wait_ge(pv_done, 4 * t + n - 1)
                    t_copy(f"p{t}", n, pT[n % 2])
                dve.wait_ge(pv_done, 4 * t + 4)
                o = zv[:, t, 0:1024].rearrange("p (h d) -> p h d", d=HD)
                V.tensor_tensor(o, flat[:, CH * W0B:CH * W0B + 1024].rearrange("p (h d) -> p h d", d=HD),
                                stats[:, 80:88].unsqueeze(2).broadcast_to([P, HEADS, HD]), ALU.mult).then_inc(o_out, 1)

            scores(0)
            products(7, range(4))
            probs_out(0)
            for n in range(2):
                t_copy("q1", n, qT[:, 4 * n:4 * n + 4, :])
            scores(1)
            products(8, range(4))
            probs_out(1)

            dve.wait_ge(y_square, 2)
            ch.link(rsqrt_mean(stats[:, 52:54], stats[:, 48:50], 1024))
            for t in range(TT):
                ins = V.tensor_scalar(zv[:, t, 0:1024], zv[:, t, 0:1024], stats[:, 52 + t:53 + t], None, ALU.mult)
            ins.then_inc(y_ready, 1)

            dve.wait_ge(gain_in, 16)
            for m in (5, 6):
                for t in range(TT):
                    dve.wait_ge(z_out, 2 * m + t + 1)
                    v = zv[:, t, CH * m:CH * m + CH]
                    for h in range(4):
                        ins = V.bn_stats(bn[:, 6 * h:6 * h + 6], v[:, HD * h:HD * h + HD])
                    ch.link(ins)
                    for h in range(4):
                        ins = V.bn_aggr(bn[:, 24 + 2 * h:26 + 2 * h], bn[:, 6 * h:6 * h + 6])
                    ch.link(ins)
                    moments = bn[:, 24:32].rearrange("p (h two) -> p h two", two=2)
                    ch.link(V.tensor_copy(stats[:, 88:92], moments[:, :, 1]))
                    ch.link(rsqrt_mean(stats[:, 92:96], stats[:, 88:92], 1))
                    for h in range(4):
                        ins = V.tensor_scalar(v[:, HD * h:HD * h + HD], v[:, HD * h:HD * h + HD], moments[:, h, 0:1],
                                              stats[:, 92 + h:93 + h], ALU.subtract, ALU.mult)
                    ch.link(ins)
                    V.tensor_tensor(v, v, gain_v[:, CH * (m - 5):CH * (m - 5) + CH], ALU.mult).then_inc(vn_ready, 1)
            for n in range(4):
                hh, t = n // 2, n % 2
                dve.wait_ge(mixed_done, n + 1)
                for k in range(4):
                    h = 4 * hh + k
                    u = zv[:, t, O_U + HD * h:O_U + HD * h + HD]
                    ins = V.scalar_tensor_tensor(u, ps[:, W0B + n % 2, HD * k:HD * k + HD],
                                                 vec_cols[:, 32 + h:33 + h], u, ALU.add, ALU.mult)
                ins.then_inc(gated, 1)

            def yT_copy(n):
                if T_AT["yT", n] % 2 == 0:
                    dve.wait_ge(t_done, T_AT["yT", n] + 1)
                    for k in range(2):
                        ins = V.tensor_scalar(T[:, 2 * n + k, :], ps[:, T0B, SEQ * k:SEQ * k + SEQ],
                                              vec_cols[:, 16 + 2 * n + k:17 + 2 * n + k], None, ALU.mult)
                    ins.then_inc(t_out[0], 1)

            for n in range(4):
                yT_copy(n)
            dve.wait_ge(y_square, 4)
            ch.link(rsqrt_mean(stats[:, 54:56], stats[:, 50:52], 1024))
            for t in range(TT):
                u = zv[:, t, O_U:O_U + 1024]
                ins = V.tensor_scalar(u, u, stats[:, 54 + t:55 + t], None, ALU.mult)
            ins.then_inc(y_ready, 1)
            for n in range(4, 8):
                yT_copy(n)
            rows(9)
            products(10, range(4))

            def mix_gain(m, t):
                dve.wait_ge(wide_out, 6)
                dve.wait_ge(z_out, 2 * (WIN + m) + t + 1)
                part = av[:, t, CH * m:CH * m + CH]
                ch.link(V.tensor_tensor(part, part, Gt[:, 0, CH * m:CH * m + CH], ALU.mult))

            for t in range(TT):
                mix_gain(0, t)
            products(11, range(4))
            for t in range(TT):
                mix_gain(1, t)
            for t in range(TT):
                mix_gain(2, t)

            dve.wait_ge(slot_free[3], 10)
            ch.link(V.memset(router_wide[:], 0.0))
            V.tensor_reduce(fold, ident[:].rearrange("p (g e) -> p e g", g=4), AX.X, ALU.add)
            dve.wait_ge(mod_in, 3 * 16)
            V.tensor_tensor(router_wide[:, :, 0:GROUPS + E], w_router[:], scale_pk.unsqueeze(2).broadcast_to([P, KC, GROUPS + E]), ALU.mult)
            shifted = X[:, 0:KC * (GROUPS + E)].rearrange("p (k e) -> p k e", k=KC)
            ch.link(V.tensor_tensor(shifted, w_router[:], shift_pk.unsqueeze(2).broadcast_to([P, KC, GROUPS + E]), ALU.mult))
            V.tensor_reduce(shift_part, shifted.rearrange("p k e -> p e k"), AX.X, ALU.add).then_inc(router_ready, 1)

            dve.wait_ge(x2_in, 16)
            for t in range(TT):
                mix_gain(3, t)
                dve.wait_ge(mix_square, 2 * WOUT - 1 + t)
                ch.link(V.tensor_reduce(stats[:, 4 + t:5 + t], stats[:, 56 + 4 * t:60 + 4 * t], AX.X, ALU.add))
                ch.link(rsqrt_mean(stats[:, 6 + t:7 + t], stats[:, 4 + t:5 + t], D))
                V.scalar_tensor_tensor(hv[:, t, :], av[:, t, :], stats[:, 6 + t:7 + t], hv[:, t, :], ALU.mult, ALU.add).then_inc(h_ready, 1)

            def parts_copy(t):
                dve.wait_ge(parts_done, t + 1)
                V.tensor_copy(logit_parts[:, t, :], ps[:, W0B + t, 0:P]).then_inc(parts_ready, 1)

            dve.wait_ge(cols_done, 2)
            V.tensor_copy(mod_cols, ps[:, T0B + 1, 0:32]).then_inc(cols_ready, 1)
            ch.link(V.tensor_tensor(logit_bias, ps[:, T0B + 1, 32:52], router_b[:], ALU.add))
            parts_copy(0)
            for n in (4, 6):
                dve.wait_ge(hT_done, n + 1)
                V.tensor_copy(T[:, 4 * (n % 4):4 * (n % 4) + 4, P:2 * P],
                              ps[:, n % 4, :].rearrange("p (k s) -> p k s", k=4)).then_inc(hT_out[0], 1)
            dve.wait_ge(h_square, TT)
            ch.link(rsqrt_mean(stats[:, 66:68], stats[:, 64:66], D))
            parts_copy(1)

            def r3(at, n):
                return route[:, at:at + TT * n].rearrange("p (t n) -> p t n", t=TT)

            def r1(at):
                return route[:, at:at + TT]

            iota4 = route[:, 0:4].unsqueeze(1).broadcast_to([P, TT, 4])

            def over4(s):
                return s.unsqueeze(2).broadcast_to([P, TT, 4])

            def first_of(to, logits, top, work, at):
                ch.link(V.tensor_tensor(work, logits, over4(top), ALU.is_lt))
                ch.link(V.scalar_tensor_tensor(work, work, 100.0, iota4, ALU.mult, ALU.add))
                ch.link(V.tensor_reduce(at, work, AX.X, ALU.min))
                return V.tensor_tensor(to, iota4, over4(at), ALU.is_equal)

            L = r3(8, 20)
            work, at = r3(48, 4), r1(56)
            gmax, pick_g = r1(58), r3(60, 4)
            esel, m1, oh1, m2, oh2 = r3(68, 4), r1(76), r3(78, 4), r1(86), r3(88, 4)
            weighted = route[:, 96:128].rearrange("p (t g e) -> p t g e", t=TT, g=GROUPS)
            esel2 = r3(130, 4)
            gaps = r3(180, 5)
            gexp = r3(200, 5)
            dve.wait_ge(logits_done, 1)
            dve.wait_ge(constants, 3)
            for t in range(TT):
                ins = V.scalar_tensor_tensor(L[:, t, :], ps[:, T0B, 64 + 20 * t:84 + 20 * t], stats[:, 66 + t:67 + t], logit_bias, ALU.mult, ALU.add)
            ch.link(ins)
            ch.link(V.tensor_reduce(gmax, L[:, :, 0:4], AX.X, ALU.max))
            V.tensor_tensor(gaps[:, :, 0:4], L[:, :, 0:4], over4(gmax), ALU.subtract)
            ch.link(first_of(pick_g, L[:, :, 0:4], gmax, work, at))
            for t in range(TT):
                ins = V.tensor_tensor(weighted[:, t], L[:, t, 4:20].rearrange("p (g e) -> p g e", g=GROUPS),
                                      pick_g[:, t].unsqueeze(2).broadcast_to([P, GROUPS, EPG]), ALU.mult)
            ch.link(ins)
            ch.link(V.tensor_reduce(esel, weighted.rearrange("p t g e -> p t e g"), AX.X, ALU.add))
            ch.link(V.tensor_reduce(m1, esel, AX.X, ALU.max))
            ch.link(first_of(oh1, esel, m1, work, at))
            ch.link(V.scalar_tensor_tensor(esel2, oh1, -1e38, esel, ALU.mult, ALU.add))
            ch.link(V.tensor_reduce(m2, esel2, AX.X, ALU.max))
            V.tensor_tensor(gaps[:, :, 4], m2, m1, ALU.subtract).then_inc(gap_ready, 1)
            ch.link(first_of(oh2, esel2, m2, work, at))
            both = r3(140, 4)
            ch.link(V.tensor_tensor(both, oh1, oh2, ALU.add))
            member = route[:, 220:252].rearrange("p (t g e) -> p t g e", t=TT, g=GROUPS)
            comb = route[:, 252:284].rearrange("p (t g e) -> p t g e", t=TT, g=GROUPS)
            for t in range(TT):
                ins = V.tensor_tensor(member[:, t], pick_g[:, t].unsqueeze(2).broadcast_to([P, GROUPS, EPG]),
                                      both[:, t].unsqueeze(1).broadcast_to([P, GROUPS, EPG]), ALU.mult)
            ins.then_inc(chosen, 1)
            rank = route[:, 284:316]
            dve.wait_ge(ranks_done, 1)
            memf = route[:, 220:252]
            ch.link(V.scalar_tensor_tensor(rank, memf, -FAR, ps[:, W0B + 1, 0:32], ALU.mult, ALU.add))
            ch.link(V.tensor_scalar(rank, rank, FAR, None, ALU.add))

            combf = route[:, 252:284]

            def list_blocks():
                dve.wait_ge(ranks_done, 2)
                f = items_f[0:1, :]
                e_id, b_id, j_id = f[:, 0:48], f[:, 48:96], f[:, 96:103]
                flag, run = f[:, 103:151], f[:, 151:199]
                for b in range(1, BLOCKS):
                    ins = V.tensor_scalar(flag[:, 16 * (b - 1):16 * b], ps[0:1, T0B, 0:16], float(CAP * b), None, ALU.is_gt)
                ch.link(ins)
                ch.link(V.tensor_copy(run, flag))
                step = 1
                tmp48 = f[:, 200:248]
                while step < 48:
                    ch.link(V.tensor_copy(tmp48, run))
                    ch.link(V.tensor_tensor(run[:, step:48], tmp48[:, step:48], tmp48[:, 0:48 - step], ALU.add))
                    step *= 2
                sel = f[:, 248:248 + 7 * 48].rearrange("p (j n) -> p j n", j=7)

                def over_j(s):
                    return s.unsqueeze(1).broadcast_to([1, 7, 48])

                prod = f[:, 600:600 + 7 * 48].rearrange("p (j n) -> p j n", j=7)
                got = f[:, 940:957]
                ch.link(V.tensor_tensor(sel, over_j(run), j_id.unsqueeze(2).broadcast_to([1, 7, 48]), ALU.is_equal))
                ch.link(V.tensor_tensor(sel, sel, over_j(flag), ALU.mult))
                ch.link(V.tensor_tensor(prod, sel, over_j(e_id), ALU.mult))
                ch.link(V.tensor_reduce(got[:, 1:8], prod, AX.X, ALU.add))
                ch.link(V.tensor_tensor(prod, sel, over_j(b_id), ALU.mult))
                ch.link(V.tensor_reduce(got[:, 8:15], prod, AX.X, ALU.add))
                ch.link(V.tensor_copy(got[:, 0:1], run[:, 47:48]))
                V.tensor_copy(items[:, 0:15], got[:, 0:15]).then_inc(list_ready, 1)


            def weigh():
                dve.wait_ge(gap_exp, 1)
                den, w1, w2, wsum = r1(150), r1(152), r1(154), r1(156)
                ch.link(V.tensor_reduce(wsum, gexp[:, :, 0:4], AX.X, ALU.add))
                ch.link(V.tensor_scalar(den, gexp[:, :, 4], 1.0, None, ALU.add))
                ch.link(V.tensor_tensor(den, den, wsum, ALU.mult))
                ch.link(V.reciprocal(w1, den))
                ch.link(V.tensor_tensor(w2, w1, gexp[:, :, 4], ALU.mult))
                V.tensor_tensor(oh1, oh1, over4(w1), ALU.mult)
                ch.link(V.tensor_tensor(oh2, oh2, over4(w2), ALU.mult))
                ch.link(V.tensor_tensor(both, oh1, oh2, ALU.add))
                for t in range(TT):
                    ins = V.tensor_tensor(comb[:, t], pick_g[:, t].unsqueeze(2).broadcast_to([P, GROUPS, EPG]),
                                          both[:, t].unsqueeze(1).broadcast_to([P, GROUPS, EPG]), ALU.mult)
                ch.link(ins)

            def picks(g, experts, ids):
                dve.wait_ge(gathered, g * 8 + 1)
                for m, e in enumerate(experts):
                    for t in range(TT):
                        ins = V.tensor_scalar(pick[:, t, BLK * m:BLK * m + BLK], ids[:, 0:BLK],
                                              rank[:, bass.ds(e + 16 * t, 1)], stats[:, 66 + t:67 + t], ALU.is_equal, ALU.mult)
                ins.then_inc(pick_ready, 1)

            def add(i, n):
                t, col = n // 4, CH * (n % 4)
                dve.wait_ge(spread, i * 8 + (n + 1))
                V.tensor_tensor(Y[:, t, col:col + CH], Y[:, t, col:col + CH], ps[:, 2 + n % 2, :], ALU.add).then_inc(summed, 1)

            def expert(i, e, ids, m=0, then=None):
                dve.wait_ge(wpickT_done, i + 1)
                for t in range(TT):
                    ins = V.tensor_scalar(wpick[:, t, :], ids, rank[:, bass.ds(e + 16 * t, 1)],
                                          combf[:, bass.ds(e + 16 * t, 1)], ALU.is_equal, ALU.mult)
                ins.then_inc(wpick_ready, 1)
                if then:
                    then()
                for n in range(8 if m else 0):
                    add(i, n)
                dve.wait_ge(silu_ready, i + 1)
                dve.wait_ge(hidT_done, i + 1)
                V.tensor_tensor(hid, silu_s, ps[:, 1, :], ALU.mult).then_inc(hid_ready, 1)
                for n in range(0 if then or m else 4):
                    add(i, n)
                dve.wait_ge(hidT_done, i + 2)
                dve.wait_ge(slot_free[5], i * 2 + 1)
                V.tensor_copy(bias_rows[:, 0:CH], ps[:, 4, :]).then_inc(hidT_ready, 1)
                for n in range(4, 4 if then or m else 8):
                    add(i, n)
                if not then:
                    dve.wait_ge(summed, i * 8 + 9)

            def group(g, then=None):
                picks(g, [g * EPG + m for m in range(EPG)], slot_id[:, 0, :])
                if then:
                    weigh()
                for m in range(EPG):
                    expert(g * EPG + m, g * EPG + m, slot_id[:, 0, :], m, then if m == 0 else None)

            dve.sem_inc(hid_ready, 1)
            dve.sem_inc(summed, 9)
            dve.wait_ge(y_clear, 1)
            group(0, list_blocks)
            with dve.Fori(1, GROUPS) as g:
                group(g)
            n_extra = dve.value_load(items[0:1, 0:1], min_val=0, max_val=MAX_EXTRA)
            with dve.If(n_extra > 0):
                with dve.Fori(0, n_extra) as j:
                    e = dve.value_load(items[0:1, bass.ds(j + 1, 1)], min_val=0, max_val=E - 1)
                    b = dve.value_load(items[0:1, bass.ds(j + 8, 1)], min_val=1, max_val=BLOCKS - 1)
                    ids = slot_id[:, bass.ds(b, 1), :].rearrange("p b s -> p (b s)")
                    picks(j + GROUPS, [e], ids)
                    expert(j + E, e, ids)
            for n in range(8):
                add(n_extra + E, n)
            dve.wait_ge(summed, n_extra * 8 + (8 * E + 9))
            ch.link(V.tensor_tensor(y_gained[:, 1, :], Y[:, 1, :], Gt[:, 1, :], ALU.mult))
            dve.wait_ge(gained, 1)
            dve.wait_ge(out_square, TT)
            ch.link(rsqrt_mean(stats[:, 4:6], stats[:, 68:70], D))
            for t in range(TT):
                for half in range(2):
                    cols = slice(HALF * half, HALF * half + HALF)
                    V.scalar_tensor_tensor(Y[:, t, cols], y_gained[:, t, cols], stats[:, 4 + t:5 + t], hv[:, t, cols],
                                           ALU.mult, ALU.add).then_inc(out_ready, 1)

        @block.tensor
        def _(pe):
            M = nc.tensor

            def t_bank(name, n):
                g = T_AT[name, n]
                if g >= 2:
                    pe.wait_ge(t_out[g % 2], g // 2)
                return ps[:, T0B + g % 2, :]

            pe.wait_ge(constants, 2)
            pe.wait_ge(c_silu, 1)
            pe.wait_ge(vec_in, 2 * 16)
            M.transpose(ps[:, 7, 0:40], vec_rows, ident[0:40, 0:40]).then_inc(vec_ps, 1)

            def ada(n):
                for s in range(4):
                    pe.wait_ge(landed[s], 16 * (n + 1))
                    if s == 0:
                        if n:
                            pe.wait_ge(rows_ready, 1 + max(m for m in PE_HALVES if m < n))
                        else:
                            pe.wait_ge(c_ready, 1)
                    for cc in range(2):
                        for j in range(4):
                            ins = M.matmul(ada_acc[32 * j:32 * j + 32, CH * cc:CH * cc + CH], c_wide[:, 4 * s + j, :],
                                           ada_slot(s)[:, j, CH * cc:CH * cc + CH], start=(s == 0), stop=(s == 3))
                    ins.then_inc(slot_free[s], 1)
                    if s == 0 and 0 < n < 4:
                        widen(n - 1)

            def widen(n):
                pe.wait_ge(rows_ready, n + 1)
                if n:
                    pe.wait_ge(wide_out, n)
                lhs = rows4 if n in PE_HALVES else ones
                for cc in range(2):
                    ins = M.matmul(ada_wide[:, CH * cc:CH * cc + CH], lhs[:], mod_rows[:, CH * cc:CH * cc + CH], start=True, stop=True)
                ins.then_inc(wide_done, 1)

            def transposes(name, n, blocks):
                bank = t_bank(name, n)
                for k, src in enumerate(blocks):
                    ins = M.transpose(bank[:, P * k:P * k + P], src, ident[:])
                ins.then_inc(t_done, 1)

            def project(m):
                for half in range(2):
                    pe.wait_ge(chunk_in[half], 16 * (m + 1))
                    for t in range(TT):
                        if half == 0 and m:
                            pe.wait_ge(z_out, 2 * m - 1 + t)
                        for k in range(8):
                            kk = 8 * half + k
                            ins = M.matmul(ps[:, W0B + t, :], T[:, kk, P * t:P * t + P], chunk_slot(4 + half)[:, k, :],
                                           start=(kk == 0), stop=(kk == KC - 1))
                        if half == 0 and t == TT - 1:
                            ins.then_inc(slot_free[4], 1)
                        elif half == 1:
                            ins.then_inc(w_done, 1)

            for n in range(4):
                ada(n)
            for half in range(2):
                if half:
                    widen(3)
                pe.wait_ge(a_ready, half + 1)
                for n in range(4 * half, 4 * half + 4):
                    transposes("aT", n, [av[:, t, P * k:P * k + P] for k in (2 * n, 2 * n + 1) for t in range(TT)])
            pe.wait_ge(small_in, 7 * 16)
            for n in range(2):
                transposes("wsT", n, [w_sp[:, h, :] for h in range(4 * n, 4 * n + 4)])
            pe.wait_ge(t_out[0], (T_AT["aT", 7] + 2) // 2)
            pe.wait_ge(t_out[1], (T_AT["aT", 7] + 1) // 2)
            project(0)
            project(1)
            widen(4)
            project(2)
            widen(5)
            project(3)
            widen(6)

            def q_tile(t):
                pe.wait_ge(roped, TT)
                for n in range(2):
                    transposes(f"q{t}", n, [zv[:, t, HD * h:HD * h + HD] for h in range(4 * n, 4 * n + 4)])

            def scores(t):
                last = T_AT["k", 0] if t == 0 else T_AT["q1", 1]
                pe.wait_ge(t_out[0], (last + 2) // 2)
                pe.wait_ge(t_out[1], (last + 1) // 2)
                for n in range(4):
                    bank = t_bank(f"s{t}", n)
                    for k in range(2):
                        h = 2 * n + k
                        own = slice(SEQ * k, SEQ * k + SEQ)
                        edge = slice(SEQ * k + P * (1 - t), SEQ * k + P * (1 - t) + P)
                        M.matmul(bank[:, own], qT[:, h, :], kT[:, h // (HEADS // KV), :], start=True, stop=True)
                        ins = M.matmul(bank[:, edge], ident[:], mask[:, t, :], start=False, stop=True, skip_group_check=True)
                    ins.then_inc(t_done, 1)

            def attend(t):
                pe.wait_ge(probs, t + 1)

                def pv(n):
                    g = T_AT[f"p{t}", n]
                    pe.wait_ge(t_out[g % 2], g // 2 + 1)
                    if n == 0:
                        pe.wait_ge(z_out, 2 * (5 + t))
                    for k in range(2):
                        h = 2 * n + k
                        v0 = O_V + HD * (h // (HEADS // KV))
                        for kc in range(2):
                            ins = M.matmul(ps[:, W0B + h // 4, HD * (h % 4):HD * (h % 4) + HD], pT[n % 2][:, k, kc, :],
                                           zv[:, kc, v0:v0 + HD], start=(kc == 0), stop=(kc == 1))
                    ins.then_inc(pv_done, 1)

                for n in range(4):
                    transposes(f"p{t}", n, [S[:, h, P * kc:P * kc + P] for h in (2 * n, 2 * n + 1) for kc in range(2)])
                    if n:
                        pv(n - 1)
                pv(3)

            q_tile(0)
            transposes("k", 0, [zv[:, t, O_K + HD * k:O_K + HD * k + HD] for k in range(KV) for t in range(TT)])
            scores(0)
            project(4)
            widen(7)
            attend(0)
            q_tile(1)
            scores(1)
            pe.wait_ge(o_out, 1)
            project(5)
            widen(8)
            attend(1)
            pe.wait_ge(o_out, 2)
            project(6)
            ada(9)
            pe.wait_ge(z_out, 2 * WIN)
            for n in range(4):
                hh, t = n // 2, n % 2
                pe.wait_ge(vn_ready, n + 1)
                if n >= 2:
                    pe.wait_ge(gated, n - 1)
                for k in range(4):
                    h = 4 * hh + k
                    ins = M.matmul(ps[:, W0B + n % 2, HD * k:HD * k + HD], wsT[:, h, :],
                                   zv[:, t, O_G + HD * h:O_G + HD * h + HD], start=True, stop=True)
                ins.then_inc(mixed_done, 1)
            for n in range(8):
                if n % 4 == 0:
                    pe.wait_ge(y_ready, 1 + n // 4)
                base = 0 if n < 4 else O_U - 1024
                transposes("yT", n, [zv[:, t, base + P * k:base + P * k + P] for k in (2 * n, 2 * n + 1) for t in range(TT)])
            pe.wait_ge(t_out[0], (T_AT["yT", 7] + 2) // 2)
            pe.wait_ge(t_out[1], (T_AT["yT", 7] + 1) // 2)
            widen(9)
            project(WIN)
            widen(10)
            project(WIN + 1)
            project(WIN + 2)
            widen(11)
            project(WIN + 3)
            pe.sem_inc(slot_free[5], 1)

            pe.wait_ge(mod_in, 3 * 16)
            M.transpose(ps[:, T0B + 1, 0:32], mod_blocks, ident[0:32, 0:32]).then_inc(cols_done, 1)
            pe.wait_ge(router_ready, 1)
            M.matmul(ps[:, T0B + 1, 32:52], ones[:], shift_part, start=True, stop=True).then_inc(cols_done, 1)

            for t in range(TT):
                pe.wait_ge(h_ready, t + 1)
                for n in range(4):
                    if t:
                        pe.wait_ge(hT_out[1], n + 1)
                    for j in range(4):
                        ins = M.transpose(ps[:, n, P * j:P * j + P], hv[:, t, 4 * n + j:D:KC], ident[:])
                    ins.then_inc(hT_done, 1)
                if t == 0:
                    pe.wait_ge(hT_out[1], 4)
                    pe.wait_ge(z_out, 2 * (WIN + WOUT))
                else:
                    pe.wait_ge(hT_out[0], 2)
                    pe.wait_ge(hT_out[1], 6)
                for k in range(KC):
                    g = k % 4
                    ins = M.matmul(ps[32 * g:32 * g + 32, W0B + t, 0:P], router_wide[:, k, :], T[:, k, P * t:P * t + P],
                                   start=(k < 4), stop=(k >= KC - 4))
                ins.then_inc(parts_done, 1)
            for t in range(TT):
                pe.wait_ge(parts_ready, t + 1)
                ins = M.matmul(ps[:, T0B, 64 + 20 * t:84 + 20 * t], logit_parts[:, t, :], fold[:, 0:GROUPS + E], start=True, stop=True)
            ins.then_inc(logits_done, 1)
            mem = [route[:, 220 + 16 * t:236 + 16 * t] for t in range(TT)]
            pe.wait_ge(chosen, 1)
            rb = ps[:, W0B + 1, :]
            M.matmul(rb[:, 0:16], before[:], mem[0], start=True, stop=True)
            M.matmul(rb[:, 16:32], ones[:], mem[0], start=True, stop=False)
            M.matmul(rb[:, 16:32], before[:], mem[1], start=False, stop=True).then_inc(ranks_done, 1)
            M.matmul(ps[:, T0B, 0:16], ones[:], mem[0], start=True, stop=False)
            M.matmul(ps[:, T0B, 0:16], ones[:], mem[1], start=False, stop=True).then_inc(ranks_done, 1)

            def gather(g, u, width):
                if u >= 5:
                    pe.wait_ge(xT_ready, g * 8 + (u - 2))
                for c in range(2):
                    k = 2 * u + c
                    for t in range(TT):
                        ins = M.matmul(ps[:, GATHER_BANK[u], width * c:width * c + width], hv[:, t, P * k:P * k + P],
                                       pick[:, t, 0:width], start=(t == 0), stop=(t == TT - 1))
                ins.then_inc(gathered, 1)

            def spread_part(i, n):
                t, col = n // 4, CH * (n % 4)
                h, cc = col // 1024, col % 1024
                if n >= 1:
                    pe.wait_ge(summed, i * 8 + n)
                else:
                    pe.wait_ge(wpickT_ready, i + 1)
                    pe.wait_ge(down_ready, i + 1)
                    pe.wait_ge(summed, i * 8 + 1)
                M.matmul(ps[:, 2 + n % 2, :], wpickT[64 * h:64 * h + 64, P * t:P * t + P],
                         down_s[64 * h:64 * h + 64, cc:cc + CH], start=True, stop=True).then_inc(spread, 1)

            def transpose_wpick(i):
                pe.wait_ge(wpick_ready, i + 1)
                for t in range(TT):
                    ins = M.transpose(ps[:, 7, P * t:P * t + P], wpick[:, t, :], ident[:])
                ins.then_inc(wpickT_done, 1)

            def expert(i, g, m, width, first=False):
                if m == 0:
                    pe.wait_ge(pick_ready, g + 1)
                    if not first:
                        pe.wait_ge(summed, i * 8 + 1)
                    for u in range(3):
                        gather(g, u, width)
                for q in range(8):
                    s, n = q % SLOTS, q // 2
                    if m == 0:
                        for u in ((), (), (3, 4), (), (5, 6), (), (7,), ())[q]:
                            gather(g, u, width)
                    if m == 0 and q % 2 == 0:
                        pe.wait_ge(xT_ready, g * 8 + (2 * n + 2))
                    pe.wait_ge(landed[s], i * 32 + 16 * (USED[s] + q // SLOTS + 1))
                    for j in range(4):
                        k = 4 * n + j
                        for h in range(2):
                            ins = M.matmul(ps[64 * h:64 * h + 64, q % 2, :], xT[:, k, BLK * m:BLK * m + BLK],
                                           ada_slot(s)[:, j, CH * h:CH * h + CH], start=(k == 0), stop=(k == KC - 1))
                    ins.then_inc(slot_free[s], 1)
                    if m:
                        spread_part(i, q)
                if m:
                    transpose_wpick(i)
                elif not first:
                    for n in range(4):
                        spread_part(i, n)
                pe.wait_ge(hid_ready, i + 2)
                for t in range(4):
                    ins = M.transpose(ps[:, 4, P * t:P * t + P], hid[:, P * t:P * t + P], ident[:])
                ins.then_inc(hidT_done, 1)
                if m == 0:
                    for n in range(4, 4 if first else 8):
                        spread_part(i, n)
                    transpose_wpick(i)
                pe.wait_ge(hidT_ready, i + 1)
                for q in range(8, 12):
                    s = q % SLOTS
                    pe.wait_ge(landed[s], i * 32 + 16 * (USED[s] + q // SLOTS + 1))
                    for j in range(2):
                        k = 2 * (q - 8) + j
                        w = hidT[:, k % 4, 64 * (k // 4):64 * (k // 4) + 64]
                        for cc in range(2):
                            for h in range(2):
                                ins = M.matmul(ps[64 * h:64 * h + 64, 5 + cc, :], w,
                                               down_slot(s)[:, j, 1024 * h + CH * cc:1024 * h + CH * cc + CH],
                                               start=(k == 0), stop=(k == 7))
                    ins.then_inc(slot_free[s], 1)

            for s in (gathered, wpickT_done, hidT_done):
                pe.sem_inc(s, 1)
            pe.sem_inc(spread, 8)
            for m in range(EPG):
                expert(m, 0, m, EPG * BLK, m == 0)
            with pe.Fori(1, GROUPS) as g:
                for m in range(EPG):
                    expert(g * EPG + m, g, m, EPG * BLK)
            pe.wait_ge(list_ready, 1)
            n_extra = pe.value_load(items[0:1, 0:1], min_val=0, max_val=MAX_EXTRA)
            with pe.If(n_extra > 0):
                with pe.Fori(0, n_extra) as j:
                    expert(j + E, j + GROUPS, 0, BLK)
            for n in range(8):
                spread_part(n_extra + E, n)


_INS = ['x', 'c', 'positions', 'w_ada', 'b_ada', 'g_mix_pre', 'g_mix_post', 'w_in', 'sink_logits',
        'gmlp_norm_g', 'w_spatial', 'b_spatial', 'g_group_out', 'w_out', 'g_ffn_pre', 'g_ffn_post',
        'w_router_group', 'b_router_group', 'w_router_expert', 'b_router_expert', 'w_gate', 'w_up', 'w_down']


def kernel(**inputs):
    import numpy as _np
    import concourse.bacc as _bacc
    from concourse import mybir as _mybir
    from concourse.bass_utils import run_bass_kernel_spmd as _run

    nc = _bacc.Bacc("TRN2", target_bir_lowering=False, num_devices=1)
    arrays, args = {}, []
    for name in _INS:
        a = _np.ascontiguousarray(inputs[name])
        arrays[f"in_{name}"] = a
        args.append(nc.dram_tensor(f"in_{name}", a.shape, _mybir.dt.from_np(a.dtype), kind="ExternalInput").ap())
    args.append(nc.dram_tensor("out_0", (1, 256, 2048), _mybir.dt.float32, kind="ExternalOutput").ap())
    hybrid_block(nc, *args)
    r = _run(nc, [arrays], core_ids=[0])
    return r.results[0]["out_0"]
```
